# Optimizing a Trainium2 kernel written in Bass

```python
import math
import jax, jax.numpy as jnp
from jax import lax
import numpy as np

D_MODEL = 2048
BATCH = 1
SEQ = 256
DEPTH = 2

CHUNK = 64
N_MIXERS = 2
Q_BLOCK = 128

MLA_HEADS = 16
QK_NOPE = 128
QK_ROPE = 64
V_HEAD = 128
Q_LORA = 512
KV_LORA = 512
ROPE_THETA = 10000.0
MLA_QK = QK_NOPE + QK_ROPE
MLA_WIDTH = MLA_HEADS * V_HEAD
MLA_IN = Q_LORA + KV_LORA + QK_ROPE + MLA_WIDTH

ML_HEADS = 8
ML_QK = 128
ML_V = 256
ML_QK_WIDTH = ML_HEADS * ML_QK
ML_WIDTH = ML_HEADS * ML_V
CONV_W = 4
ML_IN = 2 * ML_QK_WIDTH + 2 * ML_WIDTH + 2 * ML_HEADS + ML_WIDTH

ALPHA = (2 * DEPTH) ** 0.25
BETA = (8 * DEPTH) ** -0.25
EPS = 1e-6


def _rmsnorm(x, w):
    xf = x.astype(jnp.float32)
    y = xf * lax.rsqrt(jnp.mean(xf * xf, axis=-1, keepdims=True) + EPS)
    return y.astype(x.dtype) * w

def _layernorm(x, w, b):
    xf = x.astype(jnp.float32)
    mu = jnp.mean(xf, axis=-1, keepdims=True)
    var = jnp.mean(jnp.square(xf - mu), axis=-1, keepdims=True)
    return ((xf - mu) * lax.rsqrt(var + EPS)).astype(x.dtype) * w + b

def _rope_tables(positions, dtype):
    inv_freq = ROPE_THETA ** (-jnp.arange(0, QK_ROPE, 2, dtype=jnp.float32) / QK_ROPE)
    ang = positions.astype(jnp.float32)[..., None] * inv_freq
    return jnp.cos(ang).astype(dtype), jnp.sin(ang).astype(dtype)

def _rope(x, cos, sin):
    half = x.shape[-1] // 2
    x1, x2 = x[..., :half], x[..., half:]
    return jnp.concatenate([x1 * cos - x2 * sin, x1 * sin + x2 * cos], axis=-1)

def _chunk_causal_attention(q, k, v):
    b, s, h, dk = q.shape
    nb = s // Q_BLOCK
    scale = dk ** -0.5
    q_blocks = q.reshape(b, nb, Q_BLOCK, h, dk).transpose(1, 0, 2, 3, 4)
    key_chunk = jnp.arange(s) // CHUNK

    def one_block(args):
        qb, bi = args
        q_chunk = (bi * Q_BLOCK + jnp.arange(Q_BLOCK)) // CHUNK
        mask = key_chunk[None, :] <= q_chunk[:, None]
        sc = jnp.einsum('bqhd,bkhd->bhqk', qb, k).astype(jnp.float32) * scale
        sc = jnp.where(mask, sc, -jnp.inf)
        p = jax.nn.softmax(sc, axis=-1).astype(v.dtype)
        return jnp.einsum('bhqk,bkhd->bqhd', p, v)

    out = lax.map(one_block, (q_blocks, jnp.arange(nb)))
    return out.transpose(1, 0, 2, 3, 4).reshape(b, s, h, v.shape[-1])

def _mla_mixer(x, cos, sin, w_in, q_norm, w_qb, kv_norm, w_kvb, w_out):
    b, s, _ = x.shape
    proj = x @ w_in
    c_q, c_kv, k_rope, z = jnp.split(
        proj, [Q_LORA, Q_LORA + KV_LORA, Q_LORA + KV_LORA + QK_ROPE], axis=-1)
    q = (_rmsnorm(c_q, q_norm) @ w_qb).reshape(b, s, MLA_HEADS, MLA_QK)
    q_nope, q_rope = q[..., :QK_NOPE], q[..., QK_NOPE:]
    kv = (_rmsnorm(c_kv, kv_norm) @ w_kvb).reshape(b, s, MLA_HEADS, QK_NOPE + V_HEAD)
    k_nope, v = kv[..., :QK_NOPE], kv[..., QK_NOPE:]
    q_rope = _rope(q_rope, cos[:, :, None, :], sin[:, :, None, :])
    k_rope = _rope(k_rope, cos, sin)
    q = jnp.concatenate([q_nope, q_rope], axis=-1)
    k = jnp.concatenate(
        [k_nope, jnp.broadcast_to(k_rope[:, :, None, :], (b, s, MLA_HEADS, QK_ROPE))], axis=-1)
    attn = _chunk_causal_attention(q, k, v).reshape(b, s, MLA_WIDTH)
    return (attn * jax.nn.silu(z)) @ w_out

def _causal_depthwise_conv(x, w, bias):
    c = x.shape[-1]
    y = lax.conv_general_dilated(
        x, w[:, None, :], window_strides=(1,), padding=[(CONV_W - 1, 0)],
        dimension_numbers=('NWC', 'WIO', 'NWC'), feature_group_count=c)
    return y + bias

def _mlstm_chunkwise(q, k, v, i_pre, f_pre):
    b, s, h, dk = q.shape
    dv = v.shape[-1]
    nc = s // CHUNK
    f32 = jnp.float32

    def chunks(t):
        return t.astype(f32).reshape(b, nc, CHUNK, h, -1).transpose(1, 0, 3, 2, 4)

    def gate_chunks(t):
        return t.astype(f32).reshape(b, nc, CHUNK, h).transpose(1, 0, 3, 2)

    qc = chunks(q)
    kc = chunks(k) * (dk ** -0.5)
    vc = chunks(v)
    log_i = gate_chunks(i_pre)
    log_f = jax.nn.log_sigmoid(gate_chunks(f_pre))
    tril = jnp.tril(jnp.ones((CHUNK, CHUNK), dtype=bool))

    def step(carry, xs):
        c_st, n_st, m_st = carry
        qx, kx, vx, li, lf = xs
        bcum = jnp.cumsum(lf, axis=-1)
        dmat = bcum[..., :, None] - bcum[..., None, :] + li[..., None, :]
        dmat = jnp.where(tril, dmat, -jnp.inf)
        m_inter = bcum + m_st[..., None]
        m_t = jnp.maximum(m_inter, jnp.max(dmat, axis=-1))
        w_inter = jnp.exp(m_inter - m_t)
        s_qk = jnp.einsum('bhtd,bhsd->bhts', qx, kx) * jnp.exp(dmat - m_t[..., None])
        num = (w_inter[..., None] * jnp.einsum('bhtd,bhdv->bhtv', qx, c_st)
               + jnp.einsum('bhts,bhsv->bhtv', s_qk, vx))
        den = w_inter * jnp.einsum('bhtd,bhd->bht', qx, n_st) + jnp.sum(s_qk, axis=-1)
        h_out = num / jnp.maximum(jnp.abs(den), jnp.exp(-m_t))[..., None]
        b_last = bcum[..., -1]
        g = b_last[..., None] - bcum + li
        m_new = jnp.maximum(b_last + m_st, jnp.max(g, axis=-1))
        decay = jnp.exp(b_last + m_st - m_new)
        wk = jnp.exp(g - m_new[..., None])
        c_new = decay[..., None, None] * c_st + jnp.einsum('bhs,bhsd,bhsv->bhdv', wk, kx, vx)
        n_new = decay[..., None] * n_st + jnp.einsum('bhs,bhsd->bhd', wk, kx)
        return (c_new, n_new, m_new), h_out

    init = (jnp.zeros((b, h, dk, dv), f32), jnp.zeros((b, h, dk), f32), jnp.zeros((b, h), f32))
    _, hs = lax.scan(step, init, (qc, kc, vc, log_i, log_f))
    return hs.transpose(1, 0, 3, 2, 4).reshape(b, s, h, dv)

def _mlstm_mixer(x, w_in, conv_w, conv_b, gate_b, head_norm, w_out):
    b, s, _ = x.shape
    proj = x @ w_in
    o1 = 2 * ML_QK_WIDTH
    o2 = o1 + ML_WIDTH
    o3 = o2 + ML_WIDTH
    o4 = o3 + 2 * ML_HEADS
    qk, v, o, gates, z = jnp.split(proj, [o1, o2, o3, o4], axis=-1)
    qk = jax.nn.silu(_causal_depthwise_conv(qk, conv_w, conv_b))
    q, k = jnp.split(qk, 2, axis=-1)
    gates = gates + gate_b
    i_pre, f_pre = gates[..., :ML_HEADS], gates[..., ML_HEADS:]
    cell = _mlstm_chunkwise(q.reshape(b, s, ML_HEADS, ML_QK), k.reshape(b, s, ML_HEADS, ML_QK),
                            v.reshape(b, s, ML_HEADS, ML_V), i_pre, f_pre)
    cell = _rmsnorm(cell.astype(x.dtype), head_norm.reshape(ML_HEADS, ML_V)).reshape(b, s, ML_WIDTH)
    hcell = jax.nn.sigmoid(o) * cell
    return (hcell * jax.nn.silu(z)) @ w_out

def first_inputs(seed: int = 0) -> dict:
    key = jax.random.key(seed)
    ks = jax.random.split(key, 20)
    n_a = (DEPTH + N_MIXERS - 1) // N_MIXERS
    n_b = DEPTH // N_MIXERS

    def nrm(k, shape, scale):
        return jax.random.normal(k, shape, jnp.float32) * scale

    x = nrm(ks[0], (BATCH, SEQ, D_MODEL), 1.0)
    offsets = jax.random.randint(ks[1], (BATCH, 1), 0, 4096, dtype=jnp.int32)
    positions = offsets + jnp.arange(SEQ, dtype=jnp.int32)[None, :]

    mla_w_in = nrm(ks[2], (n_a, D_MODEL, MLA_IN), D_MODEL ** -0.5)
    mla_q_norm = 1.0 + nrm(ks[3], (n_a, Q_LORA), 0.02)
    mla_w_qb = nrm(ks[4], (n_a, Q_LORA, MLA_HEADS * MLA_QK), Q_LORA ** -0.5)
    mla_kv_norm = 1.0 + nrm(ks[5], (n_a, KV_LORA), 0.02)
    mla_w_kvb = nrm(ks[6], (n_a, KV_LORA, MLA_HEADS * (QK_NOPE + V_HEAD)), KV_LORA ** -0.5)
    mla_w_out = nrm(ks[7], (n_a, MLA_WIDTH, D_MODEL), BETA * MLA_WIDTH ** -0.5)

    ml_w_in = nrm(ks[8], (n_b, D_MODEL, ML_IN), D_MODEL ** -0.5)
    ml_conv_w = nrm(ks[9], (n_b, CONV_W, 2 * ML_QK_WIDTH), CONV_W ** -0.5)
    ml_conv_b = nrm(ks[10], (n_b, 2 * ML_QK_WIDTH), 0.02)
    i_bias = nrm(ks[11], (n_b, ML_HEADS), 0.1)
    f_bias = jnp.linspace(3.0, 6.0, ML_HEADS, dtype=jnp.float32)[None, :] + nrm(ks[12], (n_b, ML_HEADS), 0.1)
    ml_gate_b = jnp.concatenate([i_bias, f_bias], axis=-1)
    ml_head_norm = 1.0 + nrm(ks[13], (n_b, ML_WIDTH), 0.02)
    ml_w_out = nrm(ks[14], (n_b, ML_WIDTH, D_MODEL), BETA * ML_WIDTH ** -0.5)

    ln_w = 1.0 + nrm(ks[15], (DEPTH, D_MODEL), 0.02)
    ln_b = nrm(ks[16], (DEPTH, D_MODEL), 0.02)
    return {'x': x, 'positions': positions,
            'mla_w_in': mla_w_in, 'mla_q_norm': mla_q_norm, 'mla_w_qb': mla_w_qb,
            'mla_kv_norm': mla_kv_norm, 'mla_w_kvb': mla_w_kvb, 'mla_w_out': mla_w_out,
            'ml_w_in': ml_w_in, 'ml_conv_w': ml_conv_w, 'ml_conv_b': ml_conv_b,
            'ml_gate_b': ml_gate_b, 'ml_head_norm': ml_head_norm, 'ml_w_out': ml_w_out,
            'ln_w': ln_w, 'ln_b': ln_b}

def first_block(x, positions, mla_w_in, mla_q_norm, mla_w_qb, mla_kv_norm, mla_w_kvb, mla_w_out,
              ml_w_in, ml_conv_w, ml_conv_b, ml_gate_b, ml_head_norm, ml_w_out, ln_w, ln_b):
    cos, sin = _rope_tables(positions, x.dtype)
    for layer in range(DEPTH):
        j = layer // N_MIXERS
        if layer % N_MIXERS == 0:
            y = _mla_mixer(x, cos, sin, mla_w_in[j], mla_q_norm[j], mla_w_qb[j],
                           mla_kv_norm[j], mla_w_kvb[j], mla_w_out[j])
        else:
            y = _mlstm_mixer(x, ml_w_in[j], ml_conv_w[j], ml_conv_b[j], ml_gate_b[j],
                             ml_head_norm[j], ml_w_out[j])
        x = _layernorm(ALPHA * x + y, ln_w[layer], ln_b[layer])
    return x


DEPTH_2 = 1

HEAD_DIM = 128
N_HEADS_A = D_MODEL // 256
N_KV_A = max(1, N_HEADS_A // 4)
N_HEADS_B = D_MODEL // 256
GRID_W = 64
NA_ROWS = 8
NA_COLS = 16
ROPE_AXIS_DIM = HEAD_DIM // 2
D_FF = -(-(8 * D_MODEL) // (3 * 256)) * 256
NORM_EPS = 1e-6
IN_SPLITS = (
    N_HEADS_A * HEAD_DIM,
    N_KV_A * HEAD_DIM,
    N_KV_A * HEAD_DIM,
    N_HEADS_B * HEAD_DIM,
    N_HEADS_B * HEAD_DIM,
    N_HEADS_B * HEAD_DIM,
    D_MODEL,
    D_MODEL,
)
D_IN = sum(IN_SPLITS)


def rms_norm(x, w):
    xf = x.astype(jnp.float32)
    y = xf * lax.rsqrt(jnp.mean(xf * xf, axis=-1, keepdims=True) + NORM_EPS)
    return (y * w.astype(jnp.float32)).astype(x.dtype)

def axial_rope_tables(S):
    t = jnp.arange(S, dtype=jnp.int32)
    row = (t // GRID_W).astype(jnp.float32)
    col = (t % GRID_W).astype(jnp.float32)
    inv = ROPE_THETA ** (-jnp.arange(0, ROPE_AXIS_DIM, 2, dtype=jnp.float32) / ROPE_AXIS_DIM)
    ang = jnp.concatenate([row[:, None] * inv[None], col[:, None] * inv[None]], axis=-1)
    return jnp.cos(ang), jnp.sin(ang)

def apply_rope(x, cos, sin):
    xf = x.astype(jnp.float32).reshape(*x.shape[:-1], HEAD_DIM // 2, 2)
    x0, x1 = xf[..., 0], xf[..., 1]
    c = cos[None, :, None, :]
    s = sin[None, :, None, :]
    out = jnp.stack([x0 * c - x1 * s, x0 * s + x1 * c], axis=-1)
    return out.reshape(x.shape).astype(x.dtype)

def global_gqa(q, k, v):
    B, S, HQ, hd = q.shape
    KVH = k.shape[2]
    G = HQ // KVH
    nb = S // Q_BLOCK
    scale = hd ** -0.5
    qb = q.reshape(B, nb, Q_BLOCK, KVH, G, hd).transpose(1, 0, 2, 3, 4, 5)

    def one_block(qblk):
        s = jnp.einsum('bqkgd,bskd->bkgqs', qblk, k).astype(jnp.float32) * scale
        p = jax.nn.softmax(s, axis=-1).astype(v.dtype)
        return jnp.einsum('bkgqs,bskd->bqkgd', p, v)

    o = lax.map(one_block, qb)
    return o.transpose(1, 0, 2, 3, 4, 5).reshape(B, S, HQ * hd)

def neighbourhood_attention(q, k, v, rpb):
    B, S, H, hd = q.shape
    rows = S // GRID_W
    kr = min(NA_ROWS, rows)
    nk = kr * NA_COLS
    nb = S // Q_BLOCK
    scale = hd ** -0.5
    t = jnp.arange(S, dtype=jnp.int32)
    r = t // GRID_W
    col = t % GRID_W
    rs = jnp.clip(r - kr // 2, 0, rows - kr)
    cs = jnp.clip(col - NA_COLS // 2, 0, GRID_W - NA_COLS)
    key_r = rs[:, None, None] + jnp.arange(kr, dtype=jnp.int32)[None, :, None]
    key_c = cs[:, None, None] + jnp.arange(NA_COLS, dtype=jnp.int32)[None, None, :]
    shape3 = (S, kr, NA_COLS)
    idx = (key_r * GRID_W + key_c).reshape(nb, Q_BLOCK, nk)
    rel_r = jnp.broadcast_to(key_r - r[:, None, None] + (NA_ROWS - 1), shape3).reshape(nb, Q_BLOCK, nk)
    rel_c = jnp.broadcast_to(key_c - col[:, None, None] + (NA_COLS - 1), shape3).reshape(nb, Q_BLOCK, nk)
    qb = q.reshape(B, nb, Q_BLOCK, H, hd).transpose(1, 0, 2, 3, 4)

    def one_block(args):
        qblk, ib, rr, rc = args
        kb = k[:, ib]
        vb = v[:, ib]
        bias = rpb[:, rr, rc].astype(jnp.float32)
        s = jnp.einsum('bqhd,bqnhd->bhqn', qblk, kb).astype(jnp.float32) * scale + bias[None]
        p = jax.nn.softmax(s, axis=-1).astype(v.dtype)
        return jnp.einsum('bhqn,bqnhd->bqhd', p, vb)

    o = lax.map(one_block, (qb, idx, rel_r, rel_c))
    return o.transpose(1, 0, 2, 3, 4).reshape(B, S, H * hd)

def second_inputs(seed: int = 0) -> dict:
    key = jax.random.key(seed)
    ks = jax.random.split(key, 20)
    f32 = jnp.float32
    D = D_MODEL

    def w(k, shape, fan_in):
        return jax.random.normal(k, shape, f32) * (fan_in ** -0.5)

    def gain(k, shape):
        return 1.0 + 0.05 * jax.random.normal(k, shape, f32)

    return {
        "x": jax.random.normal(ks[0], (BATCH, SEQ, D), f32),
        "c": jax.random.normal(ks[1], (BATCH, D), f32),
        "w_ada": w(ks[2], (DEPTH_2, D, 6 * D), D) * 0.5,
        "b_ada": 0.02 * jax.random.normal(ks[3], (DEPTH_2, 6 * D), f32),
        "norm1_w": gain(ks[4], (DEPTH_2, D)),
        "w_in": w(ks[5], (DEPTH_2, D, D_IN), D),
        "q_norm_w": gain(ks[6], (DEPTH_2, HEAD_DIM)),
        "k_norm_w": gain(ks[7], (DEPTH_2, HEAD_DIM)),
        "nat_rpb": 0.1 * jax.random.normal(ks[8], (DEPTH_2, N_HEADS_B, 2 * NA_ROWS - 1, 2 * NA_COLS - 1), f32),
        "w_oa": w(ks[9], (DEPTH_2, N_HEADS_A * HEAD_DIM, D), N_HEADS_A * HEAD_DIM),
        "w_ob": w(ks[10], (DEPTH_2, N_HEADS_B * HEAD_DIM, D), N_HEADS_B * HEAD_DIM),
        "w_out": w(ks[11], (DEPTH_2, D, D), D),
        "norm2_w": gain(ks[12], (DEPTH_2, D)),
        "w_ffn_gate": w(ks[13], (DEPTH_2, D, D_FF), D),
        "w_ffn_up": w(ks[14], (DEPTH_2, D, D_FF), D),
        "w_ffn_down": w(ks[15], (DEPTH_2, D_FF, D), D_FF),
        "final_w": gain(ks[16], (D,)),
    }

def second_block(x, c, w_ada, b_ada, norm1_w, w_in, q_norm_w, k_norm_w, nat_rpb,
              w_oa, w_ob, w_out, norm2_w, w_ffn_gate, w_ffn_up, w_ffn_down, final_w):
    B, S, D = x.shape
    cos, sin = axial_rope_tables(S)
    offs = np.cumsum(IN_SPLITS)[:-1].tolist()
    c_act = jax.nn.silu(c)
    for l in range(DEPTH_2):
        mod = c_act @ w_ada[l] + b_ada[l]
        sh1, sc1, g1, sh2, sc2, g2 = [m[:, None, :] for m in jnp.split(mod, 6, axis=-1)]

        h = rms_norm(x, norm1_w[l]) * (1.0 + sc1) + sh1
        proj = h @ w_in[l]
        qa, ka, va, qb, kb, vb, ga, gb = jnp.split(proj, offs, axis=-1)
        qa = qa.reshape(B, S, N_HEADS_A, HEAD_DIM)
        ka = ka.reshape(B, S, N_KV_A, HEAD_DIM)
        va = va.reshape(B, S, N_KV_A, HEAD_DIM)
        qa = apply_rope(rms_norm(qa, q_norm_w[l]), cos, sin)
        ka = apply_rope(rms_norm(ka, k_norm_w[l]), cos, sin)
        ya = global_gqa(qa, ka, va)
        yb = neighbourhood_attention(
            qb.reshape(B, S, N_HEADS_B, HEAD_DIM),
            kb.reshape(B, S, N_HEADS_B, HEAD_DIM),
            vb.reshape(B, S, N_HEADS_B, HEAD_DIM),
            nat_rpb[l])
        merged = jax.nn.sigmoid(ga) * (ya @ w_oa[l]) + jax.nn.sigmoid(gb) * (yb @ w_ob[l])
        x = x + g1 * (merged @ w_out[l])

        h2 = rms_norm(x, norm2_w[l]) * (1.0 + sc2) + sh2
        ff = (jax.nn.silu(h2 @ w_ffn_gate[l]) * (h2 @ w_ffn_up[l])) @ w_ffn_down[l]
        x = x + g2 * ff
    return rms_norm(x, final_w)


def setup_inputs(seed=0):
    out = dict(first_inputs(seed))
    for name, value in second_inputs(seed + 1).items():
        if name != "x":
            out[name + "_2"] = value
    return out


def reference(
    x, positions, mla_w_in, mla_q_norm, mla_w_qb, mla_kv_norm, mla_w_kvb, mla_w_out, ml_w_in,
    ml_conv_w, ml_conv_b, ml_gate_b, ml_head_norm, ml_w_out, ln_w, ln_b, c_2, w_ada_2, b_ada_2,
    norm1_w_2, w_in_2, q_norm_w_2, k_norm_w_2, nat_rpb_2, w_oa_2, w_ob_2, w_out_2, norm2_w_2,
    w_ffn_gate_2, w_ffn_up_2, w_ffn_down_2, final_w_2,
):
    x = first_block(
        x, positions, mla_w_in, mla_q_norm, mla_w_qb, mla_kv_norm, mla_w_kvb, mla_w_out,
        ml_w_in, ml_conv_w, ml_conv_b, ml_gate_b, ml_head_norm, ml_w_out, ln_w, ln_b,
    )
    return second_block(
        x, c_2, w_ada_2, b_ada_2, norm1_w_2, w_in_2, q_norm_w_2, k_norm_w_2, nat_rpb_2, w_oa_2,
        w_ob_2, w_out_2, norm2_w_2, w_ffn_gate_2, w_ffn_up_2, w_ffn_down_2, final_w_2,
    )


_drawn_inputs = setup_inputs


def setup_inputs(seed=0):
    import zlib

    import numpy as np

    out = dict(_drawn_inputs(seed))
    spreads = {}
    factors = {'mla_q_norm': 8.0,
     'mla_kv_norm': 8.0,
     'ml_conv_b': 8.0,
     'ml_head_norm': 8.0,
     'b_ada_2': 3.21,
     'norm1_w_2': 8.0,
     'q_norm_w_2': 8.0,
     'k_norm_w_2': 8.0,
     'nat_rpb_2': 8.0,
     'norm2_w_2': 3.644}
    for name, (base, spread) in spreads.items():
        noise = np.random.default_rng([zlib.crc32(name.encode()), seed]).standard_normal(out[name].shape)
        drawn = base * np.exp(spread * noise) if base else spread * noise
        out[name] = __import__('jax').numpy.asarray(drawn.astype(out[name].dtype))
    for name, factor in factors.items():
        out[name] = (out[name] * factor).astype(out[name].dtype)
    return out
```

```python
from contextlib import ExitStack

import concourse.bass as bass
from concourse import mybir
import numpy as np

ALU = mybir.AluOpType
ACT = mybir.ActivationFunctionType
AX_X = mybir.AxisListType.X
F32 = mybir.dt.float32
F32R = mybir.dt.float32r
I32 = mybir.dt.int32

P = 128
SEQ = 256
TOK = SEQ // P
D = 2048
KD = D // P
COLS = 1024
HALF = 512
RING = 4
EPS = 1e-6
NEG = -3.0e38

MLA_H, NOPE, ROPE, LORA = 16, 128, 64, 512
MLA_SCALE = float(NOPE + ROPE) ** -0.5
ALPHA = 4.0 ** 0.25
ML_H, ML_QK, ML_V = 8, 128, 256
ML_SCALE = float(ML_QK) ** -0.5
TAPS = 4
N_A, N_KV, HD = 8, 2, 128
GRID_W, NA_COLS, REL_R, REL_C = 64, 16, 6, 31
HD_SCALE = float(HD) ** -0.5
D_FF = 5632
KF = D_FF // P
FFN_PASSES = D_FF // HALF

PACK = {}
for _name, _n in (("q_norm", 4), ("kv_norm", 4), ("ln_w0", 16), ("ln_b0", 16), ("head_norm", 16), ("conv_w", 64),
                  ("conv_b", 16), ("norm1", 16), ("norm2", 16), ("c", 16)):
    PACK[_name] = (sum(n for _, n in PACK.values()), _n)
N_PACK = sum(n for _, n in PACK.values())
CONST = {}
for _name, _n in (("ident", 128), ("inv_freq", 32), ("causal", 256), ("window", 64), ("toeplitz", 191),
                  ("cos", 128), ("sin", 128), ("select", 1024)):
    CONST[_name] = (sum(n for _, n in CONST.values()), _n)
N_CONST = sum(n for _, n in CONST.values())

B_C = 0
B_Z = B_C + 16
B_QN = B_Z + 32
B_QR = B_QN + 8
B_KN = B_QR + 4
B_V = B_KN + 8
B_MO = B_V + 8
B_CONV = B_MO + 32
B_VOZ = B_CONV + 32
B_LO = B_VOZ + 96
B_QA = B_LO + 32
B_KVA = B_QA + 16
B_QB = B_KVA + 8
B_KB = B_QB + 16
B_VB = B_KB + 16
B_MERGE = B_VB + 16
B_WO = B_MERGE + 96
B_FFN = B_WO + 32
B_DOWN = B_FFN + 16 * FFN_PASSES
N_BLOCKS = B_DOWN + 2 * KF

TURN_PLAN = (
    "c:dve kr:act z0:act z1:act cT:split8 qn0:act qn1:act qr:act kn0:dve kn1:dve v0:act v1:act qrT:act krT:act "
    "mo0:dve mo1:dve x1Ta:split8 x1Tb:split8 mlq:taps8 mlk:taps8 gates:act mv0:act gT:dve mv1:act mo_0:act mo_1:act "
    "mz0:act mz1:act lo0:dve lo1:dve ada1:dve g1:act hTa:split8 hTb:split8 qa:act kva:act qb:act kb:act vb:act "
    "qaT:act kaT:act biasa:dve biasb:dve ga0:act oa0:dve gb0:act ob0:dve ga1:act oa1:dve gb1:act ob1:dve "
    "mTa:split4 mTb:split4 wo0:dve wo1:dve ada2:dve h2Ta:split8 h2Tb:split8").split() \
    + [f"ffn{i}:product1" for i in range(FFN_PASSES)] + ["g2:act", "down0:dve", "down1:dve"]
TURN = {}
FREED = {}
SPLIT_BASE = {}
_total = {"act": 0, "dve": 0, "split": 0, "taps": 0, "product": 0}
for _t, _entry in enumerate(TURN_PLAN):
    _name, _who = _entry.split(":")
    _kind = _who.rstrip("0123456789")
    SPLIT_BASE[_name] = _total[_kind]
    _total[_kind] += int(_who[len(_kind):] or 1)
    TURN[_name] = _t
    FREED[_name] = (_kind, _total[_kind])

LAST_BLOCK = {"c": B_Z, "z0": B_Z + 16, "z1": B_QN, "qn0": B_QN + 4, "qn1": B_QR, "qr": B_KN, "kn0": B_KN + 4,
              "kn1": B_V, "v0": B_V + 4, "v1": B_MO, "mo0": B_MO + 16, "mo1": B_CONV, "mlq": B_CONV + 16,
              "mlk": B_VOZ, "lo0": B_LO + 16, "lo1": B_QA, "qa": B_KVA, "kva": B_QB, "qb": B_KB, "kb": B_VB,
              "vb": B_MERGE, "wo0": B_WO + 16, "wo1": B_FFN, "down0": B_DOWN + KF, "down1": B_DOWN + 2 * KF}
for _n, _name in enumerate(("mv0", "mv1", "mo_0", "mo_1", "mz0", "mz1")):
    LAST_BLOCK[_name] = B_VOZ + 16 * (_n + 1)
for _q in range(2):
    for _name, _end in (("ga", 16), ("oa", 24), ("gb", 40), ("ob", 48)):
        LAST_BLOCK[f"{_name}{_q}"] = B_MERGE + 48 * _q + _end
for _p in range(FFN_PASSES):
    LAST_BLOCK[f"ffn{_p}"] = B_FFN + 16 * (_p + 1)
TURN_COUNT = {}
for _entry in TURN_PLAN:
    _name = _entry.split(":")[0]
    if _name not in LAST_BLOCK:
        TURN_COUNT[_name] = len(TURN_COUNT) + 1

ADA_UNIT = {"z0": 0, "z1": 1, "mo0": 2, "mo1": 3, "mlq": 4, "mlk": 5, "mv0": 6, "mv1": 7,
            "mo_0": 8, "mo_1": 9, "mz0": 10, "mz1": 11,
            "qa": 12, "kva": 13, "qb": 14, "kb": 15, "vb": 16, "ga0": 17, "gb0": 18, "ga1": 19,
            "gb1": 20, "wo0": 21, "wo1": 22, "ffn0": 23}
N_UNITS = len(ADA_UNIT)


def two_block_kernel(nc, positions, x, xT, pack, const, gate_b, qk_norm, rpbT, mla_w_in, mla_w_qb, mla_w_kvb,
                     mla_w_out, ml_w_in, ml_w_out, ln_w, ln_b, w_ada, b_ada, w_in, w_oa, w_ob, w_out, w_gate, w_up,
                     w_down, final_w, out):
    K = 1024
    BASE = 16512
    with ExitStack() as ctx:
        def at(name, kb, shape, dt=F32):
            return nc.alloc_sbuf_tensor_at(name, shape, dt, offset=BASE + int(kb * K))

        def sem(name):
            return ctx.enter_context(nc.semaphore(name))

        raw = at("raw", 0, [P, RING, COLS])
        hi = at("hi", 16, [P, RING, COLS], F32R)
        lo = at("lo", 32, [P, RING, COLS], F32R)
        XH = at("XH", 48, [P, KD, SEQ], F32R)
        XL = at("XL", 64, [P, KD, SEQ], F32R)
        X = at("X", 80, [P, TOK, D])
        ada_raw = at("ada_raw", 96, [P, RING, HALF])
        acc_g = at("acc_g", 104, [P, D])
        acc_s = at("acc_s", 112, [P, 2, D])
        qT = at("qT", 48, [P, MLA_H, SEQ])
        kT = at("kT", 64, [P, MLA_H, SEQ])
        small_raw = at("small_raw", 128, [P, KD, ROPE])
        small_hi = at("small_hi", 132, [P, KD, ROPE], F32R)
        small_lo = at("small_lo", 136, [P, KD, ROPE], F32R)
        row_w = at("row_w", 128, [P, D])
        row_b = at("row_b", 136, [P, D])
        c_tok = at("c_tok", 144, [P, TOK, 2 * LORA])
        z_tok = at("z_tok", 152, [P, TOK, D])
        xT_raw = at("xT_raw", 168, [P, KD, SEQ])
        v_tok = at("v_tok", 168, [P, TOK, MLA_H * NOPE])
        CH = at("CH", 184, [P, 8, SEQ], F32R)
        CL = at("CL", 192, [P, 8, SEQ], F32R)
        qr_tok = at("qr_tok", 144, [P, TOK, MLA_H, ROPE])
        qrr_tok = at("qrr_tok", 136, [P, TOK, MLA_H, ROPE])
        qrT = at("qrT", 184, [P, MLA_H // 2, SEQ])
        rope_tmp = at("rope_tmp", 128, [P, 2, HALF])
        prob = at("prob", 192.5, [P, 2, SEQ])
        probT = at("probT", 194.5, [P, 2, SEQ])
        y_tok = at("y_tok", 196.5, [P, 4, P])
        nmax = at("nmax", 198.5, [P, 32])
        rsum = at("rsum", 198.625, [P, 32])
        rinv = at("rinv", 198.75, [P, 32])
        qkT = at("qkT", 144, [P, ML_H, 2, SEQ])
        h_tok = at("h_tok", 144, [P, ML_H, TOK, ML_V])
        mv = at("mv", 160, [P, TOK, ML_H, ML_V + 1])
        conv_tmp = at("conv_tmp", 177, [P, 8, SEQ])
        oz = at("oz", 176.5, [P, TOK, D])
        z_tmp = at("z_tmp", 136, [P, TOK, COLS])
        decay = at("decay", 192.5, [P, 2, 384])
        select = at("select", 195.5, [8, ML_H, P])
        h_norm = at("h_norm", 144, [P, TOK, D])
        qa_tok = at("qa_tok", 128, [P, TOK, N_A, HD])
        yaL = at("yaL", 128, [P, N_A, SEQ], F32R)
        g_row = at("g_row", 136, [P, D])
        qaT = at("qaT", 144, [P, N_A, SEQ])
        yaH = at("yaH", 144, [P, N_A, SEQ], F32R)
        qbT = at("qbT", 152, [P, N_A, SEQ])
        ybH = at("ybH", 152, [P, N_A, SEQ], F32R)
        kbT = at("kbT", 160, [P, N_A, SEQ])
        ybL = at("ybL", 160, [P, N_A, SEQ], F32R)
        vb_tok = at("vb_tok", 168, [P, TOK, N_A * HD])
        sig_a = at("sig_a", 168, [P, TOK, COLS])
        kva_tok = at("kva_tok", 176, [P, TOK, 4, HD])
        kaT = at("kaT", 180, [P, N_KV, SEQ])
        na_bias = at("na_bias", 182, [P, GRID_W, N_A, REL_R])
        prob2 = at("prob2", 194, [P, 2, SEQ])
        probT2 = at("probT2", 196, [P, 2, SEQ])
        y_tok2 = at("y_tok2", 198, [P, 4, P])
        merged = at("merged", 176, [P, TOK, D])
        FH = at("FH", 112, [P, KF, SEQ], F32R)
        FL = at("FL", 156, [P, KF, SEQ], F32R)
        xsq = at("xsq", 64, [P, D])
        g2_row = at("g2_row", 48, [P, D])
        final_row = at("final_row", 56, [P, D])
        tmp = at("tmp", 200, [P, COLS])
        ident = at("ident", 204, [P, P])
        ones = at("ones", 204.5, [P, P])
        pk = at("pk", 205, [P, N_PACK])
        c_act = at("c_act", 206, [P, 16])
        mods = at("mods", 206.0625, [P, 2, 16])
        A_col = at("A_col", 206.1875, [P, 16])
        st = at("st", 206.25, [P, TOK, 4, 6])
        mvar = at("mvar", 206.4375, [P, TOK, 2])
        ss = at("ss", 206.46875, [P, 32])
        ra = at("ra", 206.59375, [P, 32])
        ry = at("ry", 206.71875, [P, 32])
        rt = at("rt", 206.84375, [P, 32])
        nmax2 = at("nmax2", 206.96875, [P, 32])
        rsum2 = at("rsum2", 207.09375, [P, 32])
        rinv2 = at("rinv2", 207.21875, [P, 32])
        kr_tok = at("kr_tok", 104, [P, TOK, ROPE])
        krr_tok = at("krr_tok", 104.5, [P, TOK, 2, ROPE])
        krT = at("krT", 105.5, [P, SEQ])
        ang = at("ang", 106.5, [P, TOK, 32])
        rot = at("rot", 106.75, [P, TOK, 32])
        turns_n = at("turns_n", 107, [P, TOK, 32])
        cos_t = at("cos_t", 107.25, [P, TOK, 32])
        sin_t = at("sin_t", 107.5, [P, TOK, 32])
        pos_i = at("pos_i", 107.75, [P, TOK], I32)
        pos_f = at("pos_f", 107.78125, [P, TOK])
        inv_freq = at("inv_freq", 107.8125, [P, 32])
        gate_tok = at("gate_tok", 128, [P, TOK, 16])
        gate_bias = at("gate_bias", 128.25, [8, 2])
        gi = at("gi", 129, [8, SEQ])
        gf = at("gf", 130, [8, SEQ])
        ge = at("ge", 131, [8, SEQ])
        gF = at("gF", 132, [8, SEQ])
        gM = at("gM", 133, [8, SEQ])
        causal = at("causal", 134, [P, SEQ])
        G_col = at("G_col", 135, [P, TOK, ML_H])
        E_col = at("E_col", 135.0625, [P, TOK, ML_H])
        dens = at("dens", 135.125, [P, 16])
        dinv = at("dinv", 135.1875, [P, 16])
        cos2 = at("cos2", 188, [P, TOK, HD // 2])
        sin2 = at("sin2", 188.5, [P, TOK, HD // 2])
        qkn = at("qkn", 189, [P, 2, HD])
        window = at("window", 195.25, [P, GRID_W])
        toep = at("toep", 194, [64, 191])
        rel = at("rel", 195, [64, N_A, REL_R])
        rope2 = at("rope2", 190, [P, 2, HALF])

        ps = ctx.enter_context(nc.psum_tensor("ps", [P, 8 * HALF], F32))

        w_landed = [sem(f"w_landed{i}") for i in range(RING)]
        hi_ready, lo_ready = sem("hi_ready"), sem("lo_ready")
        block_done = sem("block_done")
        turn_done = sem("turn_done")
        tile_split = sem("tile_split")
        taps_done = sem("taps_done")
        product_done = sem("product_done")
        freed_sem = {"act": sem("act_freed"), "dve": sem("dve_freed"), "split": tile_split, "taps": taps_done,
                     "product": product_done}
        ada_landed = [sem(f"ada_landed{i}") for i in range(RING)]
        ada_used = sem("ada_used")
        acc_zero = sem("acc_zero")
        bias_landed = [sem(f"bias_landed{i}") for i in range(4)]
        s_dve, s_act = sem("s_dve"), sem("s_act")
        events = {}

        def ev(name):
            if name not in events:
                events[name] = sem("e_" + name)
            return events[name]

        def att_sems(tag):
            return {n: sem(f"{tag}_{n}") for n in ("scored", "maxed", "exped", "turned", "copied", "summed", "scaled",
                                                   "backed", "hi", "lo")}

        A1, A3 = att_sems("mla"), att_sems("blk")
        M2 = {n: sem(f"ml_{n}") for n in ("prep", "prepc", "st", "bc", "arg", "exp", "w", "pv", "h", "sq", "y", "yT",
                                          "hi", "lo")}

        def col(name, k):
            o = PACK[name][0] + k
            return pk[:, o:o + 1]

        def complete(name):
            return (block_done, LAST_BLOCK[name]) if name in LAST_BLOCK else (turn_done, TURN_COUNT[name])

        def grp(name):
            return (TURN[name] % 2) * 4 * HALF

        def T(name, tok, w=COLS):
            g = grp(name) + tok * 2 * HALF
            return ps[:, g:g + w]

        def landed(n, j):
            two = max(0, min(n + 1, B_DOWN) - B_FFN)
            two = (two + RING - 1 - j) // RING if two > 0 else 0
            return 16 * (n // RING + 1 + two)

        def acc_part(u):
            vec, part = u // 4, (u % 4) * HALF
            if vec in (2, 5):
                return acc_g[:, part:part + HALF], 1 if vec == 2 else 3
            return acc_s[:, vec % 3, part:part + HALF], 0 if vec < 2 else 2

        flat = "p a b -> p (a b)"
        block = ctx.enter_context(nc.Block())

        @block.sync
        def _(sp):
            def rows(w, k):
                return w[bass.ds(k * P, P), :] if not isinstance(k, int) else w[k * P:(k + 1) * P, :]

            def stream(n0, nb, source):
                first = 0
                if n0 == 0:
                    for j in range(RING):
                        dst, src = source(j, j)
                        sp.dma_start(dst, src).then_inc(w_landed[j], 16)
                    first = 1
                with sp.Fori(first, nb // RING) as g:
                    for j in range(RING):
                        dst, src = source(RING * g + j, j)
                        sp.wait_ge(lo_ready, n0 + RING * g + j - RING + 1)
                        sp.dma_start(dst, src).then_inc(w_landed[j], 16)

            def plain(w, c0):
                return lambda k, j: (raw[:, j, :], rows(w, k)[:, c0:c0 + COLS])

            def head_cols(w, per, h0, nh, off, width):
                def source(k, j):
                    src = rows(w, k).rearrange("p (h e) -> p h e", e=per)[:, h0:h0 + nh, off:off + width]
                    return raw[:, j, :].rearrange("p (h e) -> p h e", e=width), src
                return source

            xT_v = xT.rearrange("(k p) t -> p k t", p=P)
            for q in range(2):
                sp.dma_start(xT_raw[:, 8 * q:8 * q + 8, :], xT_v[:, 8 * q:8 * q + 8, :]).then_inc(ev(f"xT{q}"), 16)
            w = mla_w_in[0]
            stream(B_C, 16, plain(w, 0))
            for q in range(2):
                stream(B_Z + 16 * q, 16, plain(w, 2 * LORA + ROPE + q * COLS))
            for q in range(2):
                stream(B_QN + 4 * q, 4, head_cols(mla_w_qb[0], NOPE + ROPE, 8 * q, 8, 0, NOPE))
            stream(B_QR, 4, head_cols(mla_w_qb[0], NOPE + ROPE, 0, 16, NOPE, ROPE))
            for q in range(2):
                stream(B_KN + 4 * q, 4, head_cols(mla_w_kvb[0], 2 * NOPE, 8 * q, 8, 0, NOPE))
            for q in range(2):
                stream(B_V + 4 * q, 4, head_cols(mla_w_kvb[0], 2 * NOPE, 8 * q, 8, NOPE, NOPE))
            for q in range(2):
                stream(B_MO + 16 * q, 16, plain(mla_w_out[0], q * COLS))
            for q in range(6):
                stream(B_CONV + 16 * q, 16, plain(ml_w_in[0], q * COLS))
            for q in range(2):
                stream(B_VOZ + 64 + 16 * q, 16, plain(ml_w_in[0], 6160 + q * COLS))
            for q in range(2):
                stream(B_LO + 16 * q, 16, plain(ml_w_out[0], q * COLS))
            w = w_in[0]
            stream(B_QA, 16, plain(w, 0))
            pairs = w.rearrange("(b a p) n -> b p a n", a=2, p=P)

            def two_rows(k, j):
                src = pairs[k] if isinstance(k, int) else pairs[bass.ds(k, 1), :, :, :].rearrange("b p a n -> (b p) a n")
                return raw[:, j, :].rearrange("p (a n) -> p a n", a=2), src[:, :, COLS:COLS + HALF]

            stream(B_KVA, 8, two_rows)
            for q in range(3):
                stream(B_QB + 16 * q, 16, plain(w, 1536 + q * COLS))
            for q in range(2):
                n0 = B_MERGE + 48 * q
                stream(n0, 16, plain(w, 4608 + q * COLS))
                stream(n0 + 16, 8, plain(w_oa[0], q * COLS))
                stream(n0 + 24, 16, plain(w, 6656 + q * COLS))
                stream(n0 + 40, 8, plain(w_ob[0], q * COLS))
            for q in range(2):
                stream(B_WO + 16 * q, 16, plain(w_out[0], q * COLS))
            with sp.Fori(0, FFN_PASSES) as q:
                with sp.Fori(0, KD // RING) as g:
                    for j in range(RING):
                        for part, mat in enumerate((w_gate[0], w_up[0])):
                            sp.wait_ge(lo_ready, 16 * q + (RING * g + (B_FFN + j - RING + 1)))
                            sp.dma_start(raw[:, j, part * HALF:(part + 1) * HALF],
                                         mat[bass.ds((RING * g + j) * P, P), bass.ds(q * HALF, HALF)]) \
                              .then_inc(w_landed[j], 16)
            for q in range(2):
                stream(B_DOWN + KF * q, KF, plain(w_down[0], q * COLS))
            for tok in range(TOK):
                sp.wait_ge(ev("result"), tok + 1)
                sp.dma_start(out[0, tok * P:(tok + 1) * P, :], X[:, tok, :]).then_inc(ev("stored"), 16)
            sp.wait_ge(ev("stored"), 32)

        @block.gpsimd
        def _(pool):
            def load(name, dst, src):
                pool.dma_start(dst, src).then_inc(ev(name), 16)

            def cst(name, p0=0, p1=P):
                o, n = CONST[name]
                return const[p0:p1, o:o + n]

            def bcast(dst, row):
                return dst, row.partition_broadcast(P)

            def ada_units(u0, u1):
                def four(u, g, wait):
                    for j in range(RING):
                        if wait:
                            pool.wait_ge(ada_used, 16 * u + (RING * g + (j - RING + 1)))
                        pool.dma_start(ada_raw[:, j, :],
                                       w_ada[0][bass.ds((RING * g + j) * P, P), bass.ds(u * HALF, HALF)]) \
                            .then_inc(ada_landed[j], 16)
                if u0 == 0:
                    four(0, 0, False)
                    with pool.Fori(1, KD // RING) as g:
                        four(0, g, True)
                    u0 = 1
                with pool.Fori(u0, u1) as u:
                    with pool.Fori(0, KD // RING) as g:
                        four(u, g, True)

            def init_acc(i, acc, b0, n, zeroed):
                nc.gpsimd.memset(acc, 0.0).then_inc(acc_zero, 1)
                pool.wait_ge(acc_zero, zeroed)
                pool.dma_start(acc[0:1, :], b_ada[0:1, b0:b0 + n]).then_inc(bias_landed[i], 16)

            load("pack", pk[:, :], pack)
            load("ident", ident[:, :], cst("ident"))
            load("pos", pos_i[:, :], positions)
            load("inv_freq", inv_freq[:, :], cst("inv_freq"))
            load("small1", small_raw[:, :, :], mla_w_in[0][:, 2 * LORA:2 * LORA + ROPE].rearrange("(k p) n -> p k n", p=P))
            load("x", X[:, :, :], x[0].rearrange("(a p) n -> p a n", p=P))
            init_acc(0, acc_s[:, :, :].rearrange(flat), 0, 2 * D, 1)
            ada_units(0, 4)
            pool.wait_ge(ev("q_roped"), 2)
            pool.wait_ge(*complete("qrT"))
            load("rows0", *bcast(row_w[:, :], ln_w[0:1, :]))
            load("rows0", *bcast(row_b[:, :], ln_b[0:1, :]))
            ada_units(4, 5)
            pool.wait_ge(ev("x1_rows"), 4)
            load("small2", small_raw[:, :, 0:16], ml_w_in[0][:, 6144:6160].rearrange("(k p) n -> p k n", p=P))
            init_acc(1, acc_g[:, :], 2 * D, D, 2)
            ada_units(5, 6)
            pool.wait_ge(*complete("gates"))
            load("gate_bias", gate_bias[:, :], gate_b)
            load("causal", causal[:, :], cst("causal"))
            load("select", select[:, :, :].rearrange(flat), cst("select", 0, 8))
            ada_units(6, 12)
            pool.wait_ge(M2["lo"], 16)
            load("rows1", *bcast(row_w[:, :], ln_w[1:2, :]))
            load("rows1", *bcast(row_b[:, :], ln_b[1:2, :]))
            load("tables2", cos2[:, :, :].rearrange(flat), cst("cos"))
            load("tables2", sin2[:, :, :].rearrange(flat), cst("sin"))
            load("tables2", qkn[:, 0, :], qk_norm[0:1, :].partition_broadcast(P))
            load("tables2", qkn[:, 1, :], qk_norm[1:2, :].partition_broadcast(P))
            load("toep", toep[:, :], cst("toeplitz", 0, 64))
            load("window", window[:, :], cst("window"))
            nc.gpsimd.memset(rel[:, :, :], 0.0).then_inc(ev("rel_zero"), 1)
            pool.wait_ge(ev("rel_zero"), 1)
            load("rel", rel[0:31, :, :], rpbT[:, :, 5:11])
            load("rel", rel[32:63, :, :], rpbT[:, :, 4:10])
            pool.wait_ge(*complete("ada1"))
            init_acc(2, acc_s[:, :, :].rearrange(flat), 3 * D, 2 * D, 3)
            pool.wait_ge(*complete("g1"))
            init_acc(3, acc_g[:, :], 5 * D, D, 4)
            ada_units(12, N_UNITS)
            pool.wait_ge(*complete("ffn10"))
            load("final_row", *bcast(final_row[:, :], final_w))

        @block.scalar
        def _(act):
            own = [0]

            def link(ins):
                own[0] += 1
                ins.then_inc(s_act, 1)
                act.wait_ge(s_act, own[0])

            def hi_block(n, j, count):
                act.wait_ge(w_landed[j], count)
                if not isinstance(n, int) or n >= RING:
                    act.wait_ge(block_done, n - RING + 1)
                nc.scalar.copy(hi[:, j, :], raw[:, j, :]).then_inc(hi_ready, 1)

            def first4(n0):
                for j in range(RING):
                    hi_block(n0 + j, j, landed(n0 + j, j))

            def rest(n0, nb):
                c0 = landed(n0, 0)
                with act.Fori(1, nb // RING) as g:
                    for j in range(RING):
                        hi_block(RING * g + (n0 + j), j, 16 * g + c0)

            def turn(name):
                act.wait_ge(*complete(name))
                return grp(name)

            def each_tok(name, dst, func=None, scale=1.0, width=COLS, src=lambda ap: ap):
                turn(name)
                for tok in range(TOK):
                    if func is not None:
                        ins = nc.scalar.activation(dst(tok), src(T(name, tok, width)), func)
                    elif scale != 1.0:
                        ins = nc.scalar.mul(dst(tok), src(T(name, tok, width)), scale)
                    else:
                        ins = nc.scalar.copy(dst(tok), src(T(name, tok, width)))
                ins.then_inc(freed_sem["act"], 1)

            def whole(name, dst, scale=1.0, width=4 * HALF):
                g = turn(name)
                src = ps[:, g:g + width]
                (nc.scalar.mul(dst, src, scale) if scale != 1.0 else nc.scalar.copy(dst, src)) \
                    .then_inc(freed_sem["act"], 1)

            def operand_full(names, event, gain, shift):
                for n, name in enumerate(names):
                    g = turn(name)
                    for k in range(8):
                        kk = 8 * n + k
                        if kk >= 4:
                            act.wait_ge(tile_split, SPLIT_BASE[names[0]] + kk - 3)
                        nc.scalar.activation(tmp[:, (kk % 4) * SEQ:(kk % 4 + 1) * SEQ],
                                             ps[:, g + k * SEQ:g + (k + 1) * SEQ], ACT.Identity,
                                             scale=gain(kk), bias=shift(kk)).then_inc(ev(event), 1)

            def attention(S, units, pr, prT, nm, rs, keys, H):
                for i in range(units + 4):
                    if i < units:
                        u = i
                        nk = keys(u)
                        act.wait_ge(S["maxed"], u + 1)
                        if u >= 2:
                            act.wait_ge(S["turned"], u - 1)
                        nc.scalar.activation(pr[:, u % 2, 0:nk], ps[:, (u % 2) * HALF:(u % 2) * HALF + nk], ACT.Exp,
                                             bias=nm[:, u:u + 1], accum_out=rs[:, u:u + 1]).then_inc(S["exped"], 1)
                    if 1 <= i <= units:
                        u = i - 1
                        nk = keys(u)
                        b = (2 + u % 2) * HALF
                        act.wait_ge(S["turned"], u + 1)
                        if u >= 2:
                            act.wait_ge(S["summed"], u - 1)
                        nc.scalar.copy(prT[:, u % 2, 0:nk], ps[:, b:b + nk]).then_inc(S["copied"], 1)
                    if i >= 4 and i % 2 == 0:
                        h = (i - 4) // 2
                        b = (6 + h % 2) * HALF
                        act.wait_ge(S["backed"], h + 1)
                        nc.scalar.copy(H(h), ps[:, b:b + SEQ]).then_inc(S["hi"], 1)

            for q in range(4):
                act.wait_ge(ev(f"xT{q // 2}"), 16)
                nc.scalar.copy(XH[:, 4 * q:4 * q + 4, :], xT_raw[:, 4 * q:4 * q + 4, :]).then_inc(ev("x_hi"), 1)
            first4(B_C)
            act.wait_ge(ev("pack"), 16)
            nc.scalar.activation(c_act[:, :], pk[:, PACK["c"][0]:PACK["c"][0] + 16], ACT.Silu).then_inc(ev("c_act"), 1)
            rest(B_C, 16)
            act.wait_ge(ev("small1"), 16)
            nc.scalar.copy(small_hi[:, :, :], small_raw[:, :, :]).then_inc(ev("small_hi"), 1)
            first4(B_Z)
            act.wait_ge(ev("angles"), 1)
            nc.scalar.activation(sin_t[:, :, :], rot[:, :, :], ACT.Sin).then_inc(ev("sincos"), 1)
            nc.scalar.activation(cos_t[:, :, :], ang[:, :, :], ACT.Sin).then_inc(ev("sincos"), 1)
            g = turn("c")
            for i in range(4):
                if i >= 2:
                    act.wait_ge(ev("c_squares"), i - 1)
                nc.scalar.activation(tmp[:, (i % 2) * HALF:(i % 2 + 1) * HALF], ps[:, g + i * HALF:g + (i + 1) * HALF],
                                     ACT.Square, accum_out=ss[:, i:i + 1]).then_inc(ev("c_squares"), 1)
            each_tok("kr", lambda t: kr_tok[:, t, :], width=ROPE)
            rest(B_Z, 16)
            first4(B_Z + 16)
            each_tok("z0", lambda t: z_tok[:, t, 0:COLS], ACT.Silu)
            rest(B_Z + 16, 16)
            first4(B_QN)
            each_tok("z1", lambda t: z_tok[:, t, COLS:], ACT.Silu)
            g = turn("cT")
            for k in range(8):
                nc.scalar.mul(CH[:, k, :], ps[:, g + k * SEQ:g + (k + 1) * SEQ],
                              col("q_norm", k) if k < 4 else col("kv_norm", k - 4)).then_inc(ev("c_hi"), 1)
            first4(B_QN + 4)
            whole("qn0", qT[:, 0:8, :].rearrange(flat), MLA_SCALE)
            first4(B_QR)
            whole("qn1", qT[:, 8:16, :].rearrange(flat), MLA_SCALE)
            first4(B_KN)
            each_tok("qr", lambda t: qr_tok[:, t].rearrange(flat), None, MLA_SCALE)
            first4(B_KN + 4)
            first4(B_V)
            first4(B_V + 4)
            each_tok("v0", lambda t: v_tok[:, t, 0:COLS])
            first4(B_MO)
            each_tok("v1", lambda t: v_tok[:, t, COLS:])
            whole("qrT", qrT[:, :, :].rearrange(flat))
            whole("krT", krT[:, :], width=SEQ)
            attention(A1, 32, prob, probT, nmax, rsum, lambda u: P * (1 + u % 2), lambda h: XH[:, h, :])
            rest(B_MO, 16)
            first4(B_MO + 16)
            rest(B_MO + 16, 16)
            first4(B_CONV)
            operand_full(("x1Ta", "x1Tb"), "x1_full", lambda k: col("ln_w0", k), lambda k: col("ln_b0", k))
            rest(B_CONV, 16)

            for q, name in enumerate(("mlq", "mlk")):
                first4((B_CONV + 16, B_VOZ)[q])
                g = turn(name)
                for k in range(8):
                    f = 8 * q + k
                    nc.scalar.activation(conv_tmp[:, k, :], ps[:, g + k * SEQ:g + (k + 1) * SEQ], ACT.Identity,
                                         scale=col("conv_w", 3 * 16 + f), bias=col("conv_b", f)) \
                      .then_inc(ev("last_tap"), 1)
                for k in range(8):
                    act.wait_ge(taps_done, 8 * q + k + 1)
                    nc.scalar.activation(qkT[:, k, q, :], conv_tmp[:, k, :], ACT.Silu).then_inc(ev("qk"), 1)
                if q == 0:
                    rest(B_CONV + 16, 16)
                    act.wait_ge(ev("small2"), 16)
                    nc.scalar.copy(small_hi[:, :, 0:16], small_raw[:, :, 0:16]).then_inc(ev("small_hi"), 1)
            each_tok("gates", lambda t: gate_tok[:, t, :], width=16)
            rest(B_VOZ, 16)
            first4(B_VOZ + 16)

            def v_out(name, q):
                each_tok(name, lambda t: mv[:, t, 4 * q:4 * q + 4, 0:ML_V],
                         src=lambda ap: ap.rearrange("p (h e) -> p h e", e=ML_V))

            v_out("mv0", 0)
            act.wait_ge(ev("neg_abs"), 1)
            link(nc.scalar.activation(ge[:, :], ge[:, :], ACT.Exp))
            nc.scalar.activation(ge[:, :], ge[:, :], ACT.Ln, bias=1.0).then_inc(ev("log1p"), 1)
            rest(B_VOZ + 16, 16)
            act.wait_ge(ev("stabiliser"), 1)
            nc.scalar.activation(gF[:, :], gF[:, :], ACT.Exp, scale=-1.0).then_inc(ev("exp_m"), 1)
            first4(B_VOZ + 32)
            v_out("mv1", 1)
            rest(B_VOZ + 32, 16)
            first4(B_VOZ + 48)
            each_tok("mo_0", lambda t: oz[:, t, 0:COLS], ACT.Sigmoid)
            rest(B_VOZ + 48, 16)
            first4(B_VOZ + 64)
            each_tok("mo_1", lambda t: oz[:, t, COLS:], ACT.Sigmoid)
            rest(B_VOZ + 64, 16)
            first4(B_VOZ + 80)
            each_tok("mz0", lambda t: z_tmp[:, t, :], ACT.Silu)
            rest(B_VOZ + 80, 16)
            first4(B_LO)
            act.wait_ge(ev("z_used"), 1)
            each_tok("mz1", lambda t: z_tmp[:, t, :], ACT.Silu)
            for i in range(ML_H + 2):
                if i < ML_H:
                    act.wait_ge(M2["arg"], i + 1)
                    nc.scalar.activation(decay[:, i % 2, :], decay[:, i % 2, :], ACT.Exp).then_inc(M2["exp"], 1)
                if i >= 2:
                    h = i - 2
                    for tok in range(TOK):
                        u = 2 * h + tok
                        act.wait_ge(M2["h"], u + 1)
                        if u >= 4:
                            act.wait_ge(M2["sq"], u - 3)
                        nc.scalar.activation(tmp[:, (u % 4) * ML_V:(u % 4 + 1) * ML_V], h_tok[:, h, tok, :], ACT.Square,
                                             accum_out=ss[:, u:u + 1]).then_inc(M2["sq"], 1)
            for h in range(ML_H):
                act.wait_ge(M2["yT"], h + 1)
                for half in range(2):
                    k = 2 * h + half
                    nc.scalar.mul(XH[:, k, :], ps[:, h * HALF + half * SEQ:h * HALF + (half + 1) * SEQ],
                                  col("head_norm", k)).then_inc(M2["hi"], 1)
            rest(B_LO, 16)
            first4(B_LO + 16)
            rest(B_LO + 16, 16)

            first4(B_QA)
            for tok in range(TOK):
                act.wait_ge(ev("x2_rows"), tok + 1)
                nc.scalar.activation(h_norm[:, tok, :], X[:, tok, :], ACT.Square, accum_out=ss[:, tok:tok + 1]) \
                  .then_inc(ev("x_squares"), 1)
            whole("g1", g_row[:, :])
            act.wait_ge(freed_sem["dve"], FREED["ada1"][1])
            operand_full(("hTa", "hTb"), "h_full", lambda k: A_col[:, k:k + 1], lambda k: mods[:, 0, k:k + 1])
            rest(B_QA, 16)
            first4(B_KVA)
            each_tok("qa", lambda t: qa_tok[:, t].rearrange(flat))
            rest(B_KVA, 8)
            first4(B_QB)
            each_tok("kva", lambda t: kva_tok[:, t].rearrange(flat), width=HALF)
            rest(B_QB, 16)
            first4(B_KB)
            whole("qb", qbT[:, :, :].rearrange(flat), HD_SCALE)
            rest(B_KB, 16)
            first4(B_VB)
            whole("kb", kbT[:, :, :].rearrange(flat))
            rest(B_VB, 16)
            first4(B_MERGE)
            each_tok("vb", lambda t: vb_tok[:, t, :])
            whole("qaT", qaT[:, :, :].rearrange(flat), HD_SCALE)
            whole("kaT", kaT[:, :, :].rearrange(flat), width=2 * SEQ)
            attention(A3, 32, prob2, probT2, nmax2, rsum2, lambda u: SEQ,
                      lambda h: yaH[:, h, :] if h < N_A else ybH[:, h - N_A, :])
            rest(B_MERGE, 16)
            for q in range(2):
                n0 = B_MERGE + 48 * q
                first4(n0 + 16)
                if q == 1:
                    act.wait_ge(freed_sem["dve"], FREED["ob0"][1])
                each_tok(f"ga{q}", lambda t: sig_a[:, t, :], ACT.Sigmoid)
                rest(n0 + 16, 8)
                first4(n0 + 24)
                rest(n0 + 24, 16)
                first4(n0 + 40)
                act.wait_ge(freed_sem["dve"], FREED[f"oa{q}"][1])
                each_tok(f"gb{q}", lambda t: sig_a[:, t, :], ACT.Sigmoid)
                rest(n0 + 40, 8)
                first4(n0 + 48)
                if q == 0:
                    rest(n0 + 48, 16)
            for n, name in enumerate(("mTa", "mTb")):
                g = turn(name)
                for k in range(4):
                    nc.scalar.copy(XH[:, 8 * n + 2 * k:8 * n + 2 * k + 2, :].rearrange(flat),
                                   ps[:, g + k * HALF:g + (k + 1) * HALF]).then_inc(ev("m_hi"), 1)
            rest(B_WO, 16)
            first4(B_WO + 16)
            rest(B_WO + 16, 16)
            first4(B_FFN)
            for tok in range(TOK):
                act.wait_ge(ev("x3"), tok + 1)
                nc.scalar.activation(h_norm[:, tok, :], X[:, tok, :], ACT.Square, accum_out=ss[:, tok:tok + 1]) \
                  .then_inc(ev("x_squares"), 1)
            act.wait_ge(freed_sem["dve"], FREED["ada2"][1])
            operand_full(("h2Ta", "h2Tb"), "h2_full", lambda k: A_col[:, k:k + 1], lambda k: mods[:, 0, k:k + 1])

            def ffn_blocks(p, g0, g1):
                def four(g):
                    for j in range(RING):
                        hi_block(16 * p + (RING * g + (B_FFN + j)), j, 128 * p + (32 * g + landed(B_FFN, 0)))
                if g1 - g0 == 1:
                    four(g0)
                else:
                    with act.Fori(g0, g1) as g:
                        four(g)

            def ffn_out(p, parity):
                act.wait_ge(block_done, 16 * p + (B_FFN + 16))
                if not isinstance(p, int) or p > 0:
                    act.wait_ge(ev("ffn_lo"), p)
                g = ((TURN["ffn0"] + parity) % 2) * 4 * HALF
                nc.scalar.activation(tmp[:, :], ps[:, g:g + COLS], ACT.Silu).then_inc(ev("ffn_silu"), 1)
                act.wait_ge(product_done, p + 1)
                dst = FH[:, 4 * p:4 * p + 4, :] if isinstance(p, int) else FH[:, bass.ds(4 * p, 4), :]
                nc.scalar.copy(dst, tmp[:, :].rearrange("p (k t) -> p k t", k=4)).then_inc(ev("ffn_hi"), 1)

            ffn_blocks(0, 1, 4)
            for s in range(2):
                ffn_blocks(1 + s, 0, 1)
                ffn_out(s, s)
                ffn_blocks(1 + s, 1, 4)
            with act.Fori(1, (FFN_PASSES - 1) // 2) as i:
                for s in range(2):
                    ffn_blocks(2 * i + (1 + s), 0, 1)
                    ffn_out(2 * i + s, s)
                    ffn_blocks(2 * i + (1 + s), 1, 4)
            first4(B_DOWN)
            ffn_out(FFN_PASSES - 1, 0)
            whole("g2", g2_row[:, :])
            rest(B_DOWN, KF)
            first4(B_DOWN + KF)
            rest(B_DOWN + KF, KF)
            for tok in range(TOK):
                act.wait_ge(ev("x4"), tok + 1)
                act.wait_ge(ev("x_squares"), 4 + tok)
                nc.scalar.activation(xsq[:, :], X[:, tok, :], ACT.Square, accum_out=ss[:, tok:tok + 1]) \
                  .then_inc(ev("x_squares"), 1)

        @block.vector
        def _(dve):
            own = [0]

            def mark(ins):
                own[0] += 1
                ins.then_inc(s_dve, 1)
                return own[0]

            def after(n):
                dve.wait_ge(s_dve, n)

            def link(ins):
                after(mark(ins))

            def lo_block(n, j):
                dve.wait_ge(hi_ready, n + 1)
                nc.vector.tensor_tensor(lo[:, j, :], raw[:, j, :], hi[:, j, :].bitcast(F32), ALU.subtract) \
                  .then_inc(lo_ready, 1)

            def ada_block(u, k):
                acc, init = acc_part(u)
                m = 16 * u + k
                if k == 0:
                    dve.wait_ge(bias_landed[init], 16)
                else:
                    dve.wait_ge(ada_used, m)
                dve.wait_ge(ada_landed[m % RING], 16 * (m // RING + 1))
                nc.vector.scalar_tensor_tensor(out=acc, in0=ada_raw[:, m % RING, :], scalar=c_act[:, k:k + 1], in1=acc,
                                               op0=ALU.mult, op1=ALU.add).then_inc(ada_used, 1)

            def first4(n0):
                for j in range(RING):
                    lo_block(n0 + j, j)

            def rest(n0, nb, name=None, hooks=()):
                if name not in ADA_UNIT and not hooks:
                    with dve.Fori(1, nb // RING) as g:
                        for j in range(RING):
                            lo_block(RING * g + (n0 + j), j)
                    return
                k = 0
                for b in range(nb - RING):
                    lo_block(n0 + RING + b, b % RING)
                    while name in ADA_UNIT and k * (nb - RING) < 16 * (b + 1):
                        ada_block(ADA_UNIT[name], k)
                        k += 1
                    if b < len(hooks):
                        hooks[b]()

            def turn(name):
                dve.wait_ge(*complete(name))
                return grp(name)

            def free(ins):
                ins.then_inc(freed_sem["dve"], 1)

            def rsqrt(n, scale, src):
                a, y, t = ra[:, 0:n], ry[:, 0:n], rt[:, 0:n]
                link(nc.vector.tensor_scalar(a, src, scale, EPS, ALU.mult, ALU.add))
                link(nc.vector.tensor_scalar(t.bitcast(I32), a.bitcast(I32), 1, None, ALU.logical_shift_right))
                link(nc.vector.tensor_scalar(y.bitcast(I32), t.bitcast(I32), -1.0, 1597463007.0, ALU.mult, ALU.add))
                for _i in range(4):
                    link(nc.vector.scalar_tensor_tensor(out=t, in0=y, scalar=-0.5, in1=y, op0=ALU.mult, op1=ALU.mult))
                    link(nc.vector.tensor_tensor(t, t, a, ALU.mult))
                    link(nc.vector.scalar_tensor_tensor(out=y, in0=t, scalar=1.5, in1=y, op0=ALU.add, op1=ALU.mult))

            def rotate(out1, out2, x1, x2, c, s, t1, t2):
                mark(nc.vector.tensor_tensor(t1, x1, c, ALU.mult))
                link(nc.vector.tensor_tensor(t2, x2, s, ALU.mult))
                link(nc.vector.tensor_tensor(out1, t1, t2, ALU.subtract))
                mark(nc.vector.tensor_tensor(t1, x1, s, ALU.mult))
                link(nc.vector.tensor_tensor(t2, x2, c, ALU.mult))
                return nc.vector.tensor_tensor(out2, t1, t2, ALU.add)

            def residual(name, q):
                turn(name)
                for tok in range(TOK):
                    xs = X[:, tok, q * COLS:(q + 1) * COLS]
                    ins = nc.vector.scalar_tensor_tensor(out=xs, in0=xs, scalar=ALPHA, in1=T(name, tok), op0=ALU.mult,
                                                         op1=ALU.add)
                    if tok == 0:
                        mark(ins)
                free(ins)

            def standardise(freed):
                after(own[0])
                dve.wait_ge(freed_sem["dve"], freed)
                for tok in range(TOK):
                    for n in range(4):
                        n_last = mark(nc.vector.bn_stats(st[:, tok, n, :], X[:, tok, n * HALF:(n + 1) * HALF]))
                after(n_last)
                for tok in range(TOK):
                    link(nc.vector.bn_aggr(mvar[:, tok, :], st[:, tok, :, :]))
                rsqrt(TOK, 1.0, mvar[:, :, 1])
                for tok in range(TOK):
                    nc.vector.tensor_scalar(X[:, tok, :], X[:, tok, :], mvar[:, tok, 0:1], ry[:, tok:tok + 1],
                                            ALU.subtract, ALU.mult).then_inc(ev("normed"), 1)

            def split_operand(first, event):
                for k in range(KD):
                    src = tmp[:, (k % 4) * SEQ:(k % 4 + 1) * SEQ]
                    dve.wait_ge(ev(event), k + 1)
                    link(nc.vector.tensor_copy(XH[:, k, :], src))
                    nc.vector.tensor_tensor(XL[:, k, :], src, XH[:, k, :].bitcast(F32), ALU.subtract) \
                      .then_inc(tile_split, 1)

            def attention(S, units, nm, rs, ri, yt, keys, prepare, gate, H, L):
                for i in range(units + 4):
                    if i < units:
                        u = i
                        nk = keys(u)
                        b = (u % 2) * HALF
                        dve.wait_ge(S["scored"], u + 1)
                        prepare(u, b, nk)
                        nc.vector.tensor_reduce(nm[:, u:u + 1], ps[:, b:b + nk], AX_X, ALU.max, negate=True) \
                          .then_inc(S["maxed"], 1)
                    if 2 <= i < units + 2:
                        u = i - 2
                        b = (4 + u % 2) * HALF
                        dve.wait_ge(S["exped"], u + 1)
                        link(nc.vector.reciprocal(ri[:, u:u + 1], rs[:, u:u + 1]))
                        dve.wait_ge(S["summed"], u + 1)
                        if u >= 4:
                            dve.wait_ge(S["backed"], (u - 4) // 2 + 1)
                        if gate is None:
                            ins = nc.vector.tensor_scalar(yt[:, u % 4, :], ps[:, b:b + P], ri[:, u:u + 1], None,
                                                          ALU.mult)
                        else:
                            ins = nc.vector.scalar_tensor_tensor(out=yt[:, u % 4, :], in0=ps[:, b:b + P],
                                                                 scalar=ri[:, u:u + 1], in1=gate(u), op0=ALU.mult,
                                                                 op1=ALU.mult)
                        ins.then_inc(S["scaled"], 1)
                    if i >= 4 and i % 2 == 0:
                        h = (i - 4) // 2
                        b = (6 + h % 2) * HALF
                        dve.wait_ge(S["hi"], h + 1)
                        nc.vector.tensor_tensor(L(h), ps[:, b:b + SEQ], H(h).bitcast(F32), ALU.subtract) \
                          .then_inc(S["lo"], 1)

            nc.vector.memset(ones[:, :], 1.0).then_inc(ev("ones"), 1)
            for q in range(4):
                dve.wait_ge(ev("x_hi"), q + 1)
                nc.vector.tensor_tensor(XL[:, 4 * q:4 * q + 4, :], xT_raw[:, 4 * q:4 * q + 4, :],
                                        XH[:, 4 * q:4 * q + 4, :].bitcast(F32), ALU.subtract).then_inc(ev("x_lo"), 1)
            first4(B_C)
            dve.wait_ge(ev("pos"), 16)
            dve.wait_ge(ev("inv_freq"), 16)
            link(nc.vector.tensor_copy(pos_f[:, :], pos_i[:, :]))
            for tok in range(TOK):
                n_last = mark(nc.vector.tensor_scalar(ang[:, tok, :], inv_freq[:, :], pos_f[:, tok:tok + 1], None,
                                                      ALU.mult))
            after(n_last)
            magic = 12582912.0
            link(nc.vector.tensor_scalar(turns_n[:, :, :], ang[:, :, :], 1.0 / (2 * np.pi), magic, ALU.mult, ALU.add))
            link(nc.vector.tensor_scalar(turns_n[:, :, :], turns_n[:, :, :], magic, None, ALU.subtract))
            left = 2 * np.pi
            src = ang
            for part in range(4):
                c = float(np.float32(left))
                if part < 3:
                    e = int(np.floor(np.log2(left)))
                    c = float(np.floor(left / 2.0 ** (e - 7)) * 2.0 ** (e - 7))
                left -= c
                link(nc.vector.scalar_tensor_tensor(out=rot[:, :, :], in0=turns_n[:, :, :], scalar=-c, in1=src[:, :, :],
                                                    op0=ALU.mult, op1=ALU.add))
                src = rot
            link(nc.vector.tensor_scalar(ang[:, :, :], rot[:, :, :], float(np.pi / 2), None, ALU.add))
            link(nc.vector.tensor_scalar(turns_n[:, :, :], ang[:, :, :], float(np.pi), -2 * float(np.pi), ALU.is_gt,
                                         ALU.mult))
            link(nc.vector.tensor_tensor(ang[:, :, :], ang[:, :, :], turns_n[:, :, :], ALU.add))
            mark(nc.vector.tensor_scalar(ang[:, :, :], ang[:, :, :], 3.1415925, -3.1415925, ALU.min, ALU.max))
            nc.vector.tensor_scalar(rot[:, :, :], rot[:, :, :], 3.1415925, -3.1415925, ALU.min, ALU.max) \
              .then_inc(ev("angles"), 1)
            rest(B_C, 16)
            dve.wait_ge(ev("small_hi"), 1)
            nc.vector.tensor_tensor(small_lo[:, :, :], small_raw[:, :, :], small_hi[:, :, :].bitcast(F32),
                                    ALU.subtract).then_inc(ev("small_lo"), 1)
            first4(B_Z)
            g = turn("c")
            dve.wait_ge(ev("c_squares"), 4)
            rsqrt(4, 1.0 / LORA, ss[:, 0:4])
            for i in range(4):
                ins = nc.vector.tensor_scalar(c_tok[:, i // 2, (i % 2) * LORA:(i % 2 + 1) * LORA],
                                              ps[:, g + i * HALF:g + (i + 1) * HALF], ry[:, i:i + 1], None, ALU.mult)
            free(ins)
            dve.wait_ge(ev("sincos"), 2)
            dve.wait_ge(freed_sem["act"], FREED["kr"][1])
            t1, t2 = (rope_tmp[:, i, 0:64].rearrange("p (a b) -> p a b", a=TOK) for i in range(2))
            link(rotate(krr_tok[:, :, 0, 0:32], krr_tok[:, :, 0, 32:64], kr_tok[:, :, 0:32], kr_tok[:, :, 32:64],
                        cos_t[:, :, :], sin_t[:, :, :], t1, t2))
            nc.vector.tensor_copy(krr_tok[:, :, 1, :], krr_tok[:, :, 0, :]).then_inc(ev("k_roped"), 1)
            dve.wait_ge(ev("c_act"), 1)
            rest(B_Z, 16, "z0")
            first4(B_Z + 16)
            rest(B_Z + 16, 16, "z1")
            first4(B_QN)
            g = turn("cT")
            for k in range(8):
                dve.wait_ge(ev("c_hi"), (k | 1) + 1)
                nc.vector.scalar_tensor_tensor(out=CL[:, k, :], in0=ps[:, g + k * SEQ:g + (k + 1) * SEQ],
                                               scalar=col("q_norm", k) if k < 4 else col("kv_norm", k - 4),
                                               in1=CH[:, k, :].bitcast(F32), op0=ALU.mult, op1=ALU.subtract) \
                  .then_inc(tile_split, 1)
            first4(B_QN + 4)
            first4(B_QR)
            first4(B_KN)
            first4(B_KN + 4)
            g = turn("kn0")
            free(nc.vector.tensor_copy(kT[:, 0:8, :].rearrange(flat), ps[:, g:g + 4 * HALF]))
            first4(B_V)
            g = turn("kn1")
            free(nc.vector.tensor_copy(kT[:, 8:16, :].rearrange(flat), ps[:, g:g + 4 * HALF]))
            dve.wait_ge(freed_sem["act"], FREED["qr"][1])
            for tok in range(TOK):
                t1, t2 = (rope_tmp[:, i, :].rearrange("p (h e) -> p h e", h=16) for i in range(2))
                if tok:
                    dve.wait_ge(ev("q_roped"), tok)
                c, s = (tab[:, tok, :].unsqueeze(1).broadcast_to([P, 16, 32]) for tab in (cos_t, sin_t))
                rotate(qrr_tok[:, tok, :, 0:32], qrr_tok[:, tok, :, 32:64], qr_tok[:, tok, :, 0:32],
                       qr_tok[:, tok, :, 32:64], c, s, t1, t2).then_inc(ev("q_roped"), 1)
                if tok == 0:
                    first4(B_V + 4)
            first4(B_MO)

            def mask_chunk(u, b, nk):
                link(nc.vector.memset(ps[0:64, b + nk - 64:b + nk], NEG))

            attention(A1, 32, nmax, rsum, rinv, y_tok, lambda u: P * (1 + u % 2), mask_chunk,
                      lambda u: z_tok[:, u % 2, (u // 2) * P:(u // 2 + 1) * P],
                      lambda h: XH[:, h, :], lambda h: XL[:, h, :])
            rest(B_MO, 16, "mo0")
            first4(B_MO + 16)
            dve.wait_ge(ev("x"), 16)
            residual("mo0", 0)
            rest(B_MO + 16, 16, "mo1")
            first4(B_CONV)
            residual("mo1", 1)
            standardise(FREED["mo1"][1])
            split_operand("x1Ta", "x1_full")

            def x1_rows(i):
                def do():
                    tok = i // 2
                    if i == 0:
                        dve.wait_ge(ev("rows0"), 32)
                        dve.wait_ge(*complete("x1Tb"))
                    if i % 2:
                        dve.wait_ge(ev("x1_rows"), i)
                    nc.vector.tensor_tensor(X[:, tok, :], X[:, tok, :], (row_b if i % 2 else row_w)[:, :],
                                            ALU.add if i % 2 else ALU.mult).then_inc(ev("x1_rows"), 1)
                return do

            skip = lambda: None
            rest(B_CONV, 16, "mlq", [skip, x1_rows(0), skip, skip, x1_rows(1), skip, skip, x1_rows(2), skip, skip,
                                     x1_rows(3)])

            for q, name in enumerate(("mlq", "mlk")):
                first4((B_CONV + 16, B_VOZ)[q])
                g = turn(name)
                n0 = own[0]
                for s in range(1, TAPS):
                    for k in range(8):
                        if s == 1:
                            dve.wait_ge(ev("last_tap"), 8 * q + (k | 1) + 1)
                        else:
                            after(n0 + 8 * (s - 2) + k + 1)
                        f = 8 * q + k
                        ins = nc.vector.scalar_tensor_tensor(
                            out=conv_tmp[:, k, s:], in0=ps[:, g + k * SEQ:g + (k + 1) * SEQ - s],
                            scalar=col("conv_w", (TAPS - 1 - s) * 16 + f), in1=conv_tmp[:, k, s:],
                            op0=ALU.mult, op1=ALU.add)
                        ins.then_inc(taps_done, 1) if s == TAPS - 1 else mark(ins)
                if q == 0:
                    rest(B_CONV + 16, 16, "mlk")
                    dve.wait_ge(ev("small_hi"), 2)
                    nc.vector.tensor_tensor(small_lo[:, :, 0:16], small_raw[:, :, 0:16],
                                            small_hi[:, :, 0:16].bitcast(F32), ALU.subtract) \
                      .then_inc(ev("small_lo"), 1)
            for tok in range(TOK):
                n_last = mark(nc.vector.memset(mv[:, tok, :, ML_V:ML_V + 1], 1.0))
            rest(B_VOZ, 16, "mv0")
            first4(B_VOZ + 16)
            g = turn("gT")
            dve.wait_ge(ev("gate_bias"), 16)
            mark(nc.vector.tensor_scalar(gi[:, :], ps[0:8, g:g + SEQ], gate_bias[:, 0:1], None, ALU.add))
            free(nc.vector.tensor_scalar(gf[:, :], ps[0:8, g + HALF:g + HALF + SEQ], gate_bias[:, 1:2], None, ALU.add))
            dve.wait_ge(freed_sem["dve"], FREED["gT"][1])
            link(nc.vector.tensor_scalar(ge[:, :], gf[:, :], -1.0, None, ALU.mult))
            nc.vector.tensor_tensor(ge[:, :], ge[:, :], gf[:, :], ALU.min).then_inc(ev("neg_abs"), 1)
            link(nc.vector.memset(gM[:, :], 1.0))
            dve.wait_ge(ev("log1p"), 1)
            link(nc.vector.scalar_tensor_tensor(out=gf[:, :], in0=gf[:, :], scalar=0.0, in1=ge[:, :], op0=ALU.min,
                                                op1=ALU.subtract))
            link(nc.vector.tensor_tensor_scan(gF[:, :], gM[:, :], gf[:, :], 0.0, ALU.mult, ALU.add))
            link(nc.vector.tensor_tensor(gi[:, :], gi[:, :], gF[:, :], ALU.subtract))
            link(nc.vector.tensor_tensor_scan(gM[:, :], gi[:, :], gi[:, :], 0.0, ALU.max, ALU.max))
            mark(nc.vector.tensor_scalar(ge[:, :], gM[:, :], -1.0, None, ALU.mult))
            nc.vector.tensor_tensor(gF[:, :], gF[:, :], gM[:, :], ALU.add).then_inc(ev("stabiliser"), 1)
            rest(B_VOZ + 16, 16, "mv1")
            first4(B_VOZ + 32)
            rest(B_VOZ + 32, 16, "mo_0")
            first4(B_VOZ + 48)
            rest(B_VOZ + 48, 16, "mo_1")
            first4(B_VOZ + 64)
            rest(B_VOZ + 64, 16, "mz0")
            first4(B_VOZ + 80)

            def gate_z(name, q):
                dve.wait_ge(freed_sem["act"], FREED[name][1])
                for tok in range(TOK):
                    o = oz[:, tok, q * COLS:(q + 1) * COLS]
                    ins = nc.vector.tensor_tensor(o, o, z_tmp[:, tok, :], ALU.mult)
                    if tok == 0:
                        mark(ins)
                ins.then_inc(ev("z_used"), 1)

            gate_z("mz0", 0)
            rest(B_VOZ + 80, 16, "mz1")
            first4(B_LO)
            gate_z("mz1", 1)
            dve.wait_ge(M2["prep"], 1)
            mark(nc.vector.tensor_copy(G_col[:, :, :].rearrange(flat), ps[:, 6 * HALF:6 * HALF + 16]))
            nc.vector.tensor_copy(E_col[:, :, :].rearrange(flat), ps[:, 6 * HALF + 16:6 * HALF + 32]) \
              .then_inc(M2["prepc"], 1)
            dve.wait_ge(M2["prepc"], 1)
            after(own[0])
            dve.wait_ge(ev("causal"), 16)
            for i in range(ML_H + 2):
                if i < ML_H:
                    h = i
                    b = (2 + h % 2) * HALF
                    dve.wait_ge(M2["bc"], h + 1)
                    if h >= 2:
                        dve.wait_ge(M2["pv"], 2 * (h - 1))
                    mark(nc.vector.scalar_tensor_tensor(out=decay[:, h % 2, 0:SEQ], in0=ps[:, b:b + SEQ],
                                                        scalar=G_col[:, 0, h:h + 1], in1=causal[:, :], op0=ALU.add,
                                                        op1=ALU.add))
                    nc.vector.scalar_tensor_tensor(out=decay[:, h % 2, SEQ:SEQ + P], in0=ps[:, b + P:b + SEQ],
                                                   scalar=G_col[:, 1, h:h + 1], in1=causal[:, 0:P], op0=ALU.add,
                                                   op1=ALU.add).then_inc(M2["arg"], 1)
                if 1 <= i <= ML_H:
                    h = i - 1
                    b = (h % 2) * HALF
                    dve.wait_ge(M2["exp"], h + 1)
                    dve.wait_ge(M2["st"], h + 1)
                    nc.vector.scalar_tensor_tensor(out=decay[:, h % 2, :], in0=ps[:, b:b + 384], scalar=ML_SCALE,
                                                   in1=decay[:, h % 2, :], op0=ALU.mult, op1=ALU.mult) \
                      .then_inc(M2["w"], 1)
                if i >= 2:
                    h = i - 2
                    for tok in range(TOK):
                        u = 2 * h + tok
                        b = (4 + u % 4) * HALF
                        dve.wait_ge(M2["pv"], u + 1)
                        d = dens[:, u:u + 1]
                        link(nc.vector.tensor_scalar(d, ps[:, b + ML_V:b + ML_V + 1], -1.0, None, ALU.mult))
                        link(nc.vector.tensor_tensor(d, d, ps[:, b + ML_V:b + ML_V + 1], ALU.max))
                        link(nc.vector.tensor_tensor(d, d, E_col[:, tok, h:h + 1], ALU.max))
                        link(nc.vector.reciprocal(dinv[:, u:u + 1], d))
                        nc.vector.tensor_scalar(h_tok[:, h, tok, :], ps[:, b:b + ML_V], dinv[:, u:u + 1], None,
                                                ALU.mult).then_inc(M2["h"], 1)
            dve.wait_ge(M2["sq"], 16)
            dve.wait_ge(ev("z_used"), 2)
            rsqrt(16, 1.0 / ML_V, ss[:, 0:16])
            for u in range(16):
                h, tok = u // 2, u % 2
                o = oz[:, tok, h * ML_V:(h + 1) * ML_V]
                nc.vector.scalar_tensor_tensor(out=o, in0=h_tok[:, h, tok, :], scalar=ry[:, u:u + 1], in1=o,
                                               op0=ALU.mult, op1=ALU.mult).then_inc(M2["y"], 1)
            for k in range(KD):
                b = (k // 2) * HALF + (k % 2) * SEQ
                dve.wait_ge(M2["hi"], (k | 1) + 1)
                nc.vector.scalar_tensor_tensor(out=XL[:, k, :], in0=ps[:, b:b + SEQ], scalar=col("head_norm", k),
                                               in1=XH[:, k, :].bitcast(F32), op0=ALU.mult, op1=ALU.subtract) \
                  .then_inc(M2["lo"], 1)
            rest(B_LO, 16)
            first4(B_LO + 16)
            residual("lo0", 0)
            rest(B_LO + 16, 16)
            first4(B_QA)
            residual("lo1", 1)

            standardise(FREED["lo1"][1])
            dve.wait_ge(ev("normed"), 4)
            dve.wait_ge(ev("rows1"), 32)
            for tok in range(TOK):
                link(nc.vector.tensor_tensor(X[:, tok, :], X[:, tok, :], row_w[:, :], ALU.mult))
                nc.vector.tensor_tensor(X[:, tok, :], X[:, tok, :], row_b[:, :], ALU.add).then_inc(ev("x2_rows"), 1)

            def modulation(name, norm):
                g = turn(name)
                mark(nc.vector.tensor_copy(mods[:, 0, :], ps[:, g:g + 16]))
                o = PACK[norm][0]
                free(nc.vector.scalar_tensor_tensor(out=A_col[:, :], in0=ps[:, g + 16:g + 32], scalar=1.0,
                                                    in1=pk[:, o:o + 16], op0=ALU.add, op1=ALU.mult))

            def rms_rows(n_squares, event):
                dve.wait_ge(ev("x_squares"), n_squares)
                rsqrt(TOK, 1.0 / D, ss[:, 0:TOK])
                for tok in range(TOK):
                    nc.vector.tensor_scalar(h_norm[:, tok, :], X[:, tok, :], ry[:, tok:tok + 1], None, ALU.mult) \
                      .then_inc(ev(event), 1)

            modulation("ada1", "norm1")
            rms_rows(2, "h_normed")
            split_operand("hTa", "h_full")
            rest(B_QA, 16, "qa")
            first4(B_KVA)
            rest(B_KVA, 8, "kva")
            first4(B_QB)

            def norm_heads(x, heads, which):
                sq = tmp[:, 0:heads * HD].rearrange("p (h e) -> p h e", e=HD)

                def squares():
                    link(nc.vector.tensor_tensor(sq, x, x, ALU.mult))
                    link(nc.vector.tensor_reduce(ss[:, 0:heads], sq, AX_X, ALU.add))

                def scale():
                    rsqrt(heads, 1.0 / HD, ss[:, 0:heads])
                    link(nc.vector.tensor_tensor(x, x, ry[:, 0:heads].unsqueeze(2).broadcast_to([P, heads, HD]),
                                                 ALU.mult))

                def gain():
                    link(nc.vector.tensor_tensor(x, x, qkn[:, which, :].unsqueeze(1).broadcast_to([P, heads, HD]),
                                                 ALU.mult))
                return [squares, scale, gain]

            roped = [0]

            def rope_heads(x, heads, tok, event):
                v = x.rearrange("p h (i two) -> p h i two", two=2)
                x0, x1 = v[:, :, :, 0], v[:, :, :, 1]
                w = heads * HD // 2
                sh = "p (h i) -> p h i"
                t = [rope2[:, 0, 0:w].rearrange(sh, h=heads), rope2[:, 1, 0:w].rearrange(sh, h=heads),
                     tmp[:, 0:w].rearrange(sh, h=heads), tmp[:, HALF:HALF + w].rearrange(sh, h=heads)]
                c, s = (tab[:, tok, :].unsqueeze(1).broadcast_to([P, heads, HD // 2]) for tab in (cos2, sin2))

                def products():
                    mark(nc.vector.tensor_tensor(t[0], x0, c, ALU.mult))
                    mark(nc.vector.tensor_tensor(t[1], x1, s, ALU.mult))

                def products2():
                    mark(nc.vector.tensor_tensor(t[2], x0, s, ALU.mult))
                    link(nc.vector.tensor_tensor(t[3], x1, c, ALU.mult))

                def sums():
                    mark(nc.vector.tensor_tensor(x0, t[0], t[1], ALU.subtract))
                    nc.vector.tensor_tensor(x1, t[2], t[3], ALU.add).then_inc(ev(event), 1)
                    roped[0] += 1
                    dve.wait_ge(ev(event), roped[0])
                return [products, products2, sums]

            def wait_tables():
                dve.wait_ge(ev("tables2"), 64)
                dve.wait_ge(freed_sem["act"], FREED["qa"][1])

            def wait_kva():
                dve.wait_ge(freed_sem["act"], FREED["kva"][1])

            steps = []
            for tok in range(TOK):
                steps += norm_heads(qa_tok[:, tok], N_A, 0) + rope_heads(qa_tok[:, tok], N_A, tok, "qk_roped")
            for tok in range(TOK):
                steps += norm_heads(kva_tok[:, tok, 0:N_KV], N_KV, 1) \
                    + rope_heads(kva_tok[:, tok, 0:N_KV], N_KV, tok, "qk_roped")
            rest(B_QB, 16, "qb", [wait_tables] + steps[0:10])
            first4(B_KB)
            wait_kva()
            rest(B_KB, 16, "kb", steps[10:22])
            first4(B_VB)
            rest(B_VB, 16, "vb", steps[22:])
            first4(B_MERGE)
            dve.wait_ge(ev("window"), 16)
            dve.wait_ge(ev("qk_roped"), 4)
            for name, kc0, kc1 in (("biasa", 0, 40), ("biasb", 40, GRID_W)):
                g = turn(name)
                for c0 in range(kc0, kc1, 10):
                    n = min(10, kc1 - c0)
                    o = g + (c0 - kc0) // 10 * HALF
                    ins = nc.vector.tensor_tensor(
                        na_bias[:, c0:c0 + n].rearrange("p c h i -> p c (h i)"),
                        ps[:, o:o + n * N_A * REL_R].rearrange("p (c x) -> p c x", c=n),
                        window[:, c0:c0 + n].unsqueeze(2).broadcast_to([P, n, N_A * REL_R]), ALU.add)
                    if c0 + 10 < kc1:
                        mark(ins)
                free(ins)
            after(own[0])
            dve.wait_ge(freed_sem["dve"], FREED["biasb"][1])

            def add_bias(u, b, nk):
                if u >= 16:
                    h, blk = (u - 16) // 2, u % 2
                    i0 = 2 - 2 * blk
                    v = ps[:, b:b + SEQ].rearrange("p (r c) -> p r c", r=4)
                    link(nc.vector.tensor_tensor(v, v, na_bias[:, :, h, i0:i0 + 4].rearrange("p c r -> p r c"),
                                                 ALU.add))

            attention(A3, 32, nmax2, rsum2, rinv2, y_tok2, lambda u: SEQ, add_bias, None,
                      lambda h: yaH[:, h, :] if h < N_A else ybH[:, h - N_A, :],
                      lambda h: yaL[:, h, :] if h < N_A else ybL[:, h - N_A, :])
            rest(B_MERGE, 16, "ga0")
            for q in range(2):
                n0 = B_MERGE + 48 * q
                first4(n0 + 16)
                rest(n0 + 16, 8)
                first4(n0 + 24)
                turn(f"oa{q}")
                dve.wait_ge(freed_sem["act"], FREED[f"ga{q}"][1])
                for tok in range(TOK):
                    ins = nc.vector.tensor_tensor(merged[:, tok, q * COLS:(q + 1) * COLS], T(f"oa{q}", tok),
                                                  sig_a[:, tok, :], ALU.mult)
                    if tok == 0:
                        mark(ins)
                free(ins)
                rest(n0 + 24, 16, f"gb{q}")
                first4(n0 + 40)
                rest(n0 + 40, 8)
                first4(n0 + 48)
                turn(f"ob{q}")
                dve.wait_ge(freed_sem["act"], FREED[f"gb{q}"][1])
                for tok in range(TOK):
                    m = merged[:, tok, q * COLS:(q + 1) * COLS]
                    link(nc.vector.tensor_tensor(tmp[:, :], T(f"ob{q}", tok), sig_a[:, tok, :], ALU.mult))
                    if tok == 0:
                        dve.wait_ge(freed_sem["dve"], FREED[f"oa{q}"][1])
                        link(nc.vector.tensor_tensor(m, m, tmp[:, :], ALU.add))
                    else:
                        free(nc.vector.tensor_tensor(m, m, tmp[:, :], ALU.add))
                if q == 0:
                    rest(n0 + 48, 16, "ga1")
            for k in range(8):
                if k % 4 == 0:
                    g = turn(("mTa", "mTb")[k // 4])
                dve.wait_ge(ev("m_hi"), k + 1)
                nc.vector.tensor_tensor(XL[:, 2 * k:2 * k + 2, :].rearrange(flat),
                                        ps[:, g + (k % 4) * HALF:g + (k % 4 + 1) * HALF],
                                        XH[:, 2 * k:2 * k + 2, :].rearrange(flat).bitcast(F32), ALU.subtract) \
                  .then_inc(tile_split, 1)

            def gated_residual(name, q, row, event):
                turn(name)
                for tok in range(TOK):
                    xs = X[:, tok, q * COLS:(q + 1) * COLS]
                    ins = nc.vector.tensor_tensor(tmp[:, :], T(name, tok), row[:, q * COLS:(q + 1) * COLS], ALU.mult)
                    if tok == 0:
                        link(ins)
                    else:
                        free(ins)
                        dve.wait_ge(freed_sem["dve"], FREED[name][1])
                    ins = nc.vector.tensor_tensor(xs, xs, tmp[:, :], ALU.add)
                    if q == 1:
                        ins.then_inc(ev(event), 1)
                        dve.wait_ge(ev(event), tok + 1)
                    else:
                        link(ins)

            rest(B_WO, 16, "wo0")
            first4(B_WO + 16)
            dve.wait_ge(freed_sem["act"], FREED["g1"][1])
            gated_residual("wo0", 0, g_row, "x3")
            rest(B_WO + 16, 16, "wo1")
            first4(B_FFN)
            gated_residual("wo1", 1, g_row, "x3")
            modulation("ada2", "norm2")
            dve.wait_ge(ev("x3"), 2)
            rms_rows(4, "h_normed")
            split_operand("h2Ta", "h2_full")

            def ffn_blocks(p, g0, g1):
                def four(g):
                    for j in range(RING):
                        lo_block(16 * p + (RING * g + (B_FFN + j)), j)
                if g1 - g0 == 1:
                    four(g0)
                else:
                    with dve.Fori(g0, g1) as g:
                        four(g)

            def ffn_out(p, parity):
                g = ((TURN["ffn0"] + parity) % 2) * 4 * HALF
                dve.wait_ge(ev("ffn_silu"), p + 1)
                nc.vector.tensor_tensor(tmp[:, :], tmp[:, :], ps[:, g + COLS:g + 2 * COLS], ALU.mult) \
                  .then_inc(product_done, 1)
                dve.wait_ge(ev("ffn_hi"), p + 1)
                sl = (slice(None), slice(4 * p, 4 * p + 4) if isinstance(p, int) else bass.ds(4 * p, 4), slice(None))
                nc.vector.tensor_tensor(FL[sl], tmp[:, :].rearrange("p (k t) -> p k t", k=4), FH[sl].bitcast(F32),
                                        ALU.subtract).then_inc(ev("ffn_lo"), 1)

            rest(B_FFN, 16, "ffn0")
            for s in range(2):
                ffn_blocks(1 + s, 0, 1)
                ffn_out(s, s)
                ffn_blocks(1 + s, 1, 4)
            with dve.Fori(1, (FFN_PASSES - 1) // 2) as i:
                for s in range(2):
                    ffn_blocks(2 * i + (1 + s), 0, 1)
                    ffn_out(2 * i + s, s)
                    ffn_blocks(2 * i + (1 + s), 1, 4)
            first4(B_DOWN)
            ffn_out(FFN_PASSES - 1, 0)
            rest(B_DOWN, KF)
            first4(B_DOWN + KF)
            dve.wait_ge(freed_sem["act"], FREED["g2"][1])
            gated_residual("down0", 0, g2_row, "x4")
            rest(B_DOWN + KF, KF)
            gated_residual("down1", 1, g2_row, "x4")
            dve.wait_ge(ev("x_squares"), 6)
            dve.wait_ge(ev("final_row"), 16)
            rsqrt(TOK, 1.0 / D, ss[:, 0:TOK])
            for tok in range(TOK):
                nc.vector.scalar_tensor_tensor(out=X[:, tok, :], in0=X[:, tok, :], scalar=ry[:, tok:tok + 1],
                                               in1=final_row[:, :], op0=ALU.mult, op1=ALU.mult) \
                  .then_inc(ev("result"), 1)

        @block.tensor
        def _(pe):
            mm = nc.tensor.matmul

            def start(name):
                t = TURN[name]
                if t >= 2:
                    kind, n = FREED[TURN_PLAN[t - 2].split(":")[0]]
                    pe.wait_ge(freed_sem[kind], n)
                return grp(name)

            def done(ins):
                ins.then_inc(turn_done, 1)

            def token_major(name, n0, nb, H, L, need=None, width=COLS, per_block=1, close=True):
                g = start(name)
                for b in range(nb):
                    j = b % RING
                    pe.wait_ge(lo_ready, n0 + b + 1)
                    for sub in range(per_block):
                        k = b * per_block + sub
                        if need is not None:
                            pe.wait_ge(*need(k))
                        for tok in range(TOK):
                            xh, xl = (m[:, k, tok * P:(tok + 1) * P] for m in (H, L))
                            for x, w, first in ((xh, hi, k == 0), (xh, lo, False), (xl, hi, False)):
                                for c in range(COLS // per_block // HALF):
                                    o = g + (2 * tok + c) * HALF
                                    c0 = (sub + c) * HALF
                                    ins = mm(ps[:, o:o + HALF], x, w[:, j, c0:c0 + HALF], start=first,
                                             stop=(k == nb * per_block - 1 and x is xl), skip_group_check=True)
                    ins.then_inc(block_done, 1)

            def feature_block(g, k, j, H, L, first, last):
                for m in range(8):
                    for w, x, lead in ((hi, H, True), (hi, L, False), (lo, H, False)):
                        o = g + m * SEQ
                        ins = mm(ps[:, o:o + SEQ], w[:, j, m * P:(m + 1) * P], x(k),
                                 start=first and lead and m % 2 == 0, stop=last and w is lo, skip_group_check=True)
                ins.then_inc(block_done, 1)

            def feature_major(name, n0, nb, H, L, need=None):
                g = start(name)
                for j in range(RING):
                    pe.wait_ge(lo_ready, n0 + j + 1)
                    if need is not None:
                        pe.wait_ge(need[0], need[1] + j + 1)
                    feature_block(g, j, j, lambda k: H[:, k, :], lambda k: L[:, k, :], j == 0,
                                  nb == RING and j == RING - 1)
                if nb > RING:
                    with pe.Fori(1, nb // RING) as gg:
                        for j in range(RING):
                            pe.wait_ge(lo_ready, RING * gg + (n0 + j + 1))
                            if need is not None:
                                pe.wait_ge(need[0], RING * gg + (need[1] + j + 1))
                            feature_block(g, RING * gg + j, j, lambda k: H[:, bass.ds(k, 1), :].rearrange(flat),
                                          lambda k: L[:, bass.ds(k, 1), :].rearrange(flat), False, True)

            def small_linear(name, n, count):
                g = start(name)
                pe.wait_ge(ev("small_lo"), count)
                for tok in range(TOK):
                    for k in range(KD):
                        o = g + 2 * tok * HALF
                        for x, w in ((XH, small_hi), (XH, small_lo), (XL, small_hi)):
                            ins = mm(ps[:, o:o + n], x[:, k, tok * P:(tok + 1) * P], w[:, k, 0:n],
                                     start=(k == 0 and x is XH and w is small_hi), stop=(k == KD - 1 and x is XL),
                                     skip_group_check=True)
                done(ins)

            def transposes(name, tiles):
                g = start(name)
                for o, src in tiles:
                    ins = nc.tensor.transpose(ps[0:src.shape[1], g + o:g + o + P], src, ident[:, :])
                done(ins)

            def operand_tiles(src, k0):
                return [(k * SEQ + tok * P, src[:, tok, (k0 + k) * P:(k0 + k + 1) * P])
                        for k in range(8) for tok in range(TOK)]

            def attention(S, units, pr, prT, yt, keys, operands, values):
                for i in range(units + 4):
                    if i < units:
                        u = i
                        nk = keys(u)
                        b = (u % 2) * HALF
                        if u >= 2:
                            pe.wait_ge(S["exped"], u - 1)
                        ops = operands(u)
                        for n, (q, kk) in enumerate(ops):
                            ins = mm(ps[:, b:b + nk], q, kk, start=(n == 0), stop=(n == len(ops) - 1),
                                     skip_group_check=True)
                        ins.then_inc(S["scored"], 1)
                    if 1 <= i <= units:
                        u = i - 1
                        b = (2 + u % 2) * HALF
                        pe.wait_ge(S["exped"], u + 1)
                        if u >= 2:
                            pe.wait_ge(S["copied"], u - 1)
                        for t in range(keys(u) // P):
                            ins = nc.tensor.transpose(ps[:, b + t * P:b + (t + 1) * P], pr[:, u % 2, t * P:(t + 1) * P],
                                                      ident[:, :])
                        ins.then_inc(S["turned"], 1)
                    if 2 <= i < units + 2:
                        u = i - 2
                        b = (4 + u % 2) * HALF
                        pe.wait_ge(S["copied"], u + 1)
                        if u >= 2:
                            pe.wait_ge(S["scaled"], u - 1)
                        n = keys(u) // P
                        for t in range(n):
                            ins = mm(ps[:, b:b + P], prT[:, u % 2, t * P:(t + 1) * P], values(u, t), start=(t == 0),
                                     stop=(t == n - 1), skip_group_check=True)
                        ins.then_inc(S["summed"], 1)
                    if i >= 4 and i % 2 == 0:
                        h = (i - 4) // 2
                        b = (6 + h % 2) * HALF
                        pe.wait_ge(S["scaled"], 2 * h + 2)
                        if h >= 2:
                            pe.wait_ge(S["lo"], h - 1)
                        for tok in range(TOK):
                            ins = nc.tensor.transpose(ps[:, b + tok * P:b + (tok + 1) * P], yt[:, (2 * h + tok) % 4, :],
                                                      ident[:, :])
                        ins.then_inc(S["backed"], 1)

            pe.wait_ge(ev("ones"), 1)
            token_major("c", B_C, 16, XH, XL, lambda k: (ev("x_lo"), k // 4 + 1))
            small_linear("kr", ROPE, 1)
            for q in range(2):
                token_major(f"z{q}", B_Z + 16 * q, 16, XH, XL)
            pe.wait_ge(ev("ident"), 16)
            transposes("cT", operand_tiles(c_tok, 0))
            for q in range(2):
                feature_major(f"qn{q}", B_QN + 4 * q, 4, CH, CL, (tile_split, 0))
            token_major("qr", B_QR, 4, CH, CL)
            CHv, CLv = CH[:, 4:8, :], CL[:, 4:8, :]
            for q in range(2):
                feature_major(f"kn{q}", B_KN + 4 * q, 4, CHv, CLv, (tile_split, 4))
            for q in range(2):
                token_major(f"v{q}", B_V + 4 * q, 4, CHv, CLv)
            pe.wait_ge(ev("q_roped"), 2)
            transposes("qrT", [(k * SEQ + tok * P, qrr_tok[:, tok, 2 * k:2 * k + 2, :].rearrange(flat))
                               for k in range(8) for tok in range(TOK)])
            pe.wait_ge(ev("k_roped"), 1)
            transposes("krT", [(tok * P, krr_tok[:, tok].rearrange(flat)) for tok in range(TOK)])
            pe.wait_ge(freed_sem["act"], FREED["krT"][1])

            def mla_operands(u):
                h, blk = u // 2, u % 2
                r0 = (h % 2) * ROPE
                t, nk = slice(blk * P, (blk + 1) * P), P * (1 + blk)
                return [(qT[:, h, t], kT[:, h, 0:nk]), (qrT[r0:r0 + ROPE, h // 2, t], krT[r0:r0 + ROPE, 0:nk])]

            attention(A1, 32, prob, probT, y_tok, lambda u: P * (1 + u % 2), mla_operands,
                      lambda u, t: v_tok[:, t, (u // 2) * P:(u // 2 + 1) * P])
            token_major("mo0", B_MO, 16, XH, XL, lambda k: (A1["lo"], k + 1))
            token_major("mo1", B_MO + 16, 16, XH, XL)
            pe.wait_ge(ev("normed"), 2)
            transposes("x1Ta", operand_tiles(X, 0))
            transposes("x1Tb", operand_tiles(X, 8))

            feature_major("mlq", B_CONV, 16, XH, XL, (tile_split, SPLIT_BASE["x1Ta"]))
            feature_major("mlk", B_CONV + 16, 16, XH, XL)
            small_linear("gates", 16, 2)
            token_major("mv0", B_VOZ, 16, XH, XL)
            g = start("gT")
            pe.wait_ge(freed_sem["act"], FREED["gates"][1])
            for half in range(2):
                for tok in range(TOK):
                    o = g + half * HALF + tok * P
                    ins = nc.tensor.transpose(ps[0:8, o:o + P], gate_tok[:, tok, 8 * half:8 * half + 8], ident[:, :])
            done(ins)
            for n, name in enumerate(("mv1", "mo_0", "mo_1", "mz0", "mz1")):
                token_major(name, B_VOZ + 16 * (n + 1), 16, XH, XL)
            pe.wait_ge(freed_sem["act"], FREED["mz1"][1])
            pe.wait_ge(ev("exp_m"), 1)
            for n, src in enumerate((gi, gF)):
                for tok in range(TOK):
                    o = 6 * HALF + 16 * n + 8 * tok
                    ins = nc.tensor.transpose(ps[:, o:o + 8], src[:, tok * P:(tok + 1) * P], ident[0:8, 0:8])
            ins.then_inc(M2["prep"], 1)
            pe.wait_ge(ev("select"), 16)
            pe.wait_ge(ev("qk"), 16)
            for i in range(ML_H + 1):
                if i < ML_H:
                    h = i
                    if h >= 2:
                        pe.wait_ge(M2["arg"], h - 1)
                    b = (2 + h % 2) * HALF
                    mm(ps[:, b:b + SEQ], select[:, h, :], ge[:, :], start=True, stop=True,
                       skip_group_check=True).then_inc(M2["bc"], 1)
                    if h >= 2:
                        pe.wait_ge(M2["w"], h - 1)
                    b = (h % 2) * HALF
                    kk, qq = qkT[:, h, 1, :], qkT[:, h, 0, :]
                    mm(ps[:, b:b + SEQ], kk[:, 0:P], qq, start=True, stop=True, skip_group_check=True)
                    mm(ps[:, b + SEQ:b + SEQ + P], kk[:, P:SEQ], qq[:, P:SEQ], start=True, stop=True,
                       skip_group_check=True).then_inc(M2["st"], 1)
                if i >= 1:
                    h = i - 1
                    pe.wait_ge(M2["w"], h + 1)
                    d = decay[:, h % 2, :]
                    for tok in range(TOK):
                        u = 2 * h + tok
                        if u >= 4:
                            pe.wait_ge(M2["h"], u - 3)
                        elif u >= 2:
                            pe.wait_ge(M2["prepc"], 1)
                        b = (4 + u % 4) * HALF
                        parts = [(d[:, 0:P], 0)] if tok == 0 else [(d[:, P:SEQ], 0), (d[:, SEQ:SEQ + P], 1)]
                        for n, (w, s) in enumerate(parts):
                            ins = mm(ps[:, b:b + ML_V + 1], w, mv[:, s, h, :], start=(n == 0),
                                     stop=(n == len(parts) - 1), skip_group_check=True)
                        ins.then_inc(M2["pv"], 1)
            for h in range(ML_H):
                pe.wait_ge(M2["y"], 2 * h + 2)
                for half in range(2):
                    for tok in range(TOK):
                        o = h * HALF + half * SEQ + tok * P
                        c0 = h * ML_V + half * P
                        ins = nc.tensor.transpose(ps[:, o:o + P], oz[:, tok, c0:c0 + P], ident[:, :])
                ins.then_inc(M2["yT"], 1)
            pe.wait_ge(M2["lo"], 8)
            token_major("lo0", B_LO, 16, XH, XL, lambda k: (M2["lo"], k + 1))
            token_major("lo1", B_LO + 16, 16, XH, XL)

            def ada_columns(name, units):
                g = start(name)
                pe.wait_ge(ada_used, 16 * units)
                for vec in range(2):
                    for k in range(KD):
                        o = g + 16 * vec + k
                        ins = mm(ps[:, o:o + 1], acc_s[:, vec, k * P:(k + 1) * P], ones[:, 0:1], start=True, stop=True,
                                 skip_group_check=True)
                done(ins)

            def ada_row(name, units):
                g = start(name)
                pe.wait_ge(ada_used, 16 * units)
                for n in range(4):
                    ins = mm(ps[:, g + n * HALF:g + (n + 1) * HALF], ones[:, :], acc_g[:, n * HALF:(n + 1) * HALF],
                             start=True, stop=True, skip_group_check=True)
                done(ins)

            ada_columns("ada1", 8)
            ada_row("g1", 12)
            pe.wait_ge(ev("h_normed"), 2)
            transposes("hTa", operand_tiles(h_norm, 0))
            transposes("hTb", operand_tiles(h_norm, 8))
            token_major("qa", B_QA, 16, XH, XL, lambda k: (tile_split, SPLIT_BASE["hTa"] + k + 1))
            token_major("kva", B_KVA, 8, XH, XL, per_block=2)
            feature_major("qb", B_QB, 16, XH, XL)
            feature_major("kb", B_KB, 16, XH, XL)
            token_major("vb", B_VB, 16, XH, XL)
            pe.wait_ge(ev("qk_roped"), 4)
            transposes("qaT", [(h * SEQ + tok * P, qa_tok[:, tok, h, :]) for h in range(N_A) for tok in range(TOK)])
            transposes("kaT", [(h * SEQ + tok * P, kva_tok[:, tok, h, :]) for h in range(N_KV) for tok in range(TOK)])
            pe.wait_ge(ev("toep"), 16)
            pe.wait_ge(ev("rel"), 32)
            for name, kc0, kc1 in (("biasa", 0, 40), ("biasb", 40, GRID_W)):
                g = start(name)
                for kc in range(kc0, kc1):
                    o = g + (kc - kc0) // 10 * HALF + (kc - kc0) % 10 * N_A * REL_R
                    c0 = GRID_W - 1 - kc
                    ins = mm(ps[:, o:o + N_A * REL_R], toep[:, c0:c0 + P],
                             rel[:, :, :].rearrange(flat), start=True, stop=True, skip_group_check=True)
                done(ins)
            pe.wait_ge(freed_sem["dve"], FREED["biasb"][1])
            pe.wait_ge(freed_sem["act"], FREED["kaT"][1])

            def blk_operands(u):
                h, blk = (u % 16) // 2, u % 2
                t = slice(blk * P, (blk + 1) * P)
                if u < 16:
                    return [(qaT[:, h, t], kaT[:, h // (N_A // N_KV), :])]
                return [(qbT[:, h, t], kbT[:, h, :])]

            def blk_values(u, t):
                h = (u % 16) // 2
                return kva_tok[:, t, N_KV + h // (N_A // N_KV), :] if u < 16 else vb_tok[:, t, h * HD:(h + 1) * HD]

            attention(A3, 32, prob2, probT2, y_tok2, lambda u: SEQ, blk_operands, blk_values)
            pe.wait_ge(A3["lo"], 16)
            for q in range(2):
                n0 = B_MERGE + 48 * q
                token_major(f"ga{q}", n0, 16, XH, XL)
                token_major(f"oa{q}", n0 + 16, 8, yaH, yaL)
                token_major(f"gb{q}", n0 + 24, 16, XH, XL)
                token_major(f"ob{q}", n0 + 40, 8, ybH, ybL)
            pe.wait_ge(freed_sem["dve"], FREED["ob1"][1])
            transposes("mTa", operand_tiles(merged, 0))
            transposes("mTb", operand_tiles(merged, 8))
            token_major("wo0", B_WO, 16, XH, XL, lambda k: (tile_split, SPLIT_BASE["mTa"] + k // 2 + 1))
            token_major("wo1", B_WO + 16, 16, XH, XL)
            ada_columns("ada2", 20)
            pe.wait_ge(ev("h_normed"), 4)
            transposes("h2Ta", operand_tiles(h_norm, 0))
            transposes("h2Tb", operand_tiles(h_norm, 8))

            def ffn_pass(p, parity, need=None):
                g = ((TURN["ffn0"] + parity) % 2) * 4 * HALF
                if need is None:
                    pe.wait_ge(product_done, p - 1)
                else:
                    pe.wait_ge(*need)

                def four(kg, static):
                    for j in range(RING):
                        pe.wait_ge(lo_ready, 16 * p + (RING * kg + (B_FFN + j + 1)))
                        if static:
                            feature_block(g, j, j, lambda k: XH[:, k, :], lambda k: XL[:, k, :], j == 0, False)
                        else:
                            feature_block(g, RING * kg + j, j, lambda k: XH[:, bass.ds(k, 1), :].rearrange(flat),
                                          lambda k: XL[:, bass.ds(k, 1), :].rearrange(flat), False, True)
                four(0, True)
                with pe.Fori(1, KD // RING) as kg:
                    four(kg, False)

            base = SPLIT_BASE["h2Ta"]
            ffn_pass(0, 0, (tile_split, base + KD))
            ffn_pass(1, 1, (tile_split, base + KD))
            ffn_pass(2, 0)
            with pe.Fori(1, (FFN_PASSES - 1) // 2) as i:
                for s in range(2):
                    ffn_pass(2 * i + (1 + s), 1 - s)
            ada_row("g2", 24)
            token_major("down0", B_DOWN, KF, FH, FL, lambda k: (ev("ffn_lo"), k // 4 + 1))
            token_major("down1", B_DOWN + KF, KF, FH, FL)


def shape_constants():
    c = np.zeros((P, N_CONST), np.float32)

    def put(name, value, rows=P):
        o, n = CONST[name]
        c[:rows, o:o + n] = np.asarray(value, np.float32).reshape(rows, n)

    put("ident", np.eye(P))
    put("inv_freq", np.tile(10000.0 ** (-np.arange(0, ROPE, 2) / ROPE), (P, 1)))
    p, t = np.arange(P)[:, None], np.arange(SEQ)[None]
    put("causal", np.where(p <= t, 0.0, NEG))
    qc, kc = (np.arange(P) % GRID_W)[:, None], np.arange(GRID_W)[None]
    start = np.clip(qc - NA_COLS // 2, 0, GRID_W - NA_COLS)
    put("window", np.where((kc >= start) & (kc < start + NA_COLS), 0.0, NEG))
    toep = np.zeros((64, 191))
    for half in range(2):
        for j in range(REL_C):
            toep[32 * half + j, GRID_W * half + 78 - j] = 1.0
    put("toeplitz", toep, 64)
    inv = (np.float32(10000.0) ** (-np.arange(0, HD // 2, 2, dtype=np.float32) / (HD // 2))).astype(np.float32)
    tok = np.arange(SEQ)
    ang = np.concatenate([(tok // GRID_W).astype(np.float32)[:, None] * inv,
                          (tok % GRID_W).astype(np.float32)[:, None] * inv], axis=1).astype(np.float64)
    for name, f in (("cos", np.cos), ("sin", np.sin)):
        put(name, f(ang).reshape(TOK, P, HD // 2).transpose(1, 0, 2))
    put("select", np.repeat(np.eye(8), P, axis=1), 8)
    return c


_OUTS = [((1, SEQ, D), "float32")]


def kernel(**inputs):
    import concourse.bacc as _bacc
    from concourse.bass_utils import run_bass_kernel_spmd as _run

    i = {n: np.asarray(a) for n, a in inputs.items()}

    def cols(a):
        return a.reshape(-1, P).T

    pack = {"q_norm": cols(i["mla_q_norm"][0]), "kv_norm": cols(i["mla_kv_norm"][0]), "ln_w0": cols(i["ln_w"][0]),
            "ln_b0": cols(i["ln_b"][0]), "head_norm": cols(i["ml_head_norm"][0]), "conv_w": cols(i["ml_conv_w"][0]),
            "conv_b": cols(i["ml_conv_b"][0]), "norm1": cols(i["norm1_w_2"][0]), "norm2": cols(i["norm2_w_2"][0]),
            "c": cols(i["c_2"][0])}
    args = {
        "positions": i["positions"].reshape(TOK, P).T, "x": i["x"], "xT": i["x"][0].T,
        "pack": np.concatenate([pack[n] for n in PACK], axis=1), "const": shape_constants(),
        "gate_b": i["ml_gate_b"].reshape(2, ML_H).T,
        "qk_norm": np.concatenate([i["q_norm_w_2"], i["k_norm_w_2"]], axis=0),
        "rpbT": i["nat_rpb_2"][0].transpose(2, 0, 1),
        "mla_w_in": i["mla_w_in"], "mla_w_qb": i["mla_w_qb"], "mla_w_kvb": i["mla_w_kvb"], "mla_w_out": i["mla_w_out"],
        "ml_w_in": i["ml_w_in"], "ml_w_out": i["ml_w_out"], "ln_w": i["ln_w"], "ln_b": i["ln_b"],
        "w_ada": i["w_ada_2"], "b_ada": i["b_ada_2"], "w_in": i["w_in_2"], "w_oa": i["w_oa_2"], "w_ob": i["w_ob_2"],
        "w_out": i["w_out_2"], "w_gate": i["w_ffn_gate_2"], "w_up": i["w_ffn_up_2"], "w_down": i["w_ffn_down_2"],
        "final_w": i["final_w_2"].reshape(1, D),
    }
    nc = _bacc.Bacc("TRN2", target_bir_lowering=False, num_devices=1)
    arrays, aps = {}, []
    for name, a in args.items():
        a = np.ascontiguousarray(a)
        arrays[f"in_{name}_dram"] = a
        aps.append(nc.dram_tensor(f"in_{name}_dram", a.shape, mybir.dt.from_np(a.dtype), kind="ExternalInput").ap())
    for n, (shape, dtype) in enumerate(_OUTS):
        aps.append(nc.dram_tensor(f"out_{n}_dram", shape, mybir.dt.from_np(np.dtype(dtype)),
                                  kind="ExternalOutput").ap())
    two_block_kernel(nc, *aps)
    r = _run(nc, [arrays], core_ids=[0])
    return r.results[0]["out_0_dram"]
```

```python
from contextlib import ExitStack

import concourse.bass as bass
from concourse import mybir
import numpy as np

ALU = mybir.AluOpType
ACT = mybir.ActivationFunctionType
AX_X = mybir.AxisListType.X
F32 = mybir.dt.float32
F32R = mybir.dt.float32r
I32 = mybir.dt.int32

P = 128
SEQ = 256
TOK = SEQ // P
D = 2048
KD = D // P
COLS = 1024
HALF = 512
RING = 4
EPS = 1e-6
NEG = -3.0e38

MLA_H, NOPE, ROPE, LORA = 16, 128, 64, 512
MLA_SCALE = float(NOPE + ROPE) ** -0.5
ALPHA = 4.0 ** 0.25
ML_H, ML_QK, ML_V = 8, 128, 256
ML_SCALE = float(ML_QK) ** -0.5
TAPS = 4
N_A, N_KV, HD = 8, 2, 128
GRID_W, NA_COLS, REL_R, REL_C = 64, 16, 6, 31
HD_SCALE = float(HD) ** -0.5
D_FF = 5632
KF = D_FF // P
FFN_PASSES = D_FF // HALF

PACK = {}
for _name, _n in (("q_norm", 4), ("kv_norm", 4), ("ln_w0", 16), ("ln_b0", 16), ("head_norm", 16), ("conv_w", 64),
                  ("conv_b", 16), ("norm1", 16), ("norm2", 16), ("c", 16)):
    PACK[_name] = (sum(n for _, n in PACK.values()), _n)
N_PACK = sum(n for _, n in PACK.values())
CONST = {}
for _name, _n in (("ident", 128), ("inv_freq", 32), ("causal", 256), ("window", 64), ("toeplitz", 191),
                  ("cos", 128), ("sin", 128), ("select", 1024)):
    CONST[_name] = (sum(n for _, n in CONST.values()), _n)
N_CONST = sum(n for _, n in CONST.values())

B_C = 0
B_Z = B_C + 16
B_QN = B_Z + 32
B_QR = B_QN + 8
B_KN = B_QR + 4
B_V = B_KN + 8
B_MO = B_V + 8
B_CONV = B_MO + 32
B_VOZ = B_CONV + 32
B_LO = B_VOZ + 96
B_QA = B_LO + 32
B_KVA = B_QA + 16
B_QB = B_KVA + 8
B_KB = B_QB + 16
B_VB = B_KB + 16
B_MERGE = B_VB + 16
B_WO = B_MERGE + 96
B_FFN = B_WO + 32
B_DOWN = B_FFN + 16 * FFN_PASSES
N_BLOCKS = B_DOWN + 2 * KF

TURN_PLAN = (
    "c:dve z0:act kr:act krt@0:act z1@1:act cT:split8 qn0:act qn1:act qr:act kn0:dve kn1:dve v0:act v1:act qrT:act krT:act "
    "mo0:dve mo1:dve x1Ta:split4 x1Tb:split4 mlq:taps8 mlk:taps8 mv0:act gates:dve mv1:act mo_0:act mo_1:act "
    "mz0:act mz1:act lo0@0:dve lo1:dve biasa:act biasb:act ada1:dve g1:act hTa:split4 hTb:split4 qa:act kva:act qb:act kb:act vb:act "
    "qaT:act kaT:act ga0:act ga1:act gb0:act gb1:act oa0:dve ob0:dve oa1:dve ob1:dve "
    "mTa:split4 wo0:dve mTb:split4 wo1@1:dve ada2:dve h2Ta:split4 h2Tb:split4").split() \
    + [f"ffn{i}:product1" for i in range(FFN_PASSES)] + ["g2:act", "down0:dve", "down1:dve"]
GROUP = {}
LAST_IN_GROUP = {}
FREED = {}
SPLIT_BASE = {}
_total = {"act": 0, "dve": 0, "split": 0, "taps": 0, "product": 0}
_group, _last = 1, {0: None, 1: None}
for _entry in TURN_PLAN:
    _name, _who = _entry.split(":")
    _name, _, _at = _name.partition("@")
    _group = int(_at) if _at else 1 - _group
    GROUP[_name], LAST_IN_GROUP[_name] = _group, _last[_group]
    _last[_group] = _name
    _kind = _who.rstrip("0123456789")
    SPLIT_BASE[_name] = _total[_kind]
    _total[_kind] += int(_who[len(_kind):] or 1)
    FREED[_name] = (_kind, _total[_kind])

LAST_BLOCK = {"c": B_Z, "z0": B_Z + 16, "z1": B_QN, "qn0": B_QN + 4, "qn1": B_QR, "qr": B_KN, "kn0": B_KN + 4,
              "kn1": B_V, "v0": B_V + 4, "v1": B_MO, "mo0": B_MO + 16, "mo1": B_CONV, "mlq": B_CONV + 16,
              "mlk": B_VOZ, "lo0": B_LO + 16, "lo1": B_QA, "qa": B_KVA, "kva": B_QB, "qb": B_KB, "kb": B_VB,
              "vb": B_MERGE, "wo0": B_WO + 16, "wo1": B_FFN, "down0": B_DOWN + KF, "down1": B_DOWN + 2 * KF}
for _n, _name in enumerate(("mv0", "mv1", "mo_0", "mo_1", "mz0", "mz1")):
    LAST_BLOCK[_name] = B_VOZ + 16 * (_n + 1)
for _name, _end in (("ga0", 16), ("ga1", 32), ("gb0", 48), ("gb1", 64), ("oa0", 72), ("ob0", 80), ("oa1", 88),
                    ("ob1", 96)):
    LAST_BLOCK[_name] = B_MERGE + _end
for _p in range(FFN_PASSES):
    LAST_BLOCK[f"ffn{_p}"] = B_FFN + 16 * (_p + 1)
BANKS_BEFORE = {_name: 4 * _n for _n, _name in enumerate(("cT", "x1Ta", "x1Tb", "hTa", "hTb", "mTa", "mTb", "h2Ta",
                                                          "h2Tb"))}
TURN_COUNT = {}
for _name in GROUP:
    if _name not in LAST_BLOCK and _name not in BANKS_BEFORE:
        TURN_COUNT[_name] = len(TURN_COUNT) + 1

ADA_BESIDE = {"z0": 16, "z1": 16, "mo0": 16, "mo1": 16, "mlq": 12, "mlk": 12, "mv0": 20, "mv1": 16, "mo_0": 20,
              "mo_1": 20, "mz0": 14, "mz1": 14,
              "qa": 16, "kb": 8, "vb": 16, "ga0": 22, "ga1": 22, "gb0": 22, "gb1": 22, "oa0": 6, "ob0": 6, "oa1": 6,
              "ob1": 6, "wo0": 20, "wo1": 20}
ADA_FIRST = {}
for _name, _n in ADA_BESIDE.items():
    ADA_FIRST[_name] = sum(ADA_BESIDE[_m] for _m in ADA_FIRST)
N_UNITS = sum(ADA_BESIDE.values()) // KD


def two_block_kernel(nc, positions, x, xT, pack, const, gate_b, qk_norm, rpbT, mla_w_in, mla_w_qb, mla_w_kvb,
                     mla_w_out, ml_w_in, ml_w_out, ln_w, ln_b, w_ada, b_ada, w_in, w_oa, w_ob, w_out, w_gate, w_up,
                     w_down, final_w, out):
    K = 1024
    BASE = 16512
    with ExitStack() as ctx:
        def at(name, kb, shape, dt=F32):
            return nc.alloc_sbuf_tensor_at(name, shape, dt, offset=BASE + int(kb * K))

        def sem(name):
            return ctx.enter_context(nc.semaphore(name))

        raw = at("raw", 0, [P, RING, COLS])
        hi = at("hi", 16, [P, RING, COLS], F32R)
        lo = at("lo", 32, [P, RING, COLS], F32R)
        XH = at("XH", 48, [P, KD, SEQ], F32R)
        XL = at("XL", 64, [P, KD, SEQ], F32R)
        X = at("X", 80, [P, TOK, D])
        ada_raw = at("ada_raw", 96, [P, RING, HALF])
        acc_g = at("acc_g", 104, [P, D])
        acc_s = at("acc_s", 112, [P, 2, D])
        qT = at("qT", 48, [P, MLA_H, SEQ])
        kT = at("kT", 64, [P, MLA_H, SEQ])
        small_raw = at("small_raw", 128, [P, KD, ROPE])
        small_hi = at("small_hi", 132, [P, KD, ROPE], F32R)
        small_lo = at("small_lo", 136, [P, KD, ROPE], F32R)
        row_w = at("row_w", 128, [P, D])
        row_b = at("row_b", 136, [P, D])
        c_tok = at("c_tok", 144, [P, TOK, 2 * LORA])
        z_tok = at("z_tok", 152, [P, TOK, D])
        xT_raw = at("xT_raw", 168, [P, KD, SEQ])
        v_tok = at("v_tok", 168, [P, TOK, MLA_H * NOPE])
        CH = at("CH", 184, [P, 8, SEQ], F32R)
        CL = at("CL", 192, [P, 8, SEQ], F32R)
        qr_tok = at("qr_tok", 144, [P, TOK, MLA_H, ROPE])
        qrr_tok = at("qrr_tok", 136, [P, TOK, MLA_H, ROPE])
        qrT = at("qrT", 184, [P, MLA_H // 2, SEQ])
        rope_tmp = at("rope_tmp", 128, [P, 2, HALF])
        prob = at("prob", 192.5, [P, 3, SEQ])
        probT = at("probT", 195.5, [P, 2, SEQ])
        y_tok = at("y_tok", 197.5, [P, 4, P])
        nmax = at("nmax", 199.5, [P, 32])
        rsum = at("rsum", 199.625, [P, 32])
        rinv = at("rinv", 199.75, [P, 32])
        qkT = at("qkT", 144, [P, ML_H, 2, SEQ])
        h_tok = at("h_tok", 144, [P, ML_H, TOK, ML_V])
        mv = at("mv", 160, [P, TOK, ML_H, ML_V + 1])
        conv_tmp = at("conv_tmp", 177, [P, 8, SEQ])
        oz = at("oz", 176.5, [P, TOK, D])
        z_tmp = at("z_tmp", 136, [P, TOK, COLS])
        decay = at("decay", 192.5, [P, 2, 384])
        select = at("select", 195.5, [8, ML_H, P])
        h_norm = at("h_norm", 160, [P, TOK, D])
        qa_tok = at("qa_tok", 128, [P, TOK, N_A, HD])
        yaL = at("yaL", 128, [P, N_A, SEQ], F32R)
        g_row = at("g_row", 136, [P, D])
        qaT = at("qaT", 144, [P, N_A, SEQ])
        yaH = at("yaH", 144, [P, N_A, SEQ], F32R)
        qbT = at("qbT", 152, [P, N_A, SEQ])
        ybH = at("ybH", 152, [P, N_A, SEQ], F32R)
        kbT = at("kbT", 160, [P, N_A, SEQ])
        ybL = at("ybL", 160, [P, N_A, SEQ], F32R)
        vb_tok = at("vb_tok", 168, [P, TOK, N_A * HD])
        sig_a = at("sig_a", 168, [P, TOK, D])
        sig_b = at("sig_b", 184, [P, TOK, D])
        kva_tok = at("kva_tok", 176, [P, TOK, 4, HD])
        kaT = at("kaT", 180, [P, N_KV, SEQ])
        na_bias = at("na_bias", 182, [P, GRID_W, N_A, REL_R])
        prob2 = at("prob2", 194, [P, 3, SEQ])
        probT2 = at("probT2", 197, [P, 2, SEQ])
        y_tok2 = at("y_tok2", 199, [P, 4, P])
        merged = sig_a
        FH = at("FH", 112, [P, KF, SEQ], F32R)
        FL = at("FL", 156, [P, KF, SEQ], F32R)
        xsq = at("xsq", 64, [P, 2 * TOK, COLS])
        g2_row = at("g2_row", 48, [P, D])
        final_row = at("final_row", 56, [P, D])
        tmp = at("tmp", 200, [P, COLS])
        ident = at("ident", 204, [P, P])
        ones = at("ones", 204.5, [P, P])
        pk = at("pk", 205, [P, N_PACK])
        c_act = at("c_act", 206, [P, 16])
        mods = at("mods", 206.0625, [P, 2, 16])
        A_col = at("A_col", 206.1875, [P, 16])
        st = at("st", 206.25, [P, TOK, 4, 6])
        mvar = at("mvar", 206.4375, [P, TOK, 2])
        ss = at("ss", 206.46875, [P, 32])
        ra = at("ra", 206.59375, [P, 32])
        ry = at("ry", 206.71875, [P, 32])
        rt = at("rt", 206.84375, [P, 32])
        shift_col = at("shift_col", 207.34375, [P, 1])
        nmax2 = at("nmax2", 206.96875, [P, 32])
        rsum2 = at("rsum2", 207.09375, [P, 32])
        rinv2 = at("rinv2", 207.21875, [P, 32])
        kr_tok = at("kr_tok", 104, [P, TOK, ROPE])
        krf = at("krf", 106.5, [ROPE, SEQ])
        krr_tok = at("krr_tok", 104.5, [P, TOK, 2, ROPE])
        krT = at("krT", 105.5, [P, SEQ])
        ang = at("ang", 107.5, [P, TOK, 32])
        rot = at("rot", 107.75, [P, TOK, 32])
        turns_n = at("turns_n", 108, [P, TOK, 32])
        cos_t = at("cos_t", 108.25, [P, TOK, 32])
        sin_t = at("sin_t", 108.5, [P, TOK, 32])
        pos_i = at("pos_i", 108.75, [P, TOK], I32)
        pos_f = at("pos_f", 108.78125, [P, TOK])
        inv_freq = at("inv_freq", 108.8125, [P, 32])
        gate_bias = at("gate_bias", 128.25, [64, 1])
        gi = at("gi", 129, [8, SEQ])
        gf = at("gf", 130, [8, SEQ])
        ge = at("ge", 131, [8, SEQ])
        gF = at("gF", 132, [8, SEQ])
        gM = at("gM", 133, [8, SEQ])
        causal = at("causal", 134, [P, SEQ])
        G_col = at("G_col", 135, [P, TOK, ML_H])
        E_col = at("E_col", 135.0625, [P, TOK, ML_H])
        dens = at("dens", 135.125, [P, 16])
        dinv = at("dinv", 135.1875, [P, 16])
        cos2 = at("cos2", 144, [P, TOK, HD // 2])
        sin2 = at("sin2", 144.5, [P, TOK, HD // 2])
        qkn = at("qkn", 145, [P, 2, HD])
        window = at("window", 195.25, [P, GRID_W])
        toep = at("toep", 194, [P, 191])
        toep_r = at("toep_r", 195.5, [P, 191], F32R)
        rel = at("rel", 195, [P, N_A, REL_R])
        rel_parts = at("rel_parts", 196.5, [P, N_A, REL_R], F32R)
        rope2 = at("rope2", 146, [P, 2, HALF])

        ps = ctx.enter_context(nc.psum_tensor("ps", [P, 8 * HALF], F32))

        w_landed = [sem(f"w_landed{i}") for i in range(RING)]
        hi_ready, lo_ready = sem("hi_ready"), sem("lo_ready")
        block_done = sem("block_done")
        tiles_turned = sem("tiles_turned")
        turn_done = sem("turn_done")
        tile_split = sem("tile_split")
        taps_done = sem("taps_done")
        product_done = sem("product_done")
        freed_sem = {"act": sem("act_freed"), "dve": sem("dve_freed"), "split": tile_split, "taps": taps_done,
                     "product": product_done}
        ada_landed = [sem(f"ada_landed{i}") for i in range(RING)]
        ada_used = sem("ada_used")
        acc_zero = sem("acc_zero")
        bias_landed = [sem(f"bias_landed{i}") for i in range(4)]
        s_dve, s_act = sem("s_dve"), sem("s_act")
        events = {}

        def ev(name):
            if name not in events:
                events[name] = sem("e_" + name)
            return events[name]

        def att_sems(tag):
            return {n: sem(f"{tag}_{n}") for n in ("scored", "maxed", "exped", "turned", "copied", "summed", "scaled",
                                                   "backed", "hi", "lo")}

        A1, A3 = att_sems("mla"), att_sems("blk")
        M2 = {n: sem(f"ml_{n}") for n in ("prep", "prepc", "st", "bc", "arg", "exp", "w", "pv", "h", "sq", "y", "yT",
                                          "hi", "lo")}

        def col(name, k):
            o = PACK[name][0] + k
            return pk[:, o:o + 1]

        def complete(name):
            if name in BANKS_BEFORE:
                return tiles_turned, BANKS_BEFORE[name] + 4
            return (block_done, LAST_BLOCK[name]) if name in LAST_BLOCK else (turn_done, TURN_COUNT[name])

        def grp(name):
            return GROUP[name] * 4 * HALF

        def T(name, tok, w=COLS):
            g = grp(name) + tok * 2 * HALF
            return ps[:, g:g + w]

        def landed(n, j):
            two = max(0, min(n + 1, B_DOWN) - B_FFN)
            two = (two + RING - 1 - j) // RING if two > 0 else 0
            return 16 * (n // RING + 1 + two)

        def acc_part(u):
            vec, part = u // 4, (u % 4) * HALF
            if vec in (2, 5):
                return acc_g[:, part:part + HALF], 1 if vec == 2 else 3
            return acc_s[:, vec % 3, part:part + HALF], 0 if vec < 2 else 2

        flat = "p a b -> p (a b)"
        block = ctx.enter_context(nc.Block())

        @block.sync
        def _(sp):
            def rows(w, k):
                return w[bass.ds(k * P, P), :] if not isinstance(k, int) else w[k * P:(k + 1) * P, :]

            def stream(n0, nb, source):
                first = 0
                if n0 == 0:
                    for j in range(RING):
                        dst, src = source(j, j)
                        sp.dma_start(dst, src).then_inc(w_landed[j], 16)
                    first = 1
                with sp.Fori(first, nb // RING) as g:
                    for j in range(RING):
                        dst, src = source(RING * g + j, j)
                        sp.wait_ge(lo_ready, n0 + RING * g + j - RING + 1)
                        sp.dma_start(dst, src).then_inc(w_landed[j], 16)

            def plain(w, c0):
                return lambda k, j: (raw[:, j, :], rows(w, k)[:, c0:c0 + COLS])

            def head_cols(w, per, h0, nh, off, width):
                def source(k, j):
                    src = rows(w, k).rearrange("p (h e) -> p h e", e=per)[:, h0:h0 + nh, off:off + width]
                    return raw[:, j, :].rearrange("p (h e) -> p h e", e=width), src
                return source

            xT_v = xT.rearrange("(k p) t -> p k t", p=P)
            for q in range(2):
                sp.dma_start(xT_raw[:, 8 * q:8 * q + 8, :], xT_v[:, 8 * q:8 * q + 8, :]).then_inc(ev(f"xT{q}"), 16)
            w = mla_w_in[0]
            stream(B_C, 16, plain(w, 0))
            for q in range(2):
                stream(B_Z + 16 * q, 16, plain(w, 2 * LORA + ROPE + q * COLS))
            for q in range(2):
                stream(B_QN + 4 * q, 4, head_cols(mla_w_qb[0], NOPE + ROPE, 8 * q, 8, 0, NOPE))
            stream(B_QR, 4, head_cols(mla_w_qb[0], NOPE + ROPE, 0, 16, NOPE, ROPE))
            for q in range(2):
                stream(B_KN + 4 * q, 4, head_cols(mla_w_kvb[0], 2 * NOPE, 8 * q, 8, 0, NOPE))
            for q in range(2):
                stream(B_V + 4 * q, 4, head_cols(mla_w_kvb[0], 2 * NOPE, 8 * q, 8, NOPE, NOPE))
            for q in range(2):
                stream(B_MO + 16 * q, 16, plain(mla_w_out[0], q * COLS))
            for q in range(6):
                stream(B_CONV + 16 * q, 16, plain(ml_w_in[0], q * COLS))
            for q in range(2):
                stream(B_VOZ + 64 + 16 * q, 16, plain(ml_w_in[0], 6160 + q * COLS))
            for q in range(2):
                stream(B_LO + 16 * q, 16, plain(ml_w_out[0], q * COLS))
            w = w_in[0]
            stream(B_QA, 16, plain(w, 0))
            pairs = w.rearrange("(b a p) n -> b p a n", a=2, p=P)

            def two_rows(k, j):
                src = pairs[k] if isinstance(k, int) else pairs[bass.ds(k, 1), :, :, :].rearrange("b p a n -> (b p) a n")
                return raw[:, j, :].rearrange("p (a n) -> p a n", a=2), src[:, :, COLS:COLS + HALF]

            stream(B_KVA, 8, two_rows)
            for q in range(3):
                stream(B_QB + 16 * q, 16, plain(w, 1536 + q * COLS))
            for n, c0 in enumerate((4608, 4608 + COLS, 6656, 6656 + COLS)):
                stream(B_MERGE + 16 * n, 16, plain(w, c0))
            for q in range(2):
                stream(B_MERGE + 64 + 16 * q, 8, plain(w_oa[0], q * COLS))
                stream(B_MERGE + 72 + 16 * q, 8, plain(w_ob[0], q * COLS))
            for q in range(2):
                stream(B_WO + 16 * q, 16, plain(w_out[0], q * COLS))
            with sp.Fori(0, FFN_PASSES) as q:
                with sp.Fori(0, KD // RING) as g:
                    for j in range(RING):
                        for part, mat in enumerate((w_gate[0], w_up[0])):
                            sp.wait_ge(lo_ready, 16 * q + (RING * g + (B_FFN + j - RING + 1)))
                            sp.dma_start(raw[:, j, part * HALF:(part + 1) * HALF],
                                         mat[bass.ds((RING * g + j) * P, P), bass.ds(q * HALF, HALF)]) \
                              .then_inc(w_landed[j], 16)
            for q in range(2):
                stream(B_DOWN + KF * q, KF, plain(w_down[0], q * COLS))
            for tok in range(TOK):
                for q in range(2):
                    sp.wait_ge(ev(f"result{q}"), tok + 1)
                    sp.dma_start(out[0, tok * P:(tok + 1) * P, q * COLS:(q + 1) * COLS],
                                 X[:, tok, q * COLS:(q + 1) * COLS]).then_inc(ev("stored"), 16)
            sp.wait_ge(ev("stored"), 64)

        @block.gpsimd
        def _(pool):
            def load(name, dst, src):
                pool.dma_start(dst, src).then_inc(ev(name), 16)

            def cst(name, p0=0, p1=P):
                o, n = CONST[name]
                return const[p0:p1, o:o + n]

            def bcast(dst, row):
                return dst, row.partition_broadcast(P)

            def ada_units(u0, u1):
                def four(u, g, wait):
                    for j in range(RING):
                        if wait:
                            pool.wait_ge(ada_used, 16 * u + (RING * g + (j - RING + 1)))
                        pool.dma_start(ada_raw[:, j, :],
                                       w_ada[0][bass.ds((RING * g + j) * P, P), bass.ds(u * HALF, HALF)]) \
                            .then_inc(ada_landed[j], 16)
                if u0 == 0:
                    four(0, 0, False)
                    with pool.Fori(1, KD // RING) as g:
                        four(0, g, True)
                    u0 = 1
                with pool.Fori(u0, u1) as u:
                    with pool.Fori(0, KD // RING) as g:
                        four(u, g, True)

            def init_acc(i, acc, b0, n, zeroed):
                nc.gpsimd.memset(acc, 0.0).then_inc(acc_zero, 1)
                pool.wait_ge(acc_zero, zeroed)
                pool.dma_start(acc[0:1, :], b_ada[0:1, b0:b0 + n]).then_inc(bias_landed[i], 16)

            load("pack", pk[:, :], pack)
            load("ident", ident[:, :], cst("ident"))
            load("pos", pos_i[:, :], positions)
            load("inv_freq", inv_freq[:, :], cst("inv_freq"))
            load("small1", small_raw[:, :, :], mla_w_in[0][:, 2 * LORA:2 * LORA + ROPE].rearrange("(k p) n -> p k n", p=P))
            load("x", X[:, :, :], x[0].rearrange("(a p) n -> p a n", p=P))
            init_acc(0, acc_s[:, :, :].rearrange(flat), 0, 2 * D, 1)
            ada_units(0, 4)
            pool.wait_ge(ev("q_roped"), 2)
            pool.wait_ge(*complete("qrT"))
            load("rows0", *bcast(row_w[:, :], ln_w[0:1, :]))
            load("rows0", *bcast(row_b[:, :], ln_b[0:1, :]))
            ada_units(4, 5)
            pool.wait_ge(ev("x1_rows"), 4)
            nc.gpsimd.memset(small_raw[:, :, 0:40], 0.0).then_inc(ev("small_zero"), 1)
            pool.wait_ge(ev("small_zero"), 1)
            for half in range(2):
                load("small2", small_raw[:, :, 32 * half:32 * half + 8],
                     ml_w_in[0][:, 6144 + 8 * half:6152 + 8 * half].rearrange("(k p) n -> p k n", p=P))
            init_acc(1, acc_g[:, :], 2 * D, D, 2)
            ada_units(5, 7)
            pool.wait_ge(*complete("gates"))
            for half in range(2):
                load("gate_bias", gate_bias[32 * half:32 * half + 8, :], gate_b[8 * half:8 * half + 8, :])
            load("causal", causal[:, :], cst("causal"))
            load("select", select[:, :, :].rearrange(flat), cst("select", 0, 8))
            ada_units(7, 12)
            pool.wait_ge(M2["lo"], 16)
            load("rows1", *bcast(row_w[:, :], ln_w[1:2, :]))
            load("rows1", *bcast(row_b[:, :], ln_b[1:2, :]))
            load("tables2", cos2[:, :, :].rearrange(flat), cst("cos"))
            load("tables2", sin2[:, :, :].rearrange(flat), cst("sin"))
            load("tables2", qkn[:, 0, :], qk_norm[0:1, :].partition_broadcast(P))
            load("tables2", qkn[:, 1, :], qk_norm[1:2, :].partition_broadcast(P))
            load("toep", toep[:, :], cst("toeplitz"))
            load("window", window[:, :], cst("window"))
            nc.gpsimd.memset(rel[:, :, :], 0.0).then_inc(ev("rel_zero"), 1)
            pool.wait_ge(ev("rel_zero"), 1)
            for part in range(2):
                load("rel", rel[64 * part:64 * part + 31, :, :], rpbT[:, :, 5:11])
                load("rel", rel[64 * part + 32:64 * part + 63, :, :], rpbT[:, :, 4:10])
            pool.wait_ge(*complete("ada1"))
            init_acc(2, acc_s[:, :, :].rearrange(flat), 3 * D, 2 * D, 3)
            pool.wait_ge(*complete("g1"))
            init_acc(3, acc_g[:, :], 5 * D, D, 4)
            ada_units(12, N_UNITS)
            pool.wait_ge(*complete("ffn10"))
            load("final_row", *bcast(final_row[:, :], final_w))

        @block.scalar
        def _(act):
            own = [0]

            def link(ins):
                own[0] += 1
                ins.then_inc(s_act, 1)
                act.wait_ge(s_act, own[0])

            def hi_block(n, j, count):
                act.wait_ge(w_landed[j], count)
                if not isinstance(n, int) or n >= RING:
                    act.wait_ge(block_done, n - RING + 1)
                nc.scalar.copy(hi[:, j, :], raw[:, j, :]).then_inc(hi_ready, 1)

            def first4(n0):
                for j in range(RING):
                    hi_block(n0 + j, j, landed(n0 + j, j))

            def rest(n0, nb):
                c0 = landed(n0, 0)
                with act.Fori(1, nb // RING) as g:
                    for j in range(RING):
                        hi_block(RING * g + (n0 + j), j, 16 * g + c0)

            def rest_blocks(n0, b0, b1):
                for b in range(b0, b1):
                    hi_block(n0 + b, b % RING, landed(n0 + b, b % RING))

            def turn(name):
                act.wait_ge(*complete(name))
                return grp(name)

            def bank_turned(name, n):
                act.wait_ge(tiles_turned, BANKS_BEFORE[name] + n + 1)

            def each_tok(name, dst, func=None, scale=1.0, width=COLS, src=lambda ap: ap):
                turn(name)
                for tok in range(TOK):
                    if func is not None:
                        ins = nc.scalar.activation(dst(tok), src(T(name, tok, width)), func)
                    elif scale != 1.0:
                        ins = nc.scalar.mul(dst(tok), src(T(name, tok, width)), scale)
                    else:
                        ins = nc.scalar.copy(dst(tok), src(T(name, tok, width)))
                ins.then_inc(freed_sem["act"], 1)

            def whole(name, dst, scale=1.0, width=4 * HALF):
                g = turn(name)
                src = ps[:, g:g + width]
                (nc.scalar.mul(dst, src, scale) if scale != 1.0 else nc.scalar.copy(dst, src)) \
                    .then_inc(freed_sem["act"], 1)

            def operand_full(names, event, gain, shift):
                for n, name in enumerate(names):
                    g = grp(name)
                    for k in range(8):
                        kk = 8 * n + k
                        if k % 2 == 0:
                            bank_turned(name, k // 2)
                        if kk >= 4 and kk % 2 == 0:
                            act.wait_ge(tile_split, SPLIT_BASE[names[0]] + kk // 2 - 1)
                        ins = nc.scalar.activation(tmp[:, (kk % 4) * SEQ:(kk % 4 + 1) * SEQ],
                                                   ps[:, g + k * SEQ:g + (k + 1) * SEQ], ACT.Identity,
                                                   scale=gain(kk), bias=shift(kk))
                        if kk % 2:
                            ins.then_inc(ev(event), 1)

            def half_squares(q, event, scratch):
                for tok in range(TOK):
                    act.wait_ge(ev(event), 2 * q + tok + 1)
                    nc.scalar.activation(scratch(tok, q), X[:, tok, q * COLS:(q + 1) * COLS], ACT.Square,
                                         accum_out=ss[:, 2 * q + tok:2 * q + tok + 1]).then_inc(ev("x_squares"), 1)

            def rms_tile(n, squares):
                act.wait_ge(ev("x_squares"), squares)
                act.wait_ge(ev("rms"), n)
                nc.scalar.mul(h_norm[:, 1, :], X[:, 1, :], ry[:, 1:2]).then_inc(ev("h_normed"), 1)

            def attention(S, units, pr, prT, nm, rs, keys, H):
                for i in range(units + 6):
                    if 2 <= i < units + 2:
                        u = i - 2
                        nk = keys(u)
                        b = (3 + u % 2) * HALF
                        act.wait_ge(S["turned"], u + 1)
                        if u >= 2:
                            act.wait_ge(S["summed"], u - 1)
                        nc.scalar.copy(prT[:, u % 2, 0:nk], ps[:, b:b + nk]).then_inc(S["copied"], 1)
                    if i < units:
                        u = i
                        nk = keys(u)
                        act.wait_ge(S["maxed"], u + 1)
                        if u >= 3:
                            act.wait_ge(S["turned"], u - 2)
                        nc.scalar.activation(pr[:, u % 3, 0:nk], ps[:, (u % 3) * HALF:(u % 3) * HALF + nk], ACT.Exp,
                                             bias=nm[:, u:u + 1], accum_out=rs[:, u:u + 1]).then_inc(S["exped"], 1)
                    if i >= 6 and i % 2 == 0:
                        h = (i - 6) // 2
                        act.wait_ge(S["backed"], h + 1)
                        nc.scalar.copy(H(h), ps[:, 7 * HALF:7 * HALF + SEQ]).then_inc(S["hi"], 1)

            for q in range(4):
                act.wait_ge(ev(f"xT{q // 2}"), 16)
                nc.scalar.copy(XH[:, 4 * q:4 * q + 4, :], xT_raw[:, 4 * q:4 * q + 4, :]).then_inc(ev("x_hi"), 1)
            first4(B_C)
            act.wait_ge(ev("pack"), 16)
            nc.scalar.activation(c_act[:, :], pk[:, PACK["c"][0]:PACK["c"][0] + 16], ACT.Silu).then_inc(ev("c_act"), 1)
            rest(B_C, 16)
            act.wait_ge(ev("small1"), 16)
            nc.scalar.copy(small_hi[:, :, :], small_raw[:, :, :]).then_inc(ev("small_hi"), 1)
            first4(B_Z)
            act.wait_ge(ev("angles"), 1)
            nc.scalar.activation(sin_t[:, :, :], rot[:, :, :], ACT.Sin).then_inc(ev("sincos"), 1)
            nc.scalar.activation(cos_t[:, :, :], ang[:, :, :], ACT.Sin).then_inc(ev("sincos"), 1)
            g = turn("c")
            for i in range(4):
                if i >= 2:
                    act.wait_ge(ev("c_squares"), i - 1)
                nc.scalar.activation(tmp[:, (i % 2) * HALF:(i % 2 + 1) * HALF], ps[:, g + i * HALF:g + (i + 1) * HALF],
                                     ACT.Square, accum_out=ss[:, i:i + 1]).then_inc(ev("c_squares"), 1)
            rest(B_Z, 16)
            first4(B_Z + 16)
            each_tok("z0", lambda t: z_tok[:, t, 0:COLS], ACT.Silu)
            act.wait_ge(*complete("kr"))
            nc.scalar.copy(krf[:, :], ps[0:ROPE, grp("kr"):grp("kr") + SEQ]).then_inc(freed_sem["act"], 1)
            each_tok("krt", lambda t: kr_tok[:, t, :], width=ROPE)
            rest(B_Z + 16, 16)
            first4(B_QN)
            each_tok("z1", lambda t: z_tok[:, t, COLS:], ACT.Silu)
            g = grp("cT")
            for k in range(8):
                if k % 2 == 0:
                    bank_turned("cT", k // 2)
                nc.scalar.mul(CH[:, k, :], ps[:, g + k * SEQ:g + (k + 1) * SEQ],
                              col("q_norm", k) if k < 4 else col("kv_norm", k - 4)).then_inc(ev("c_hi"), 1)
            first4(B_QN + 4)
            whole("qn0", qT[:, 0:8, :].rearrange(flat), MLA_SCALE)
            first4(B_QR)
            whole("qn1", qT[:, 8:16, :].rearrange(flat), MLA_SCALE)
            first4(B_KN)
            each_tok("qr", lambda t: qr_tok[:, t].rearrange(flat), None, MLA_SCALE)
            first4(B_KN + 4)
            first4(B_V)
            first4(B_V + 4)
            each_tok("v0", lambda t: v_tok[:, t, 0:COLS])
            first4(B_MO)
            each_tok("v1", lambda t: v_tok[:, t, COLS:])
            whole("qrT", qrT[:, :, :].rearrange(flat))
            whole("krT", krT[:, :], width=SEQ)
            attention(A1, 32, prob, probT, nmax, rsum, lambda u: P * (1 + u % 2), lambda h: XH[:, h, :])
            rest(B_MO, 16)
            first4(B_MO + 16)
            rest(B_MO + 16, 16)
            first4(B_CONV)
            act.wait_ge(ev("shift_col"), 1)
            nc.scalar.activation(X[:, 1, :], X[:, 1, :], ACT.Identity, scale=ry[:, 1:2], bias=shift_col[:, :]) \
              .then_inc(ev("normed"), 1)
            operand_full(("x1Ta", "x1Tb"), "x1_full", lambda k: col("ln_w0", k), lambda k: col("ln_b0", k))
            rest(B_CONV, 16)

            for q, name in enumerate(("mlq", "mlk")):
                first4((B_CONV + 16, B_VOZ)[q])
                g = turn(name)
                for k in range(8):
                    f = 8 * q + k
                    nc.scalar.activation(conv_tmp[:, k, :], ps[:, g + k * SEQ:g + (k + 1) * SEQ], ACT.Identity,
                                         scale=col("conv_w", 3 * 16 + f), bias=col("conv_b", f)) \
                      .then_inc(ev("last_tap"), 1)
                for k in range(8):
                    act.wait_ge(taps_done, 8 * q + k + 1)
                    nc.scalar.activation(qkT[:, k, q, :], conv_tmp[:, k, :], ACT.Silu).then_inc(ev("qk"), 1)
                if q == 0:
                    rest(B_CONV + 16, 16)
                    act.wait_ge(ev("small2"), 32)
                    nc.scalar.copy(small_hi[:, :, 0:40], small_raw[:, :, 0:40]).then_inc(ev("small_hi"), 1)
            rest(B_VOZ, 16)
            first4(B_VOZ + 16)

            def v_out(name, q):
                each_tok(name, lambda t: mv[:, t, 4 * q:4 * q + 4, 0:ML_V],
                         src=lambda ap: ap.rearrange("p (h e) -> p h e", e=ML_V))

            v_out("mv0", 0)
            act.wait_ge(ev("neg_abs"), 1)
            link(nc.scalar.activation(ge[:, :], ge[:, :], ACT.Exp))
            nc.scalar.activation(ge[:, :], ge[:, :], ACT.Ln, bias=1.0).then_inc(ev("log1p"), 1)
            rest(B_VOZ + 16, 16)
            act.wait_ge(ev("stabiliser"), 1)
            nc.scalar.activation(gF[:, :], gF[:, :], ACT.Exp, scale=-1.0).then_inc(ev("exp_m"), 1)
            first4(B_VOZ + 32)
            v_out("mv1", 1)
            rest(B_VOZ + 32, 16)
            first4(B_VOZ + 48)
            each_tok("mo_0", lambda t: oz[:, t, 0:COLS], ACT.Sigmoid)
            rest(B_VOZ + 48, 16)
            first4(B_VOZ + 64)
            each_tok("mo_1", lambda t: oz[:, t, COLS:], ACT.Sigmoid)
            rest(B_VOZ + 64, 16)
            first4(B_VOZ + 80)
            each_tok("mz0", lambda t: z_tmp[:, t, :], ACT.Silu)
            rest(B_VOZ + 80, 16)
            first4(B_LO)
            act.wait_ge(ev("z_used"), 1)
            each_tok("mz1", lambda t: z_tmp[:, t, :], ACT.Silu)
            for i in range(ML_H + 2):
                if i < ML_H:
                    act.wait_ge(M2["arg"], i + 1)
                    nc.scalar.activation(decay[:, i % 2, :], decay[:, i % 2, :], ACT.Exp).then_inc(M2["exp"], 1)
                if i >= 2:
                    h = i - 2
                    for tok in range(TOK):
                        u = 2 * h + tok
                        act.wait_ge(M2["h"], u + 1)
                        if u >= 4:
                            act.wait_ge(M2["sq"], u - 3)
                        nc.scalar.activation(tmp[:, (u % 4) * ML_V:(u % 4 + 1) * ML_V], h_tok[:, h, tok, :], ACT.Square,
                                             accum_out=ss[:, u:u + 1]).then_inc(M2["sq"], 1)
            for h in range(ML_H):
                act.wait_ge(M2["yT"], h + 1)
                for half in range(2):
                    k = 2 * h + half
                    nc.scalar.mul(XH[:, k, :], ps[:, h * HALF + half * SEQ:h * HALF + (half + 1) * SEQ],
                                  col("head_norm", k)).then_inc(M2["hi"], 1)
            rest(B_LO, 16)
            first4(B_LO + 16)
            act.wait_ge(ev("toep"), 16)
            nc.scalar.copy(toep_r[:, :], toep[:, :]).then_inc(ev("toep_r"), 1)
            act.wait_ge(ev("rel"), 64)
            nc.scalar.copy(rel_parts[:, :, :], rel[:, :, :]).then_inc(ev("rel_hi"), 1)
            rest(B_LO + 16, 16)

            first4(B_QA)
            for name, kc0, kc1 in (("biasa", 0, 40), ("biasb", 40, GRID_W)):
                g = turn(name)
                for c0 in range(kc0, kc1, 10):
                    n = min(10, kc1 - c0)
                    o = g + (c0 - kc0) // 10 * HALF
                    ins = nc.scalar.copy(na_bias[:, c0:c0 + n].rearrange("p c h i -> p (c h i)"),
                                         ps[:, o:o + n * N_A * REL_R])
                ins.then_inc(freed_sem["act"], 1)
            for tok in range(TOK):
                act.wait_ge(ev("x2_rows"), tok + 1)
                nc.scalar.activation(h_norm[:, tok, :], X[:, tok, :], ACT.Square, accum_out=ss[:, tok:tok + 1]) \
                  .then_inc(ev("x_squares"), 1)
            whole("g1", g_row[:, :])
            rms_tile(1, 2)
            act.wait_ge(freed_sem["dve"], FREED["ada1"][1])
            operand_full(("hTa", "hTb"), "h_full", lambda k: A_col[:, k:k + 1], lambda k: mods[:, 0, k:k + 1])
            rest(B_QA, 16)
            first4(B_KVA)
            each_tok("qa", lambda t: qa_tok[:, t].rearrange(flat))
            rest(B_KVA, 8)
            first4(B_QB)
            each_tok("kva", lambda t: kva_tok[:, t].rearrange(flat), width=HALF)
            rest(B_QB, 16)
            first4(B_KB)
            whole("qb", qbT[:, :, :].rearrange(flat), HD_SCALE)
            rest(B_KB, 16)
            first4(B_VB)
            whole("kb", kbT[:, :, :].rearrange(flat))
            rest(B_VB, 16)
            first4(B_MERGE)
            each_tok("vb", lambda t: vb_tok[:, t, :])
            whole("qaT", qaT[:, :, :].rearrange(flat), HD_SCALE)
            whole("kaT", kaT[:, :, :].rearrange(flat), width=2 * SEQ)
            attention(A3, 32, prob2, probT2, nmax2, rsum2, lambda u: SEQ,
                      lambda h: yaH[:, h, :] if h < N_A else ybH[:, h - N_A, :])
            rest(B_MERGE, 16)
            for n, (name, sig) in enumerate((("ga0", sig_a), ("ga1", sig_a), ("gb0", sig_b), ("gb1", sig_b))):
                first4(B_MERGE + 16 * (n + 1))
                c0 = n % 2 * COLS
                each_tok(name, lambda t: sig[:, t, c0:c0 + COLS], ACT.Sigmoid)
                rest(B_MERGE + 16 * (n + 1), 16 if n < 3 else 8)
            for n in range(3):
                first4(B_MERGE + 72 + 8 * n)
                rest(B_MERGE + 72 + 8 * n, 8)
            first4(B_WO)
            for name in ("mTa", "mTb"):
                g = grp(name)
                for k in range(4):
                    k0 = (8 if name == "mTb" else 0) + 2 * k
                    bank_turned(name, k)
                    nc.scalar.copy(XH[:, k0:k0 + 2, :].rearrange(flat), ps[:, g + k * HALF:g + (k + 1) * HALF]) \
                      .then_inc(ev("m_hi"), 1)
                if name == "mTa":
                    rest_blocks(B_WO, 4, 8)
            rest_blocks(B_WO, 8, 16)
            first4(B_WO + 16)
            half_squares(0, "x3", lambda t, q: h_norm[:, t, q * COLS:(q + 1) * COLS])
            rest(B_WO + 16, 16)
            first4(B_FFN)
            half_squares(1, "x3", lambda t, q: h_norm[:, t, q * COLS:(q + 1) * COLS])
            rms_tile(2, 6)
            act.wait_ge(freed_sem["dve"], FREED["ada2"][1])
            operand_full(("h2Ta", "h2Tb"), "h2_full", lambda k: A_col[:, k:k + 1], lambda k: mods[:, 0, k:k + 1])

            def ffn_blocks(p, g0, g1):
                def four(g):
                    for j in range(RING):
                        hi_block(16 * p + (RING * g + (B_FFN + j)), j, 128 * p + (32 * g + landed(B_FFN, 0)))
                if g1 - g0 == 1:
                    four(g0)
                else:
                    with act.Fori(g0, g1) as g:
                        four(g)

            def ffn_out(p, parity):
                act.wait_ge(block_done, 16 * p + (B_FFN + 16))
                if not isinstance(p, int) or p > 0:
                    act.wait_ge(ev("ffn_lo"), p)
                g = ((GROUP["ffn0"] + parity) % 2) * 4 * HALF
                nc.scalar.activation(tmp[:, :], ps[:, g:g + COLS], ACT.Silu).then_inc(ev("ffn_silu"), 1)
                act.wait_ge(product_done, p + 1)
                dst = FH[:, 4 * p:4 * p + 4, :] if isinstance(p, int) else FH[:, bass.ds(4 * p, 4), :]
                nc.scalar.copy(dst, tmp[:, :].rearrange("p (k t) -> p k t", k=4)).then_inc(ev("ffn_hi"), 1)

            ffn_blocks(0, 1, 4)
            for s in range(2):
                ffn_blocks(1 + s, 0, 1)
                ffn_out(s, s)
                ffn_blocks(1 + s, 1, 4)
            with act.Fori(1, (FFN_PASSES - 1) // 2) as i:
                for s in range(2):
                    ffn_blocks(2 * i + (1 + s), 0, 1)
                    ffn_out(2 * i + s, s)
                    ffn_blocks(2 * i + (1 + s), 1, 4)
            first4(B_DOWN)
            ffn_out(FFN_PASSES - 1, 0)
            whole("g2", g2_row[:, :])
            rest(B_DOWN, KF)
            first4(B_DOWN + KF)
            half_squares(0, "x4", lambda t, q: xsq[:, 2 * t + q, :])
            rest(B_DOWN + KF, KF)
            half_squares(1, "x4", lambda t, q: xsq[:, 2 * t + q, :])
            act.wait_ge(ev("rms"), 3)
            act.wait_ge(ev("x4_weighted"), 2)
            for tok in range(TOK):
                nc.scalar.mul(X[:, tok, 0:COLS], X[:, tok, 0:COLS], ry[:, tok:tok + 1]).then_inc(ev("result0"), 1)

        @block.vector
        def _(dve):
            own = [0]

            def mark(ins):
                own[0] += 1
                ins.then_inc(s_dve, 1)
                return own[0]

            def after(n):
                dve.wait_ge(s_dve, n)

            def link(ins):
                after(mark(ins))

            def lo_block(n, j):
                dve.wait_ge(hi_ready, n + 1)
                nc.vector.tensor_tensor(lo[:, j, :], raw[:, j, :], hi[:, j, :].bitcast(F32), ALU.subtract) \
                  .then_inc(lo_ready, 1)

            def ada_block(u, k):
                acc, init = acc_part(u)
                m = 16 * u + k
                if k == 0:
                    dve.wait_ge(bias_landed[init], 16)
                else:
                    dve.wait_ge(ada_used, m)
                dve.wait_ge(ada_landed[m % RING], 16 * (m // RING + 1))
                nc.vector.scalar_tensor_tensor(out=acc, in0=ada_raw[:, m % RING, :], scalar=c_act[:, k:k + 1], in1=acc,
                                               op0=ALU.mult, op1=ALU.add).then_inc(ada_used, 1)

            def first4(n0):
                for j in range(RING):
                    lo_block(n0 + j, j)

            def rest(n0, nb, name=None, hooks=()):
                if name not in ADA_BESIDE and not hooks:
                    with dve.Fori(1, nb // RING) as g:
                        for j in range(RING):
                            lo_block(RING * g + (n0 + j), j)
                    return
                rest_blocks(n0, RING, nb, nb, name, hooks)

            def rest_blocks(n0, b0, b1, nb, name=None, hooks=()):
                count = ADA_BESIDE.get(name, 0)
                for b in range(b0, b1):
                    lo_block(n0 + b, b % RING)
                    done = b - RING
                    for m in range(count * done // (nb - RING), count * (done + 1) // (nb - RING)):
                        ada_block((ADA_FIRST[name] + m) // KD, (ADA_FIRST[name] + m) % KD)
                    if done < len(hooks):
                        hooks[done]()

            def turn(name):
                dve.wait_ge(*complete(name))
                return grp(name)

            def free(ins):
                ins.then_inc(freed_sem["dve"], 1)

            rms_done = [0]

            def rsqrt(n, scale, src, event=None):
                a, y, t = ra[:, 0:n], ry[:, 0:n], rt[:, 0:n]
                link(nc.vector.tensor_scalar(a, src, scale, EPS, ALU.mult, ALU.add))
                link(nc.vector.tensor_scalar(t.bitcast(I32), a.bitcast(I32), 1, None, ALU.logical_shift_right))
                link(nc.vector.tensor_scalar(y.bitcast(I32), t.bitcast(I32), -1.0, 1597463007.0, ALU.mult, ALU.add))
                for _i in range(3):
                    link(nc.vector.scalar_tensor_tensor(out=t, in0=y, scalar=-0.5, in1=y, op0=ALU.mult, op1=ALU.mult))
                    link(nc.vector.tensor_tensor(t, t, a, ALU.mult))
                    ins = nc.vector.scalar_tensor_tensor(out=y, in0=t, scalar=1.5, in1=y, op0=ALU.add, op1=ALU.mult)
                    if event is not None and _i == 2:
                        rms_done[0] += 1
                        ins.then_inc(event, 1)
                        dve.wait_ge(event, rms_done[0])
                    else:
                        link(ins)

            def rotate(out1, out2, x1, x2, c, s, t1, t2):
                mark(nc.vector.tensor_tensor(t1, x1, c, ALU.mult))
                link(nc.vector.tensor_tensor(t2, x2, s, ALU.mult))
                link(nc.vector.tensor_tensor(out1, t1, t2, ALU.subtract))
                mark(nc.vector.tensor_tensor(t1, x1, s, ALU.mult))
                link(nc.vector.tensor_tensor(t2, x2, c, ALU.mult))
                return nc.vector.tensor_tensor(out2, t1, t2, ALU.add)

            def residual(name, q):
                turn(name)
                for tok in range(TOK):
                    xs = X[:, tok, q * COLS:(q + 1) * COLS]
                    ins = nc.vector.scalar_tensor_tensor(out=xs, in0=xs, scalar=ALPHA, in1=T(name, tok), op0=ALU.mult,
                                                         op1=ALU.add)
                    if tok == 0:
                        n_first = mark(ins)
                free(ins)
                for tok in range(TOK):
                    if tok == 0:
                        after(n_first)
                    else:
                        dve.wait_ge(freed_sem["dve"], FREED[name][1])
                    for n in range(2 * q, 2 * q + 2):
                        mark(nc.vector.bn_stats(st[:, tok, n, :], X[:, tok, n * HALF:(n + 1) * HALF]))

            def mean_and_rstd():
                after(own[0])
                for tok in range(TOK):
                    n_last = mark(nc.vector.bn_aggr(mvar[:, tok, :], st[:, tok, :, :]))
                after(n_last)
                rsqrt(TOK, 1.0, mvar[:, :, 1])

            def split_operand(first, event):
                for k in range(0, KD, 2):
                    src = tmp[:, (k % 4) * SEQ:(k % 4 + 2) * SEQ]
                    h, l = (m[:, k:k + 2, :].rearrange(flat) for m in (XH, XL))
                    dve.wait_ge(ev(event), k // 2 + 1)
                    link(nc.vector.tensor_copy(h, src))
                    nc.vector.tensor_tensor(l, src, h.bitcast(F32), ALU.subtract).then_inc(tile_split, 1)

            def attention(S, units, nm, rs, ri, yt, keys, prepare, gate, H, L):
                inverse = {}
                for i in range(units + 6):
                    if i < units:
                        u = i
                        nk = keys(u)
                        b = (u % 3) * HALF
                        dve.wait_ge(S["scored"], u + 1)
                        prepare(u, b, nk)
                        nc.vector.tensor_reduce(nm[:, u:u + 1], ps[:, b:b + nk], AX_X, ALU.max, negate=True) \
                          .then_inc(S["maxed"], 1)
                    if 1 <= i <= units:
                        u = i - 1
                        dve.wait_ge(S["exped"], u + 1)
                        mark(nc.vector.reciprocal(ri[:, u:u + 1], rs[:, u:u + 1]))
                        inverse[u] = own[0]
                    if 4 <= i < units + 4:
                        u = i - 4
                        b = (5 + u % 2) * HALF
                        after(inverse[u])
                        dve.wait_ge(S["summed"], u + 1)
                        if u >= 4:
                            dve.wait_ge(S["backed"], (u - 4) // 2 + 1)
                        if gate is None:
                            ins = nc.vector.tensor_scalar(yt[:, u % 4, :], ps[:, b:b + P], ri[:, u:u + 1], None,
                                                          ALU.mult)
                        else:
                            ins = nc.vector.scalar_tensor_tensor(out=yt[:, u % 4, :], in0=ps[:, b:b + P],
                                                                 scalar=ri[:, u:u + 1], in1=gate(u), op0=ALU.mult,
                                                                 op1=ALU.mult)
                        ins.then_inc(S["scaled"], 1)
                    if i >= 7 and i % 2 == 1:
                        h = (i - 7) // 2
                        dve.wait_ge(S["hi"], h + 1)
                        nc.vector.tensor_tensor(L(h), ps[:, 7 * HALF:7 * HALF + SEQ], H(h).bitcast(F32), ALU.subtract) \
                          .then_inc(S["lo"], 1)

            nc.vector.memset(ones[:, :], 1.0).then_inc(ev("ones"), 1)
            for q in range(4):
                dve.wait_ge(ev("x_hi"), q + 1)
                nc.vector.tensor_tensor(XL[:, 4 * q:4 * q + 4, :], xT_raw[:, 4 * q:4 * q + 4, :],
                                        XH[:, 4 * q:4 * q + 4, :].bitcast(F32), ALU.subtract).then_inc(ev("x_lo"), 1)
            first4(B_C)
            dve.wait_ge(ev("pos"), 16)
            dve.wait_ge(ev("inv_freq"), 16)
            link(nc.vector.tensor_copy(pos_f[:, :], pos_i[:, :]))
            for tok in range(TOK):
                n_last = mark(nc.vector.tensor_scalar(ang[:, tok, :], inv_freq[:, :], pos_f[:, tok:tok + 1], None,
                                                      ALU.mult))
            after(n_last)
            magic = 12582912.0
            link(nc.vector.tensor_scalar(turns_n[:, :, :], ang[:, :, :], 1.0 / (2 * np.pi), magic, ALU.mult, ALU.add))
            link(nc.vector.tensor_scalar(turns_n[:, :, :], turns_n[:, :, :], magic, None, ALU.subtract))
            left = 2 * np.pi
            src = ang
            for part in range(4):
                c = float(np.float32(left))
                if part < 3:
                    e = int(np.floor(np.log2(left)))
                    c = float(np.floor(left / 2.0 ** (e - 7)) * 2.0 ** (e - 7))
                left -= c
                link(nc.vector.scalar_tensor_tensor(out=rot[:, :, :], in0=turns_n[:, :, :], scalar=-c, in1=src[:, :, :],
                                                    op0=ALU.mult, op1=ALU.add))
                src = rot
            link(nc.vector.tensor_scalar(ang[:, :, :], rot[:, :, :], float(np.pi / 2), None, ALU.add))
            link(nc.vector.tensor_scalar(turns_n[:, :, :], ang[:, :, :], float(np.pi), -2 * float(np.pi), ALU.is_gt,
                                         ALU.mult))
            link(nc.vector.tensor_tensor(ang[:, :, :], ang[:, :, :], turns_n[:, :, :], ALU.add))
            mark(nc.vector.tensor_scalar(ang[:, :, :], ang[:, :, :], 3.1415925, -3.1415925, ALU.min, ALU.max))
            nc.vector.tensor_scalar(rot[:, :, :], rot[:, :, :], 3.1415925, -3.1415925, ALU.min, ALU.max) \
              .then_inc(ev("angles"), 1)
            rest(B_C, 16)
            dve.wait_ge(ev("small_hi"), 1)
            nc.vector.tensor_tensor(small_lo[:, :, :], small_raw[:, :, :], small_hi[:, :, :].bitcast(F32),
                                    ALU.subtract).then_inc(ev("small_lo"), 1)
            first4(B_Z)
            g = turn("c")
            dve.wait_ge(ev("c_squares"), 4)
            rsqrt(4, 1.0 / LORA, ss[:, 0:4])
            for i in range(4):
                ins = nc.vector.tensor_scalar(c_tok[:, i // 2, (i % 2) * LORA:(i % 2 + 1) * LORA],
                                              ps[:, g + i * HALF:g + (i + 1) * HALF], ry[:, i:i + 1], None, ALU.mult)
            free(ins)
            dve.wait_ge(ev("c_act"), 1)
            rest(B_Z, 16, "z0")
            first4(B_Z + 16)
            rest(B_Z + 16, 16, "z1")
            first4(B_QN)
            dve.wait_ge(ev("sincos"), 2)
            dve.wait_ge(freed_sem["act"], FREED["krt"][1])
            t1, t2 = (rope_tmp[:, i, 0:64].rearrange("p (a b) -> p a b", a=TOK) for i in range(2))
            link(rotate(krr_tok[:, :, 0, 0:32], krr_tok[:, :, 0, 32:64], kr_tok[:, :, 0:32], kr_tok[:, :, 32:64],
                        cos_t[:, :, :], sin_t[:, :, :], t1, t2))
            nc.vector.tensor_copy(krr_tok[:, :, 1, :], krr_tok[:, :, 0, :]).then_inc(ev("k_roped"), 1)
            g = grp("cT")
            for k in range(8):
                dve.wait_ge(ev("c_hi"), (k | 1) + 1)
                nc.vector.scalar_tensor_tensor(out=CL[:, k, :], in0=ps[:, g + k * SEQ:g + (k + 1) * SEQ],
                                               scalar=col("q_norm", k) if k < 4 else col("kv_norm", k - 4),
                                               in1=CH[:, k, :].bitcast(F32), op0=ALU.mult, op1=ALU.subtract) \
                  .then_inc(tile_split, 1)
            first4(B_QN + 4)
            first4(B_QR)
            first4(B_KN)
            first4(B_KN + 4)
            g = turn("kn0")
            free(nc.vector.tensor_copy(kT[:, 0:8, :].rearrange(flat), ps[:, g:g + 4 * HALF]))
            first4(B_V)
            g = turn("kn1")
            free(nc.vector.tensor_copy(kT[:, 8:16, :].rearrange(flat), ps[:, g:g + 4 * HALF]))
            dve.wait_ge(freed_sem["act"], FREED["qr"][1])
            for tok in range(TOK):
                t1, t2 = (rope_tmp[:, i, :].rearrange("p (h e) -> p h e", h=16) for i in range(2))
                if tok:
                    dve.wait_ge(ev("q_roped"), tok)
                c, s = (tab[:, tok, :].unsqueeze(1).broadcast_to([P, 16, 32]) for tab in (cos_t, sin_t))
                rotate(qrr_tok[:, tok, :, 0:32], qrr_tok[:, tok, :, 32:64], qr_tok[:, tok, :, 0:32],
                       qr_tok[:, tok, :, 32:64], c, s, t1, t2).then_inc(ev("q_roped"), 1)
                if tok == 0:
                    first4(B_V + 4)
            first4(B_MO)

            def mask_chunk(u, b, nk):
                link(nc.vector.memset(ps[0:64, b + nk - 64:b + nk], NEG))

            attention(A1, 32, nmax, rsum, rinv, y_tok, lambda u: P * (1 + u % 2), mask_chunk,
                      lambda u: z_tok[:, u % 2, (u // 2) * P:(u // 2 + 1) * P],
                      lambda h: XH[:, h, :], lambda h: XL[:, h, :])
            rest(B_MO, 16, "mo0")
            first4(B_MO + 16)
            dve.wait_ge(ev("x"), 16)
            residual("mo0", 0)
            rest(B_MO + 16, 16, "mo1")
            first4(B_CONV)
            residual("mo1", 1)
            mean_and_rstd()
            nc.vector.scalar_tensor_tensor(out=shift_col[:, :], in0=mvar[:, 1, 0:1], scalar=-1.0, in1=ry[:, 1:2],
                                           op0=ALU.mult, op1=ALU.mult).then_inc(ev("shift_col"), 1)
            nc.vector.tensor_scalar(X[:, 0, :], X[:, 0, :], mvar[:, 0, 0:1], ry[:, 0:1], ALU.subtract, ALU.mult) \
              .then_inc(ev("normed"), 1)
            split_operand("x1Ta", "x1_full")

            def x1_rows(i):
                def do():
                    tok = i // 2
                    if i == 0:
                        dve.wait_ge(ev("rows0"), 32)
                        dve.wait_ge(*complete("x1Tb"))
                    if i % 2:
                        dve.wait_ge(ev("x1_rows"), i)
                    nc.vector.tensor_tensor(X[:, tok, :], X[:, tok, :], (row_b if i % 2 else row_w)[:, :],
                                            ALU.add if i % 2 else ALU.mult).then_inc(ev("x1_rows"), 1)
                return do

            skip = lambda: None
            rest(B_CONV, 16, "mlq", [skip, x1_rows(0), skip, skip, x1_rows(1), skip, skip, x1_rows(2), skip, skip,
                                     x1_rows(3)])

            for q, name in enumerate(("mlq", "mlk")):
                first4((B_CONV + 16, B_VOZ)[q])
                g = turn(name)
                n0 = own[0]
                for s in range(1, TAPS):
                    for k in range(8):
                        if s == 1:
                            dve.wait_ge(ev("last_tap"), 8 * q + (k | 1) + 1)
                        else:
                            after(n0 + 8 * (s - 2) + k + 1)
                        f = 8 * q + k
                        ins = nc.vector.scalar_tensor_tensor(
                            out=conv_tmp[:, k, s:], in0=ps[:, g + k * SEQ:g + (k + 1) * SEQ - s],
                            scalar=col("conv_w", (TAPS - 1 - s) * 16 + f), in1=conv_tmp[:, k, s:],
                            op0=ALU.mult, op1=ALU.add)
                        ins.then_inc(taps_done, 1) if s == TAPS - 1 else mark(ins)
                if q == 0:
                    rest(B_CONV + 16, 16, "mlk")
                    dve.wait_ge(ev("small_hi"), 2)
                    nc.vector.tensor_tensor(small_lo[:, :, 0:40], small_raw[:, :, 0:40],
                                            small_hi[:, :, 0:40].bitcast(F32), ALU.subtract) \
                      .then_inc(ev("small_lo"), 1)
            for tok in range(TOK):
                n_last = mark(nc.vector.memset(mv[:, tok, :, ML_V:ML_V + 1], 1.0))
            rest(B_VOZ, 16, "mv0")
            first4(B_VOZ + 16)
            g = turn("gates")
            dve.wait_ge(ev("gate_bias"), 32)
            mark(nc.vector.tensor_scalar(gi[:, :], ps[0:8, g:g + SEQ], gate_bias[0:8, :], None, ALU.add))
            free(nc.vector.tensor_scalar(gf[:, :], ps[32:40, g:g + SEQ], gate_bias[32:40, :], None, ALU.add))
            dve.wait_ge(freed_sem["dve"], FREED["gates"][1])
            link(nc.vector.tensor_scalar(ge[:, :], gf[:, :], -1.0, None, ALU.mult))
            nc.vector.tensor_tensor(ge[:, :], ge[:, :], gf[:, :], ALU.min).then_inc(ev("neg_abs"), 1)
            link(nc.vector.memset(gM[:, :], 1.0))
            dve.wait_ge(ev("log1p"), 1)
            link(nc.vector.scalar_tensor_tensor(out=gf[:, :], in0=gf[:, :], scalar=0.0, in1=ge[:, :], op0=ALU.min,
                                                op1=ALU.subtract))
            link(nc.vector.tensor_tensor_scan(gF[:, :], gM[:, :], gf[:, :], 0.0, ALU.mult, ALU.add))
            link(nc.vector.tensor_tensor(gi[:, :], gi[:, :], gF[:, :], ALU.subtract))
            link(nc.vector.tensor_tensor_scan(gM[:, :], gi[:, :], gi[:, :], 0.0, ALU.max, ALU.max))
            mark(nc.vector.tensor_scalar(ge[:, :], gM[:, :], -1.0, None, ALU.mult))
            nc.vector.tensor_tensor(gF[:, :], gF[:, :], gM[:, :], ALU.add).then_inc(ev("stabiliser"), 1)
            rest(B_VOZ + 16, 16, "mv1")
            first4(B_VOZ + 32)
            rest(B_VOZ + 32, 16, "mo_0")
            first4(B_VOZ + 48)
            rest(B_VOZ + 48, 16, "mo_1")
            first4(B_VOZ + 64)
            rest(B_VOZ + 64, 16, "mz0")
            first4(B_VOZ + 80)

            def gate_z(name, q):
                dve.wait_ge(freed_sem["act"], FREED[name][1])
                for tok in range(TOK):
                    o = oz[:, tok, q * COLS:(q + 1) * COLS]
                    ins = nc.vector.tensor_tensor(o, o, z_tmp[:, tok, :], ALU.mult)
                    if tok == 0:
                        mark(ins)
                ins.then_inc(ev("z_used"), 1)

            gate_z("mz0", 0)
            rest(B_VOZ + 80, 16, "mz1")
            first4(B_LO)
            gate_z("mz1", 1)
            dve.wait_ge(M2["prep"], 1)
            mark(nc.vector.tensor_copy(G_col[:, :, :].rearrange(flat), ps[:, 6 * HALF:6 * HALF + 16]))
            nc.vector.tensor_copy(E_col[:, :, :].rearrange(flat), ps[:, 6 * HALF + 16:6 * HALF + 32]) \
              .then_inc(M2["prepc"], 1)
            dve.wait_ge(M2["prepc"], 1)
            after(own[0])
            dve.wait_ge(ev("causal"), 16)
            for i in range(ML_H + 2):
                if i < ML_H:
                    h = i
                    b = (2 + h % 2) * HALF
                    dve.wait_ge(M2["bc"], h + 1)
                    if h >= 2:
                        dve.wait_ge(M2["pv"], 2 * (h - 1))
                    mark(nc.vector.scalar_tensor_tensor(out=decay[:, h % 2, 0:SEQ], in0=ps[:, b:b + SEQ],
                                                        scalar=G_col[:, 0, h:h + 1], in1=causal[:, :], op0=ALU.add,
                                                        op1=ALU.add))
                    nc.vector.scalar_tensor_tensor(out=decay[:, h % 2, SEQ:SEQ + P], in0=ps[:, b + P:b + SEQ],
                                                   scalar=G_col[:, 1, h:h + 1], in1=causal[:, 0:P], op0=ALU.add,
                                                   op1=ALU.add).then_inc(M2["arg"], 1)
                if 1 <= i <= ML_H:
                    h = i - 1
                    b = (h % 2) * HALF
                    dve.wait_ge(M2["exp"], h + 1)
                    dve.wait_ge(M2["st"], h + 1)
                    nc.vector.scalar_tensor_tensor(out=decay[:, h % 2, :], in0=ps[:, b:b + 384], scalar=ML_SCALE,
                                                   in1=decay[:, h % 2, :], op0=ALU.mult, op1=ALU.mult) \
                      .then_inc(M2["w"], 1)
                if i >= 2:
                    h = i - 2
                    for tok in range(TOK):
                        u = 2 * h + tok
                        b = (4 + u % 4) * HALF
                        dve.wait_ge(M2["pv"], u + 1)
                        d = dens[:, u:u + 1]
                        link(nc.vector.tensor_scalar(d, ps[:, b + ML_V:b + ML_V + 1], -1.0, None, ALU.mult))
                        link(nc.vector.tensor_tensor(d, d, ps[:, b + ML_V:b + ML_V + 1], ALU.max))
                        link(nc.vector.tensor_tensor(d, d, E_col[:, tok, h:h + 1], ALU.max))
                        link(nc.vector.reciprocal(dinv[:, u:u + 1], d))
                        nc.vector.tensor_scalar(h_tok[:, h, tok, :], ps[:, b:b + ML_V], dinv[:, u:u + 1], None,
                                                ALU.mult).then_inc(M2["h"], 1)
            dve.wait_ge(M2["sq"], 16)
            dve.wait_ge(ev("z_used"), 2)
            rsqrt(16, 1.0 / ML_V, ss[:, 0:16])
            for u in range(16):
                h, tok = u // 2, u % 2
                o = oz[:, tok, h * ML_V:(h + 1) * ML_V]
                nc.vector.scalar_tensor_tensor(out=o, in0=h_tok[:, h, tok, :], scalar=ry[:, u:u + 1], in1=o,
                                               op0=ALU.mult, op1=ALU.mult).then_inc(M2["y"], 1)
            for k in range(KD):
                b = (k // 2) * HALF + (k % 2) * SEQ
                dve.wait_ge(M2["hi"], (k | 1) + 1)
                nc.vector.scalar_tensor_tensor(out=XL[:, k, :], in0=ps[:, b:b + SEQ], scalar=col("head_norm", k),
                                               in1=XH[:, k, :].bitcast(F32), op0=ALU.mult, op1=ALU.subtract) \
                  .then_inc(M2["lo"], 1)
            rest(B_LO, 16)
            first4(B_LO + 16)
            residual("lo0", 0)
            rest(B_LO + 16, 16)
            first4(B_QA)
            dve.wait_ge(ev("rel_hi"), 1)
            nc.vector.tensor_tensor(rel_parts[64:, :, :], rel[64:, :, :], rel_parts[64:, :, :].bitcast(F32),
                                    ALU.subtract).then_inc(ev("rel_parts"), 1)
            residual("lo1", 1)

            mean_and_rstd()
            dve.wait_ge(ev("rows1"), 32)
            for tok in range(TOK):
                link(nc.vector.scalar_tensor_tensor(out=X[:, tok, :], in0=X[:, tok, :], scalar=mvar[:, tok, 0:1],
                                                    in1=row_w[:, :], op0=ALU.subtract, op1=ALU.mult))
                nc.vector.scalar_tensor_tensor(out=X[:, tok, :], in0=X[:, tok, :], scalar=ry[:, tok:tok + 1],
                                               in1=row_b[:, :], op0=ALU.mult, op1=ALU.add) \
                  .then_inc(ev("x2_rows"), 1)

            def modulation(name, norm):
                g = turn(name)
                mark(nc.vector.tensor_copy(mods[:, 0, :], ps[:, g:g + 16]))
                o = PACK[norm][0]
                free(nc.vector.scalar_tensor_tensor(out=A_col[:, :], in0=ps[:, g + 16:g + 32], scalar=1.0,
                                                    in1=pk[:, o:o + 16], op0=ALU.add, op1=ALU.mult))

            def rms_rows(n_squares, src):
                dve.wait_ge(ev("x_squares"), n_squares)
                if src is None:
                    src = ss[:, 4:6]
                    link(nc.vector.tensor_tensor(src, ss[:, 0:2], ss[:, 2:4], ALU.add))
                rsqrt(TOK, 1.0 / D, src, ev("rms"))
                nc.vector.tensor_scalar(h_norm[:, 0, :], X[:, 0, :], ry[:, 0:1], None, ALU.mult) \
                  .then_inc(ev("h_normed"), 1)

            modulation("ada1", "norm1")
            rms_rows(2, ss[:, 0:2])
            split_operand("hTa", "h_full")
            rest(B_QA, 16, "qa")
            first4(B_KVA)
            rest(B_KVA, 8, "kva")
            first4(B_QB)

            def norm_heads(x, heads, which):
                sq = tmp[:, 0:heads * HD].rearrange("p (h e) -> p h e", e=HD)

                def squares():
                    link(nc.vector.tensor_tensor(sq, x, x, ALU.mult))
                    link(nc.vector.tensor_reduce(ss[:, 0:heads], sq, AX_X, ALU.add))

                def scale():
                    rsqrt(heads, 1.0 / HD, ss[:, 0:heads])
                    link(nc.vector.tensor_tensor(x, x, ry[:, 0:heads].unsqueeze(2).broadcast_to([P, heads, HD]),
                                                 ALU.mult))

                def gain():
                    link(nc.vector.tensor_tensor(x, x, qkn[:, which, :].unsqueeze(1).broadcast_to([P, heads, HD]),
                                                 ALU.mult))
                return [squares, scale, gain]

            roped = [0]

            def rope_heads(x, heads, tok, event):
                v = x.rearrange("p h (i two) -> p h i two", two=2)
                x0, x1 = v[:, :, :, 0], v[:, :, :, 1]
                w = heads * HD // 2
                sh = "p (h i) -> p h i"
                t = [rope2[:, 0, 0:w].rearrange(sh, h=heads), rope2[:, 1, 0:w].rearrange(sh, h=heads),
                     tmp[:, 0:w].rearrange(sh, h=heads), tmp[:, HALF:HALF + w].rearrange(sh, h=heads)]
                c, s = (tab[:, tok, :].unsqueeze(1).broadcast_to([P, heads, HD // 2]) for tab in (cos2, sin2))

                def products():
                    mark(nc.vector.tensor_tensor(t[0], x0, c, ALU.mult))
                    mark(nc.vector.tensor_tensor(t[1], x1, s, ALU.mult))

                def products2():
                    mark(nc.vector.tensor_tensor(t[2], x0, s, ALU.mult))
                    link(nc.vector.tensor_tensor(t[3], x1, c, ALU.mult))

                def sums():
                    mark(nc.vector.tensor_tensor(x0, t[0], t[1], ALU.subtract))
                    nc.vector.tensor_tensor(x1, t[2], t[3], ALU.add).then_inc(ev(event), 1)
                    roped[0] += 1
                    dve.wait_ge(ev(event), roped[0])
                return [products, products2, sums]

            def wait_tables():
                dve.wait_ge(ev("tables2"), 64)
                dve.wait_ge(freed_sem["act"], FREED["qa"][1])

            def wait_kva():
                dve.wait_ge(freed_sem["act"], FREED["kva"][1])

            steps = []
            for tok in range(TOK):
                steps += norm_heads(qa_tok[:, tok], N_A, 0) + rope_heads(qa_tok[:, tok], N_A, tok, "qk_roped")
            for tok in range(TOK):
                steps += norm_heads(kva_tok[:, tok, 0:N_KV], N_KV, 1) \
                    + rope_heads(kva_tok[:, tok, 0:N_KV], N_KV, tok, "qk_roped")
            rest(B_QB, 16, "qb", [wait_tables] + steps[0:10])
            first4(B_KB)
            wait_kva()
            rest(B_KB, 16, "kb", steps[10:22])
            first4(B_VB)
            def add_window(c0, c1):
                def do():
                    if c0 == 0:
                        dve.wait_ge(ev("window"), 16)
                        dve.wait_ge(freed_sem["act"], FREED["biasb"][1])
                    v = na_bias[:, c0:c1].rearrange("p c h i -> p c (h i)")
                    mark(nc.vector.tensor_tensor(
                        v, v, window[:, c0:c1].unsqueeze(2).broadcast_to([P, c1 - c0, N_A * REL_R]), ALU.add))
                return do

            rest(B_VB, 16, "vb", steps[22:] + [add_window(16 * i, 16 * i + 16) for i in range(4)])
            first4(B_MERGE)
            after(own[0])
            dve.wait_ge(ev("qk_roped"), 4)

            def add_bias(u, b, nk):
                if u >= 16:
                    h, blk = (u - 16) // 2, u % 2
                    i0 = 2 - 2 * blk
                    v = ps[:, b:b + SEQ].rearrange("p (r c) -> p r c", r=4)
                    link(nc.vector.tensor_tensor(v, v, na_bias[:, :, h, i0:i0 + 4].rearrange("p c r -> p r c"),
                                                 ALU.add))

            attention(A3, 32, nmax2, rsum2, rinv2, y_tok2, lambda u: SEQ, add_bias, None,
                      lambda h: yaH[:, h, :] if h < N_A else ybH[:, h - N_A, :],
                      lambda h: yaL[:, h, :] if h < N_A else ybL[:, h - N_A, :])
            rest(B_MERGE, 16, "ga0")
            for n, name in enumerate(("ga1", "gb0", "gb1")):
                first4(B_MERGE + 16 * (n + 1))
                rest(B_MERGE + 16 * (n + 1), 16, name)
            first4(B_MERGE + 64)
            rest(B_MERGE + 64, 8, "oa0")
            for n, name in enumerate(("oa0", "ob0", "oa1", "ob1")):
                n0 = B_MERGE + 72 + 8 * n
                first4(n0)
                turn(name)
                q = n // 2
                sig = (sig_a, sig_b)[n % 2]
                dve.wait_ge(freed_sem["act"], FREED[("ga", "gb")[n % 2] + str(q)][1])
                for tok in range(TOK):
                    v = sig[:, tok, q * COLS:(q + 1) * COLS]
                    ins = nc.vector.tensor_tensor(v, v, T(name, tok), ALU.mult)
                    if tok == 0:
                        first_tok = mark(ins)
                free(ins)
                if n % 2:
                    for tok in range(TOK):
                        if tok == 0:
                            after(first_tok)
                        else:
                            dve.wait_ge(freed_sem["dve"], FREED[name][1])
                        m = merged[:, tok, q * COLS:(q + 1) * COLS]
                        nc.vector.tensor_tensor(m, m, sig_b[:, tok, q * COLS:(q + 1) * COLS], ALU.add) \
                          .then_inc(ev("merged"), 1)
                if n < 3:
                    rest(n0, 8, ("ob0", "oa1", "ob1")[n])
            for name in ("mTa", "mTb"):
                g = grp(name)
                for k in range(4):
                    k0 = (8 if name == "mTb" else 0) + 2 * k
                    dve.wait_ge(ev("m_hi"), k0 // 2 + 1)
                    nc.vector.tensor_tensor(XL[:, k0:k0 + 2, :].rearrange(flat), ps[:, g + k * HALF:g + (k + 1) * HALF],
                                            XH[:, k0:k0 + 2, :].rearrange(flat).bitcast(F32), ALU.subtract) \
                      .then_inc(tile_split, 1)
                if name == "mTa":
                    rest_blocks(B_WO, 4, 8, 16, "wo0")

            def gated_residual(name, q, row, event):
                turn(name)
                for tok in range(TOK):
                    xs = X[:, tok, q * COLS:(q + 1) * COLS]
                    ins = nc.vector.tensor_tensor(tmp[:, :], T(name, tok), row[:, q * COLS:(q + 1) * COLS], ALU.mult)
                    if tok == 0:
                        link(ins)
                    else:
                        free(ins)
                        dve.wait_ge(freed_sem["dve"], FREED[name][1])
                    nc.vector.tensor_tensor(xs, xs, tmp[:, :], ALU.add).then_inc(ev(event), 1)
                    dve.wait_ge(ev(event), 2 * q + tok + 1)

            rest_blocks(B_WO, 8, 16, 16, "wo0")
            first4(B_WO + 16)
            dve.wait_ge(freed_sem["act"], FREED["g1"][1])
            gated_residual("wo0", 0, g_row, "x3")
            rest(B_WO + 16, 16, "wo1")
            first4(B_FFN)
            gated_residual("wo1", 1, g_row, "x3")
            modulation("ada2", "norm2")
            rms_rows(6, None)
            split_operand("h2Ta", "h2_full")

            def ffn_blocks(p, g0, g1):
                def four(g):
                    for j in range(RING):
                        lo_block(16 * p + (RING * g + (B_FFN + j)), j)
                if g1 - g0 == 1:
                    four(g0)
                else:
                    with dve.Fori(g0, g1) as g:
                        four(g)

            def ffn_out(p, parity):
                g = ((GROUP["ffn0"] + parity) % 2) * 4 * HALF
                dve.wait_ge(ev("ffn_silu"), p + 1)
                nc.vector.tensor_tensor(tmp[:, :], tmp[:, :], ps[:, g + COLS:g + 2 * COLS], ALU.mult) \
                  .then_inc(product_done, 1)
                dve.wait_ge(ev("ffn_hi"), p + 1)
                sl = (slice(None), slice(4 * p, 4 * p + 4) if isinstance(p, int) else bass.ds(4 * p, 4), slice(None))
                nc.vector.tensor_tensor(FL[sl], tmp[:, :].rearrange("p (k t) -> p k t", k=4), FH[sl].bitcast(F32),
                                        ALU.subtract).then_inc(ev("ffn_lo"), 1)

            rest(B_FFN, 16, "ffn0")
            for s in range(2):
                ffn_blocks(1 + s, 0, 1)
                ffn_out(s, s)
                ffn_blocks(1 + s, 1, 4)
            with dve.Fori(1, (FFN_PASSES - 1) // 2) as i:
                for s in range(2):
                    ffn_blocks(2 * i + (1 + s), 0, 1)
                    ffn_out(2 * i + s, s)
                    ffn_blocks(2 * i + (1 + s), 1, 4)
            first4(B_DOWN)
            ffn_out(FFN_PASSES - 1, 0)
            rest(B_DOWN, KF)
            first4(B_DOWN + KF)
            dve.wait_ge(freed_sem["act"], FREED["g2"][1])
            gated_residual("down0", 0, g2_row, "x4")
            dve.wait_ge(ev("x_squares"), 8)
            dve.wait_ge(ev("final_row"), 16)
            for tok in range(TOK):
                nc.vector.tensor_tensor(X[:, tok, 0:COLS], X[:, tok, 0:COLS], final_row[:, 0:COLS], ALU.mult) \
                  .then_inc(ev("x4_weighted"), 1)
            rest(B_DOWN + KF, KF)
            gated_residual("down1", 1, g2_row, "x4")
            dve.wait_ge(ev("x_squares"), 10)
            link(nc.vector.tensor_tensor(ss[:, 4:6], ss[:, 0:2], ss[:, 2:4], ALU.add))
            rsqrt(TOK, 1.0 / D, ss[:, 4:6], ev("rms"))
            for tok in range(TOK):
                nc.vector.scalar_tensor_tensor(out=X[:, tok, COLS:], in0=X[:, tok, COLS:], scalar=ry[:, tok:tok + 1],
                                               in1=final_row[:, COLS:], op0=ALU.mult, op1=ALU.mult) \
                  .then_inc(ev("result1"), 1)

        @block.tensor
        def _(pe):
            mm = nc.tensor.matmul

            def start(name):
                if LAST_IN_GROUP[name] is not None:
                    kind, n = FREED[LAST_IN_GROUP[name]]
                    pe.wait_ge(freed_sem[kind], n)
                return grp(name)

            def done(ins):
                ins.then_inc(turn_done, 1)

            def token_major(name, n0, nb, H, L, need=None, width=COLS, per_block=1, blocks=None):
                b0, b1 = blocks or (0, nb)
                g = start(name) if b0 == 0 else grp(name)
                for b in range(b0, b1):
                    j = b % RING
                    pe.wait_ge(lo_ready, n0 + b + 1)
                    for sub in range(per_block):
                        k = b * per_block + sub
                        if need is not None:
                            pe.wait_ge(*need(k))
                        for tok in range(TOK):
                            xh, xl = (m[:, k, tok * P:(tok + 1) * P] for m in (H, L))
                            for x, w, first in ((xh, hi, k == 0), (xh, lo, False), (xl, hi, False)):
                                for c in range(COLS // per_block // HALF):
                                    o = g + (2 * tok + c) * HALF
                                    c0 = (sub + c) * HALF
                                    ins = mm(ps[:, o:o + HALF], x, w[:, j, c0:c0 + HALF], start=first,
                                             stop=(k == nb * per_block - 1 and x is xl), skip_group_check=True)
                    ins.then_inc(block_done, 1)

            def feature_block(g, k, j, H, L, first, last):
                for m in range(8):
                    for w, x, lead in ((hi, H, True), (hi, L, False), (lo, H, False)):
                        o = g + m * SEQ
                        ins = mm(ps[:, o:o + SEQ], w[:, j, m * P:(m + 1) * P], x(k),
                                 start=first and lead and m % 2 == 0, stop=last and w is lo, skip_group_check=True)
                ins.then_inc(block_done, 1)

            def feature_major(name, n0, nb, H, L, need=None, per=1):
                g = start(name)
                for j in range(RING):
                    pe.wait_ge(lo_ready, n0 + j + 1)
                    if need is not None:
                        pe.wait_ge(need[0], need[1] + j // per + 1)
                    feature_block(g, j, j, lambda k: H[:, k, :], lambda k: L[:, k, :], j == 0,
                                  nb == RING and j == RING - 1)
                if nb > RING:
                    with pe.Fori(1, nb // RING) as gg:
                        for j in range(RING):
                            pe.wait_ge(lo_ready, RING * gg + (n0 + j + 1))
                            if need is not None:
                                pe.wait_ge(need[0], RING // per * gg + (need[1] + j // per + 1))
                            feature_block(g, RING * gg + j, j, lambda k: H[:, bass.ds(k, 1), :].rearrange(flat),
                                          lambda k: L[:, bass.ds(k, 1), :].rearrange(flat), False, True)

            def small_linear(name, n, count):
                g = start(name)
                pe.wait_ge(ev("small_lo"), count)
                for k in range(KD):
                    for w, x in ((small_hi, XH), (small_hi, XL), (small_lo, XH)):
                        ins = mm(ps[0:n, g:g + SEQ], w[:, k, 0:n], x[:, k, :], start=(k == 0 and w is small_hi and x is XH),
                                 stop=(k == KD - 1 and w is small_lo), skip_group_check=True)
                done(ins)

            def transposes(name, tiles):
                g = start(name)
                for n, (o, src) in enumerate(tiles):
                    ins = nc.tensor.transpose(ps[0:src.shape[1], g + o:g + o + P], src, ident[:, :])
                    if name in BANKS_BEFORE and n % 4 == 3:
                        ins.then_inc(tiles_turned, 1)
                if name not in BANKS_BEFORE:
                    done(ins)

            def operand_tiles(src, k0):
                return [(k * SEQ + tok * P, src[:, tok, (k0 + k) * P:(k0 + k + 1) * P])
                        for k in range(8) for tok in range(TOK)]

            def attention(S, units, pr, prT, yt, keys, operands, values):
                for i in range(units + 6):
                    if i < units:
                        u = i
                        nk = keys(u)
                        b = (u % 3) * HALF
                        if u >= 3:
                            pe.wait_ge(S["exped"], u - 2)
                        ops = operands(u)
                        for n, (q, kk) in enumerate(ops):
                            ins = mm(ps[:, b:b + nk], q, kk, start=(n == 0), stop=(n == len(ops) - 1),
                                     skip_group_check=True)
                        ins.then_inc(S["scored"], 1)
                    if 2 <= i < units + 2:
                        u = i - 2
                        b = (3 + u % 2) * HALF
                        pe.wait_ge(S["exped"], u + 1)
                        if u >= 2:
                            pe.wait_ge(S["copied"], u - 1)
                        for t in range(keys(u) // P):
                            ins = nc.tensor.transpose(ps[:, b + t * P:b + (t + 1) * P], pr[:, u % 3, t * P:(t + 1) * P],
                                                      ident[:, :])
                        ins.then_inc(S["turned"], 1)
                    if 3 <= i < units + 3:
                        u = i - 3
                        b = (5 + u % 2) * HALF
                        pe.wait_ge(S["copied"], u + 1)
                        if u >= 2:
                            pe.wait_ge(S["scaled"], u - 1)
                        n = keys(u) // P
                        for t in range(n):
                            ins = mm(ps[:, b:b + P], prT[:, u % 2, t * P:(t + 1) * P], values(u, t), start=(t == 0),
                                     stop=(t == n - 1), skip_group_check=True)
                        ins.then_inc(S["summed"], 1)
                    if i >= 6 and i % 2 == 0:
                        h = (i - 6) // 2
                        pe.wait_ge(S["scaled"], 2 * h + 2)
                        if h >= 1:
                            pe.wait_ge(S["lo"], h)
                        for tok in range(TOK):
                            ins = nc.tensor.transpose(ps[:, 7 * HALF + tok * P:7 * HALF + (tok + 1) * P],
                                                      yt[:, (2 * h + tok) % 4, :], ident[:, :])
                        ins.then_inc(S["backed"], 1)

            pe.wait_ge(ev("ones"), 1)
            token_major("c", B_C, 16, XH, XL, lambda k: (ev("x_lo"), k // 4 + 1))
            token_major("z0", B_Z, 16, XH, XL)
            small_linear("kr", ROPE, 1)
            g = start("krt")
            pe.wait_ge(ev("ident"), 16)
            pe.wait_ge(freed_sem["act"], FREED["kr"][1])
            for tok in range(TOK):
                ins = nc.tensor.transpose(ps[:, g + 2 * tok * HALF:g + 2 * tok * HALF + ROPE],
                                          krf[:, tok * P:(tok + 1) * P], ident[0:ROPE, 0:ROPE])
            done(ins)
            token_major("z1", B_Z + 16, 16, XH, XL)
            transposes("cT", operand_tiles(c_tok, 0))
            for q in range(2):
                feature_major(f"qn{q}", B_QN + 4 * q, 4, CH, CL, (tile_split, 0))
            token_major("qr", B_QR, 4, CH, CL)
            CHv, CLv = CH[:, 4:8, :], CL[:, 4:8, :]
            for q in range(2):
                feature_major(f"kn{q}", B_KN + 4 * q, 4, CHv, CLv, (tile_split, 4))
            for q in range(2):
                token_major(f"v{q}", B_V + 4 * q, 4, CHv, CLv)
            pe.wait_ge(ev("q_roped"), 2)
            transposes("qrT", [(k * SEQ + tok * P, qrr_tok[:, tok, 2 * k:2 * k + 2, :].rearrange(flat))
                               for k in range(8) for tok in range(TOK)])
            pe.wait_ge(ev("k_roped"), 1)
            transposes("krT", [(tok * P, krr_tok[:, tok].rearrange(flat)) for tok in range(TOK)])
            pe.wait_ge(freed_sem["act"], FREED["krT"][1])

            def mla_operands(u):
                h, blk = u // 2, u % 2
                r0 = (h % 2) * ROPE
                t, nk = slice(blk * P, (blk + 1) * P), P * (1 + blk)
                return [(qT[:, h, t], kT[:, h, 0:nk]), (qrT[r0:r0 + ROPE, h // 2, t], krT[r0:r0 + ROPE, 0:nk])]

            attention(A1, 32, prob, probT, y_tok, lambda u: P * (1 + u % 2), mla_operands,
                      lambda u, t: v_tok[:, t, (u // 2) * P:(u // 2 + 1) * P])
            token_major("mo0", B_MO, 16, XH, XL, lambda k: (A1["lo"], k + 1))
            token_major("mo1", B_MO + 16, 16, XH, XL)
            pe.wait_ge(ev("normed"), 2)
            transposes("x1Ta", operand_tiles(X, 0))
            transposes("x1Tb", operand_tiles(X, 8))

            feature_major("mlq", B_CONV, 16, XH, XL, (tile_split, SPLIT_BASE["x1Ta"]), 2)
            feature_major("mlk", B_CONV + 16, 16, XH, XL)
            token_major("mv0", B_VOZ, 16, XH, XL)
            small_linear("gates", 40, 2)
            for n, name in enumerate(("mv1", "mo_0", "mo_1", "mz0", "mz1")):
                token_major(name, B_VOZ + 16 * (n + 1), 16, XH, XL)
            pe.wait_ge(freed_sem["act"], FREED["mz1"][1])
            pe.wait_ge(ev("exp_m"), 1)
            for n, src in enumerate((gi, gF)):
                for tok in range(TOK):
                    o = 6 * HALF + 16 * n + 8 * tok
                    ins = nc.tensor.transpose(ps[:, o:o + 8], src[:, tok * P:(tok + 1) * P], ident[0:8, 0:8])
            ins.then_inc(M2["prep"], 1)
            pe.wait_ge(ev("select"), 16)
            pe.wait_ge(ev("qk"), 16)
            for i in range(ML_H + 1):
                if i < ML_H:
                    h = i
                    if h >= 2:
                        pe.wait_ge(M2["arg"], h - 1)
                    b = (2 + h % 2) * HALF
                    mm(ps[:, b:b + SEQ], select[:, h, :], ge[:, :], start=True, stop=True,
                       skip_group_check=True).then_inc(M2["bc"], 1)
                    if h >= 2:
                        pe.wait_ge(M2["w"], h - 1)
                    b = (h % 2) * HALF
                    kk, qq = qkT[:, h, 1, :], qkT[:, h, 0, :]
                    mm(ps[:, b:b + SEQ], kk[:, 0:P], qq, start=True, stop=True, skip_group_check=True)
                    mm(ps[:, b + SEQ:b + SEQ + P], kk[:, P:SEQ], qq[:, P:SEQ], start=True, stop=True,
                       skip_group_check=True).then_inc(M2["st"], 1)
                if i >= 1:
                    h = i - 1
                    pe.wait_ge(M2["w"], h + 1)
                    d = decay[:, h % 2, :]
                    for tok in range(TOK):
                        u = 2 * h + tok
                        if u >= 4:
                            pe.wait_ge(M2["h"], u - 3)
                        elif u >= 2:
                            pe.wait_ge(M2["prepc"], 1)
                        b = (4 + u % 4) * HALF
                        parts = [(d[:, 0:P], 0)] if tok == 0 else [(d[:, P:SEQ], 0), (d[:, SEQ:SEQ + P], 1)]
                        for n, (w, s) in enumerate(parts):
                            ins = mm(ps[:, b:b + ML_V + 1], w, mv[:, s, h, :], start=(n == 0),
                                     stop=(n == len(parts) - 1), skip_group_check=True)
                        ins.then_inc(M2["pv"], 1)
            for h in range(ML_H):
                pe.wait_ge(M2["y"], 2 * h + 2)
                for half in range(2):
                    for tok in range(TOK):
                        o = h * HALF + half * SEQ + tok * P
                        c0 = h * ML_V + half * P
                        ins = nc.tensor.transpose(ps[:, o:o + P], oz[:, tok, c0:c0 + P], ident[:, :])
                ins.then_inc(M2["yT"], 1)
            pe.wait_ge(M2["lo"], 8)
            token_major("lo0", B_LO, 16, XH, XL, lambda k: (M2["lo"], k + 1))
            token_major("lo1", B_LO + 16, 16, XH, XL)

            def ada_columns(name, units):
                g = start(name)
                pe.wait_ge(ada_used, 16 * units)
                for vec in range(2):
                    for k in range(KD):
                        o = g + 16 * vec + k
                        ins = mm(ps[:, o:o + 1], acc_s[:, vec, k * P:(k + 1) * P], ones[:, 0:1], start=True, stop=True,
                                 skip_group_check=True)
                done(ins)

            def ada_row(name, units):
                g = start(name)
                pe.wait_ge(ada_used, 16 * units)
                for n in range(4):
                    ins = mm(ps[:, g + n * HALF:g + (n + 1) * HALF], ones[:, :], acc_g[:, n * HALF:(n + 1) * HALF],
                             start=True, stop=True, skip_group_check=True)
                done(ins)

            pe.wait_ge(ev("toep_r"), 1)
            pe.wait_ge(ev("rel_parts"), 1)
            for name, kc0, kc1 in (("biasa", 0, 40), ("biasb", 40, GRID_W)):
                g = start(name)
                for kc in range(kc0, kc1):
                    o = g + (kc - kc0) // 10 * HALF + (kc - kc0) % 10 * N_A * REL_R
                    c0 = GRID_W - 1 - kc
                    ins = mm(ps[:, o:o + N_A * REL_R], toep_r[:, c0:c0 + P],
                             rel_parts[:, :, :].rearrange(flat), start=True, stop=True, skip_group_check=True)
                done(ins)
            ada_columns("ada1", 8)
            ada_row("g1", 12)
            pe.wait_ge(ev("h_normed"), 2)
            transposes("hTa", operand_tiles(h_norm, 0))
            transposes("hTb", operand_tiles(h_norm, 8))
            token_major("qa", B_QA, 16, XH, XL, lambda k: (tile_split, SPLIT_BASE["hTa"] + k // 2 + 1))
            token_major("kva", B_KVA, 8, XH, XL, per_block=2)
            feature_major("qb", B_QB, 16, XH, XL)
            feature_major("kb", B_KB, 16, XH, XL)
            token_major("vb", B_VB, 16, XH, XL)
            pe.wait_ge(ev("qk_roped"), 4)
            transposes("qaT", [(h * SEQ + tok * P, qa_tok[:, tok, h, :]) for h in range(N_A) for tok in range(TOK)])
            transposes("kaT", [(h * SEQ + tok * P, kva_tok[:, tok, h, :]) for h in range(N_KV) for tok in range(TOK)])
            pe.wait_ge(freed_sem["act"], FREED["kaT"][1])

            def blk_operands(u):
                h, blk = (u % 16) // 2, u % 2
                t = slice(blk * P, (blk + 1) * P)
                if u < 16:
                    return [(qaT[:, h, t], kaT[:, h // (N_A // N_KV), :])]
                return [(qbT[:, h, t], kbT[:, h, :])]

            def blk_values(u, t):
                h = (u % 16) // 2
                return kva_tok[:, t, N_KV + h // (N_A // N_KV), :] if u < 16 else vb_tok[:, t, h * HD:(h + 1) * HD]

            attention(A3, 32, prob2, probT2, y_tok2, lambda u: SEQ, blk_operands, blk_values)
            pe.wait_ge(A3["lo"], 16)
            for n, name in enumerate(("ga0", "ga1", "gb0", "gb1")):
                token_major(name, B_MERGE + 16 * n, 16, XH, XL)
            for n, name in enumerate(("oa0", "ob0", "oa1", "ob1")):
                token_major(name, B_MERGE + 64 + 8 * n, 8, *((yaH, yaL) if n % 2 == 0 else (ybH, ybL)))
            pe.wait_ge(ev("merged"), 2)
            transposes("mTa", operand_tiles(merged, 0))
            m_tiles = lambda k: (tile_split, SPLIT_BASE["mTa"] + k // 2 + 1)
            token_major("wo0", B_WO, 16, XH, XL, m_tiles, blocks=(0, 5))
            pe.wait_ge(ev("merged"), 4)
            transposes("mTb", operand_tiles(merged, 8))
            token_major("wo0", B_WO, 16, XH, XL, m_tiles, blocks=(5, 16))
            token_major("wo1", B_WO + 16, 16, XH, XL)
            ada_columns("ada2", 20)
            pe.wait_ge(ev("h_normed"), 4)
            transposes("h2Ta", operand_tiles(h_norm, 0))
            transposes("h2Tb", operand_tiles(h_norm, 8))

            def ffn_pass(p, parity, freed=None, tiles=None):
                g = ((GROUP["ffn0"] + parity) % 2) * 4 * HALF
                if freed is None:
                    pe.wait_ge(product_done, p - 1)
                else:
                    pe.wait_ge(tile_split, freed)

                def four(kg, static):
                    for j in range(RING):
                        pe.wait_ge(lo_ready, 16 * p + (RING * kg + (B_FFN + j + 1)))
                        if tiles is not None:
                            pe.wait_ge(tile_split, 2 * kg + (tiles + j // 2 + 1))
                        if static:
                            feature_block(g, j, j, lambda k: XH[:, k, :], lambda k: XL[:, k, :], j == 0, False)
                        else:
                            feature_block(g, RING * kg + j, j, lambda k: XH[:, bass.ds(k, 1), :].rearrange(flat),
                                          lambda k: XL[:, bass.ds(k, 1), :].rearrange(flat), False, True)
                four(0, True)
                with pe.Fori(1, KD // RING) as kg:
                    four(kg, False)

            base = SPLIT_BASE["h2Ta"]
            ffn_pass(0, 0, base + 4, base)
            ffn_pass(1, 1, base + 8)
            ffn_pass(2, 0)
            with pe.Fori(1, (FFN_PASSES - 1) // 2) as i:
                for s in range(2):
                    ffn_pass(2 * i + (1 + s), 1 - s)
            ada_row("g2", 24)
            token_major("down0", B_DOWN, KF, FH, FL, lambda k: (ev("ffn_lo"), k // 4 + 1))
            token_major("down1", B_DOWN + KF, KF, FH, FL)


def shape_constants():
    c = np.zeros((P, N_CONST), np.float32)

    def put(name, value, rows=P):
        o, n = CONST[name]
        c[:rows, o:o + n] = np.asarray(value, np.float32).reshape(rows, n)

    put("ident", np.eye(P))
    put("inv_freq", np.tile(10000.0 ** (-np.arange(0, ROPE, 2) / ROPE), (P, 1)))
    p, t = np.arange(P)[:, None], np.arange(SEQ)[None]
    put("causal", np.where(p <= t, 0.0, NEG))
    qc, kc = (np.arange(P) % GRID_W)[:, None], np.arange(GRID_W)[None]
    start = np.clip(qc - NA_COLS // 2, 0, GRID_W - NA_COLS)
    put("window", np.where((kc >= start) & (kc < start + NA_COLS), 0.0, NEG))
    toep = np.zeros((64, 191))
    for half in range(2):
        for j in range(REL_C):
            toep[32 * half + j, GRID_W * half + 78 - j] = 1.0
    put("toeplitz", np.tile(toep, (2, 1)))
    inv = (np.float32(10000.0) ** (-np.arange(0, HD // 2, 2, dtype=np.float32) / (HD // 2))).astype(np.float32)
    tok = np.arange(SEQ)
    ang = np.concatenate([(tok // GRID_W).astype(np.float32)[:, None] * inv,
                          (tok % GRID_W).astype(np.float32)[:, None] * inv], axis=1).astype(np.float64)
    for name, f in (("cos", np.cos), ("sin", np.sin)):
        put(name, f(ang).reshape(TOK, P, HD // 2).transpose(1, 0, 2))
    put("select", np.repeat(np.eye(8), P, axis=1), 8)
    return c


_OUTS = [((1, SEQ, D), "float32")]


def kernel(**inputs):
    import concourse.bacc as _bacc
    from concourse.bass_utils import run_bass_kernel_spmd as _run

    i = {n: np.asarray(a) for n, a in inputs.items()}

    def cols(a):
        return a.reshape(-1, P).T

    pack = {"q_norm": cols(i["mla_q_norm"][0]), "kv_norm": cols(i["mla_kv_norm"][0]), "ln_w0": cols(i["ln_w"][0]),
            "ln_b0": cols(i["ln_b"][0]), "head_norm": cols(i["ml_head_norm"][0]), "conv_w": cols(i["ml_conv_w"][0]),
            "conv_b": cols(i["ml_conv_b"][0]), "norm1": cols(i["norm1_w_2"][0]), "norm2": cols(i["norm2_w_2"][0]),
            "c": cols(i["c_2"][0])}
    args = {
        "positions": i["positions"].reshape(TOK, P).T, "x": i["x"], "xT": i["x"][0].T,
        "pack": np.concatenate([pack[n] for n in PACK], axis=1), "const": shape_constants(),
        "gate_b": i["ml_gate_b"].reshape(2 * ML_H, 1),
        "qk_norm": np.concatenate([i["q_norm_w_2"], i["k_norm_w_2"]], axis=0),
        "rpbT": i["nat_rpb_2"][0].transpose(2, 0, 1),
        "mla_w_in": i["mla_w_in"], "mla_w_qb": i["mla_w_qb"], "mla_w_kvb": i["mla_w_kvb"], "mla_w_out": i["mla_w_out"],
        "ml_w_in": i["ml_w_in"], "ml_w_out": i["ml_w_out"], "ln_w": i["ln_w"], "ln_b": i["ln_b"],
        "w_ada": i["w_ada_2"], "b_ada": i["b_ada_2"], "w_in": i["w_in_2"], "w_oa": i["w_oa_2"], "w_ob": i["w_ob_2"],
        "w_out": i["w_out_2"], "w_gate": i["w_ffn_gate_2"], "w_up": i["w_ffn_up_2"], "w_down": i["w_ffn_down_2"],
        "final_w": i["final_w_2"].reshape(1, D),
    }
    nc = _bacc.Bacc("TRN2", target_bir_lowering=False, num_devices=1)
    arrays, aps = {}, []
    for name, a in args.items():
        a = np.ascontiguousarray(a)
        arrays[f"in_{name}_dram"] = a
        aps.append(nc.dram_tensor(f"in_{name}_dram", a.shape, mybir.dt.from_np(a.dtype), kind="ExternalInput").ap())
    for n, (shape, dtype) in enumerate(_OUTS):
        aps.append(nc.dram_tensor(f"out_{n}_dram", shape, mybir.dt.from_np(np.dtype(dtype)),
                                  kind="ExternalOutput").ap())
    two_block_kernel(nc, *aps)
    r = _run(nc, [arrays], core_ids=[0])
    return r.results[0]["out_0_dram"]
```

```python
from contextlib import ExitStack

import concourse.bass as bass
from concourse import mybir
import numpy as np

ALU = mybir.AluOpType
ACT = mybir.ActivationFunctionType
AX_X = mybir.AxisListType.X
F32 = mybir.dt.float32
F32R = mybir.dt.float32r
I32 = mybir.dt.int32

P = 128
SEQ = 256
TOK = SEQ // P
D = 2048
KD = D // P
COLS = 1024
HALF = 512
RING = 4
EPS = 1e-6
NEG = -3.0e38

MLA_H, NOPE, ROPE, LORA = 16, 128, 64, 512
MLA_SCALE = float(NOPE + ROPE) ** -0.5
ALPHA = 4.0 ** 0.25
ML_H, ML_QK, ML_V = 8, 128, 256
ML_SCALE = float(ML_QK) ** -0.5
TAPS = 4
N_A, N_KV, HD = 8, 2, 128
GRID_W, NA_COLS, REL_R, REL_C = 64, 16, 6, 31
HD_SCALE = float(HD) ** -0.5
D_FF = 5632
KF = D_FF // P
FFN_PASSES = D_FF // HALF

PACK = {}
for _name, _n in (("q_norm", 4), ("kv_norm", 4), ("ln_w0", 16), ("ln_b0", 16), ("head_norm", 16), ("conv_w", 64),
                  ("conv_b", 16), ("norm1", 16), ("norm2", 16), ("c", 16)):
    PACK[_name] = (sum(n for _, n in PACK.values()), _n)
N_PACK = sum(n for _, n in PACK.values())
CONST = {}
for _name, _n in (("ident", 128), ("inv_freq", 32), ("causal", 256), ("window", 64), ("toeplitz", 191),
                  ("cos", 128), ("sin", 128), ("select", 1024)):
    CONST[_name] = (sum(n for _, n in CONST.values()), _n)
N_CONST = sum(n for _, n in CONST.values())

B_C = 0
B_Z = B_C + 16
B_QN = B_Z + 32
B_QR = B_QN + 8
B_KN = B_QR + 4
B_V = B_KN + 8
B_MO = B_V + 8
B_CONV = B_MO + 32
B_VOZ = B_CONV + 32
B_LO = B_VOZ + 96
B_QA = B_LO + 32
B_KVA = B_QA + 16
B_QB = B_KVA + 8
B_KB = B_QB + 16
B_VB = B_KB + 16
B_MERGE = B_VB + 16
B_WO = B_MERGE + 96
B_FFN = B_WO + 32
B_DOWN = B_FFN + 16 * FFN_PASSES

TURN_PLAN = (
    "c:dve z0:act kr:act krt@0:act z1@1:act cT:split8 krT:act qn0@1:act qn1:act qr:act kn0:dve kn1:act qrT:dve "
    "v0:act v1:act mo0@1:dve mo1:dve "
    "x1Ta@1:split4 x1Tb:split4 mlq:taps8 mlk:taps8 mv0:act gates:dve mv1:act mo_0:act mo_1:act mz0:act mz1@0:act "
    "yTa:split8 lo0:dve yTb:split8 lo1@1:dve "
    "biasa:act biasb:act ada1:dve hTa@1:split4 hTb:split4 qa:act kva:act qb:act kb:act vb:act g1:act qaT:act kaT:act "
    "ga0@0:act ga1:act gb0:act gb1:act oa0:dve ob0:dve oa1:dve ob1:dve mTa:split4 wo0:dve mTb:split4 wo1@0:dve "
    "g2:act ada2:dve h2Ta:split4 h2Tb:split4").split() \
    + [f"ffn{i}:product1" for i in range(FFN_PASSES)] + ["down0:dve", "down1:dve"]
GROUP = {}
LAST_IN_GROUP = {}
FREED = {}
SPLIT_BASE = {}
_total = {"act": 0, "dve": 0, "split": 0, "taps": 0, "product": 0}
_group, _last = 1, {0: None, 1: None}
for _entry in TURN_PLAN:
    _name, _who = _entry.split(":")
    _name, _, _at = _name.partition("@")
    _group = int(_at) if _at else 1 - _group
    GROUP[_name], LAST_IN_GROUP[_name] = _group, _last[_group]
    _last[_group] = _name
    _kind = _who.rstrip("0123456789")
    SPLIT_BASE[_name] = _total[_kind]
    _total[_kind] += int(_who[len(_kind):] or 1)
    FREED[_name] = (_kind, _total[_kind])

LAST_BLOCK = {"c": B_Z, "z0": B_Z + 16, "z1": B_QN, "qn0": B_QN + 4, "qn1": B_QR, "qr": B_KN, "kn0": B_KN + 4,
              "kn1": B_V, "v0": B_V + 4, "v1": B_MO, "mo0": B_MO + 16, "mo1": B_CONV, "mlq": B_CONV + 16,
              "mlk": B_VOZ, "lo0": B_LO + 16, "lo1": B_QA, "qa": B_KVA, "kva": B_QB, "qb": B_KB, "kb": B_VB,
              "vb": B_MERGE, "wo0": B_WO + 16, "wo1": B_FFN, "down0": B_DOWN + KF, "down1": B_DOWN + 2 * KF}
for _n, _name in enumerate(("mv0", "mv1", "mo_0", "mo_1", "mz0", "mz1")):
    LAST_BLOCK[_name] = B_VOZ + 16 * (_n + 1)
for _name, _end in (("ga0", 16), ("ga1", 32), ("gb0", 48), ("gb1", 64), ("oa0", 72), ("ob0", 80), ("oa1", 88),
                    ("ob1", 96)):
    LAST_BLOCK[_name] = B_MERGE + _end
for _p in range(FFN_PASSES):
    LAST_BLOCK[f"ffn{_p}"] = B_FFN + 16 * (_p + 1)
BANKS_BEFORE = {_name: 4 * _n for _n, _name in enumerate(
    ("cT", "x1Ta", "x1Tb", "yTa", "yTb", "hTa", "hTb", "mTa", "mTb", "h2Ta", "h2Tb"))}
TURN_COUNT = {}
for _name in GROUP:
    if _name not in LAST_BLOCK and _name not in BANKS_BEFORE:
        TURN_COUNT[_name] = len(TURN_COUNT) + 1

ADA_BESIDE = {"z0": 16, "z1": 16, "mo0": 16, "mo1": 16, "mlq": 14, "mlk": 14, "mv0": 16, "mv1": 16, "mo_0": 20,
              "mo_1": 20, "mz0": 6, "mz1": 6, "lo0": 16,
              "qa": 16, "kb": 8, "vb": 16, "ga0": 22, "ga1": 22, "gb0": 22, "gb1": 22, "oa0": 6, "ob0": 6, "oa1": 6,
              "ob1": 6, "wo0": 20, "wo1": 20}
ADA_FIRST = {}
for _name, _n in ADA_BESIDE.items():
    ADA_FIRST[_name] = sum(ADA_BESIDE[_m] for _m in ADA_FIRST)
N_UNITS = sum(ADA_BESIDE.values()) // KD


def two_block_kernel(nc, positions, x, xT, pack, const, gate_b, qk_norm, rpbT, mla_w_in, mla_w_qb, mla_w_kvb,
                     mla_w_out, ml_w_in, ml_w_out, ln_w, ln_b, w_ada, b_ada, w_in, w_oa, w_ob, w_out, w_gate, w_up,
                     w_down, final_w, out):
    K = 1024
    BASE = 16512
    with ExitStack() as ctx:
        def at(name, kb, shape, dt=F32):
            return nc.alloc_sbuf_tensor_at(name, shape, dt, offset=BASE + int(kb * K))

        def sem(name):
            return ctx.enter_context(nc.semaphore(name))

        raw = at("raw", 0, [P, RING, COLS])
        hi = at("hi", 16, [P, RING, COLS], F32R)
        lo = at("lo", 32, [P, RING, COLS], F32R)
        XH = at("XH", 48, [P, KD, SEQ], F32R)
        XL = at("XL", 64, [P, KD, SEQ], F32R)
        X = at("X", 80, [P, TOK, D])
        ada_raw = at("ada_raw", 96, [P, RING, HALF])
        acc_g = at("acc_g", 104, [P, D])
        acc_s = at("acc_s", 112, [P, 2, D])
        qT = at("qT", 48, [P, MLA_H, SEQ])
        kT = at("kT", 64, [P, MLA_H, SEQ])
        small_raw = at("small_raw", 128, [P, KD, ROPE])
        small_hi = at("small_hi", 132, [P, KD, ROPE], F32R)
        small_lo = at("small_lo", 136, [P, KD, ROPE], F32R)
        row_w = at("row_w", 128, [P, D])
        row_b = at("row_b", 136, [P, D])
        c_tok = at("c_tok", 144, [P, TOK, 2 * LORA])
        z_tok = at("z_tok", 152, [P, TOK, D])
        xT_raw = at("xT_raw", 168, [P, KD, SEQ])
        v_tok = at("v_tok", 168, [P, TOK, MLA_H * NOPE])
        CH = at("CH", 184, [P, 8, SEQ], F32R)
        CL = at("CL", 192, [P, 8, SEQ], F32R)
        qr_tok = at("qr_tok", 144, [P, TOK, MLA_H, ROPE])
        qrr_tok = at("qrr_tok", 136, [P, TOK, MLA_H, ROPE])
        qrT = at("qrT", 144, [P, MLA_H // 2, SEQ])
        rope_tmp = at("rope_tmp", 128, [P, 2, HALF])
        prob = at("prob", 192.5, [P, 3, SEQ])
        probT = at("probT", 195.5, [P, 2, SEQ])
        y_tok = at("y_tok", 197.5, [P, 4, P])
        nmax = at("nmax", 199.5, [P, 32])
        rsum = at("rsum", 199.625, [P, 32])
        rinv = at("rinv", 199.75, [P, 32])
        qkT = at("qkT", 144, [P, ML_H, 2, SEQ])
        h_tok = at("h_tok", 144, [P, ML_H, TOK, ML_V])
        mv = at("mv", 160, [P, TOK, ML_H, ML_V + 1])
        conv_tmp = at("conv_tmp", 177, [P, 8, SEQ])
        oz = at("oz", 176.5, [P, TOK, D])
        z_tmp = at("z_tmp", 136, [P, TOK, COLS])
        decay = at("decay", 192.5, [P, 2, 384])
        select = at("select", 195.5, [8, ML_H, P])
        h_norm = at("h_norm", 160, [P, TOK, D])
        qa_tok = at("qa_tok", 128, [P, TOK, N_A, HD])
        yaL = at("yaL", 128, [P, N_A, SEQ], F32R)
        g_row = at("g_row", 136, [P, D])
        qaT = at("qaT", 144, [P, N_A, SEQ])
        yaH = at("yaH", 144, [P, N_A, SEQ], F32R)
        qbT = at("qbT", 152, [P, N_A, SEQ])
        ybH = at("ybH", 152, [P, N_A, SEQ], F32R)
        kbT = at("kbT", 160, [P, N_A, SEQ])
        ybL = at("ybL", 160, [P, N_A, SEQ], F32R)
        vb_tok = at("vb_tok", 168, [P, TOK, N_A * HD])
        sig_a = at("sig_a", 168, [P, TOK, D])
        sig_b = at("sig_b", 184, [P, TOK, D])
        kva_tok = at("kva_tok", 176, [P, TOK, 4, HD])
        kaT = at("kaT", 180, [P, N_KV, SEQ])
        na_bias = at("na_bias", 182, [P, GRID_W, N_A, REL_R])
        prob2 = at("prob2", 194, [P, 3, SEQ])
        probT2 = at("probT2", 197, [P, 2, SEQ])
        y_tok2 = at("y_tok2", 199, [P, 4, P])
        merged = sig_a
        FH = at("FH", 112, [P, KF, SEQ], F32R)
        FL = at("FL", 156, [P, KF, SEQ], F32R)
        xsq = at("xsq", 64, [P, 2 * TOK, COLS])
        g2_row = at("g2_row", 96, [P, D])
        final_row = at("final_row", 56, [P, D])
        tmp = at("tmp", 200, [P, COLS])
        ident = at("ident", 204, [P, P])
        ones = at("ones", 204.5, [P, P])
        pk = at("pk", 205, [P, N_PACK])
        c_act = at("c_act", 206, [P, 16])
        mods = at("mods", 206.0625, [P, 2, 16])
        A_col = at("A_col", 206.1875, [P, 16])
        st = at("st", 206.25, [P, TOK, 4, 6])
        mvar = at("mvar", 206.4375, [P, TOK, 2])
        ss = at("ss", 206.46875, [P, 32])
        ra = at("ra", 206.59375, [P, 32])
        ry = at("ry", 206.71875, [P, 32])
        rt = at("rt", 206.84375, [P, 32])
        shift_col = at("shift_col", 207.34375, [P, 1])
        nmax2 = at("nmax2", 206.96875, [P, 32])
        rsum2 = at("rsum2", 207.09375, [P, 32])
        rinv2 = at("rinv2", 207.21875, [P, 32])
        kr_tok = at("kr_tok", 104, [P, TOK, ROPE])
        krf = at("krf", 106.5, [ROPE, SEQ])
        krr_tok = at("krr_tok", 104.5, [P, TOK, 2, ROPE])
        krT = at("krT", 105.5, [P, SEQ])
        ang = at("ang", 107.5, [P, TOK, 32])
        rot = at("rot", 107.75, [P, TOK, 32])
        turns_n = at("turns_n", 108, [P, TOK, 32])
        cos_t = at("cos_t", 108.25, [P, TOK, 32])
        sin_t = at("sin_t", 108.5, [P, TOK, 32])
        pos_i = at("pos_i", 108.75, [P, TOK], I32)
        pos_f = at("pos_f", 108.78125, [P, TOK])
        inv_freq = at("inv_freq", 108.8125, [P, 32])
        gate_bias = at("gate_bias", 128.25, [64, 1])
        gi = at("gi", 129, [8, SEQ])
        gf = at("gf", 130, [8, SEQ])
        ge = at("ge", 131, [8, SEQ])
        gF = at("gF", 132, [8, SEQ])
        gM = at("gM", 133, [8, SEQ])
        causal = at("causal", 134, [P, SEQ])
        G_col = at("G_col", 135, [P, TOK, ML_H])
        E_col = at("E_col", 135.0625, [P, TOK, ML_H])
        dens = at("dens", 135.125, [P, 16])
        dinv = at("dinv", 135.1875, [P, 16])
        cos2 = at("cos2", 144, [P, TOK, HD // 2])
        sin2 = at("sin2", 144.5, [P, TOK, HD // 2])
        qkn = at("qkn", 145, [P, 2, HD])
        window = at("window", 195.25, [P, GRID_W])
        toep = at("toep", 194, [P, 191])
        toep_r = at("toep_r", 195.5, [P, 191], F32R)
        rel = at("rel", 195, [P, N_A, REL_R])
        rel_parts = at("rel_parts", 196.5, [P, N_A, REL_R], F32R)
        rope2 = at("rope2", 146, [P, 2, HALF])

        ps = ctx.enter_context(nc.psum_tensor("ps", [P, 8 * HALF], F32))

        w_landed = [sem(f"w_landed{i}") for i in range(RING)]
        hi_ready, lo_ready = sem("hi_ready"), sem("lo_ready")
        block_done = sem("block_done")
        tiles_turned = sem("tiles_turned")
        turn_done = sem("turn_done")
        tile_split = sem("tile_split")
        taps_done = sem("taps_done")
        product_done = sem("product_done")
        freed_sem = {"act": sem("act_freed"), "dve": sem("dve_freed"), "split": tile_split, "taps": taps_done,
                     "product": product_done}
        ada_landed = [sem(f"ada_landed{i}") for i in range(RING)]
        ada_used = sem("ada_used")
        acc_zero = sem("acc_zero")
        bias_landed = [sem(f"bias_landed{i}") for i in range(4)]
        s_dve, s_act = sem("s_dve"), sem("s_act")
        events = {}

        def ev(name):
            if name not in events:
                events[name] = sem("e_" + name)
            return events[name]

        def att_sems(tag):
            return {n: sem(f"{tag}_{n}") for n in ("scored", "maxed", "exped", "turned", "copied", "summed", "scaled",
                                                   "backed", "hi", "lo")}

        A1, A3 = att_sems("mla"), att_sems("blk")

        def bank(S, n):
            return ((n + 4) % 8 if S is A1 else n) * HALF
        M2 = {n: sem(f"ml_{n}") for n in ("prep", "prepc", "st", "bc", "arg", "exp", "w", "pv", "h", "sq", "y",
                                          "hi")}

        def col(name, k):
            o = PACK[name][0] + k
            return pk[:, o:o + 1]

        def complete(name):
            if name in BANKS_BEFORE:
                return tiles_turned, BANKS_BEFORE[name] + 4
            return (block_done, LAST_BLOCK[name]) if name in LAST_BLOCK else (turn_done, TURN_COUNT[name])

        def grp(name):
            return GROUP[name] * 4 * HALF

        def T(name, tok, w=COLS):
            g = grp(name) + tok * 2 * HALF
            return ps[:, g:g + w]

        def landed(n, j):
            two = max(0, min(n + 1, B_DOWN) - B_FFN)
            two = (two + RING - 1 - j) // RING if two > 0 else 0
            return 16 * (n // RING + 1 + two)

        def acc_part(u):
            vec, part = u // 4, (u % 4) * HALF
            if vec in (2, 5):
                return acc_g[:, part:part + HALF], 1 if vec == 2 else 3
            return acc_s[:, vec % 3, part:part + HALF], 0 if vec < 2 else 2

        flat = "p a b -> p (a b)"
        block = ctx.enter_context(nc.Block())

        @block.sync
        def _(sp):
            def rows(w, k):
                return w[bass.ds(k * P, P), :] if not isinstance(k, int) else w[k * P:(k + 1) * P, :]

            def stream(n0, nb, source):
                first = 0
                if n0 == 0:
                    for j in range(RING):
                        dst, src = source(j, j)
                        sp.dma_start(dst, src).then_inc(w_landed[j], 16)
                    for q in range(1, 4):
                        load_x(q)
                    first = 1
                with sp.Fori(first, nb // RING) as g:
                    for j in range(RING):
                        dst, src = source(RING * g + j, j)
                        sp.wait_ge(lo_ready, n0 + RING * g + j - RING + 1)
                        sp.dma_start(dst, src).then_inc(w_landed[j], 16)

            def plain(w, c0):
                return lambda k, j: (raw[:, j, :], rows(w, k)[:, c0:c0 + COLS])

            def head_cols(w, per, h0, nh, off, width):
                def source(k, j):
                    src = rows(w, k).rearrange("p (h e) -> p h e", e=per)[:, h0:h0 + nh, off:off + width]
                    return raw[:, j, :].rearrange("p (h e) -> p h e", e=width), src
                return source

            xT_v = xT.rearrange("(k p) t -> p k t", p=P)

            def load_x(q):
                sp.dma_start(xT_raw[:, 4 * q:4 * q + 4, :], xT_v[:, 4 * q:4 * q + 4, :]).then_inc(ev(f"xT{q}"), 16)

            load_x(0)
            w = mla_w_in[0]
            stream(B_C, 16, plain(w, 0))
            for q in range(2):
                stream(B_Z + 16 * q, 16, plain(w, 2 * LORA + ROPE + q * COLS))
            for q in range(2):
                stream(B_QN + 4 * q, 4, head_cols(mla_w_qb[0], NOPE + ROPE, 8 * q, 8, 0, NOPE))
            stream(B_QR, 4, head_cols(mla_w_qb[0], NOPE + ROPE, 0, 16, NOPE, ROPE))
            for q in range(2):
                stream(B_KN + 4 * q, 4, head_cols(mla_w_kvb[0], 2 * NOPE, 8 * q, 8, 0, NOPE))
            for q in range(2):
                stream(B_V + 4 * q, 4, head_cols(mla_w_kvb[0], 2 * NOPE, 8 * q, 8, NOPE, NOPE))
            for q in range(2):
                stream(B_MO + 16 * q, 16, plain(mla_w_out[0], q * COLS))
            for q in range(6):
                stream(B_CONV + 16 * q, 16, plain(ml_w_in[0], q * COLS))
            for q in range(2):
                stream(B_VOZ + 64 + 16 * q, 16, plain(ml_w_in[0], 6160 + q * COLS))
            for q in range(2):
                stream(B_LO + 16 * q, 16, plain(ml_w_out[0], q * COLS))
            w = w_in[0]
            stream(B_QA, 16, plain(w, 0))
            pairs = w.rearrange("(b a p) n -> b p a n", a=2, p=P)

            def two_rows(k, j):
                src = pairs[k] if isinstance(k, int) \
                    else pairs[bass.ds(k, 1), :, :, :].rearrange("b p a n -> (b p) a n")
                return raw[:, j, :].rearrange("p (a n) -> p a n", a=2), src[:, :, COLS:COLS + HALF]

            stream(B_KVA, 8, two_rows)
            for q in range(3):
                stream(B_QB + 16 * q, 16, plain(w, 1536 + q * COLS))
            for n, c0 in enumerate((4608, 4608 + COLS, 6656, 6656 + COLS)):
                stream(B_MERGE + 16 * n, 16, plain(w, c0))
            for q in range(2):
                stream(B_MERGE + 64 + 16 * q, 8, plain(w_oa[0], q * COLS))
                stream(B_MERGE + 72 + 16 * q, 8, plain(w_ob[0], q * COLS))
            for q in range(2):
                stream(B_WO + 16 * q, 16, plain(w_out[0], q * COLS))
            with sp.Fori(0, FFN_PASSES) as q:
                with sp.Fori(0, KD // RING) as g:
                    for j in range(RING):
                        for part, mat in enumerate((w_gate[0], w_up[0])):
                            sp.wait_ge(lo_ready, 16 * q + (RING * g + (B_FFN + j - RING + 1)))
                            sp.dma_start(raw[:, j, part * HALF:(part + 1) * HALF],
                                         mat[bass.ds((RING * g + j) * P, P), bass.ds(q * HALF, HALF)]) \
                              .then_inc(w_landed[j], 16)
            for q in range(2):
                stream(B_DOWN + KF * q, KF, plain(w_down[0], q * COLS))
            for tok in range(TOK):
                for q in range(2):
                    sp.wait_ge(ev(f"result{q}"), tok + 1)
                    sp.dma_start(out[0, tok * P:(tok + 1) * P, q * COLS:(q + 1) * COLS],
                                 X[:, tok, q * COLS:(q + 1) * COLS]).then_inc(ev("stored"), 16)
            sp.wait_ge(ev("stored"), 64)

        @block.gpsimd
        def _(pool):
            def load(name, dst, src):
                pool.dma_start(dst, src).then_inc(ev(name), 16)

            def cst(name, p0=0, p1=P):
                o, n = CONST[name]
                return const[p0:p1, o:o + n]

            def bcast(dst, row):
                return dst, row.partition_broadcast(P)

            def ada_units(u0, u1):
                def four(u, g, wait):
                    for j in range(RING):
                        if wait:
                            pool.wait_ge(ada_used, 16 * u + (RING * g + (j - RING + 1)))
                        pool.dma_start(ada_raw[:, j, :],
                                       w_ada[0][bass.ds((RING * g + j) * P, P), bass.ds(u * HALF, HALF)]) \
                            .then_inc(ada_landed[j], 16)
                if u0 == 0:
                    four(0, 0, False)
                    with pool.Fori(1, KD // RING) as g:
                        four(0, g, True)
                    u0 = 1
                with pool.Fori(u0, u1) as u:
                    with pool.Fori(0, KD // RING) as g:
                        four(u, g, True)

            def init_acc(i, acc, b0, n, zeroed):
                nc.gpsimd.memset(acc, 0.0).then_inc(acc_zero, 1)
                pool.wait_ge(acc_zero, zeroed)
                pool.dma_start(acc[0:1, :], b_ada[0:1, b0:b0 + n]).then_inc(bias_landed[i], 16)

            load("pack", pk[:, :], pack)
            load("ident", ident[:, :], cst("ident"))
            load("pos", pos_i[:, :], positions)
            load("inv_freq", inv_freq[:, :], cst("inv_freq"))
            init_acc(0, acc_s[:, :, :].rearrange(flat), 0, 2 * D, 1)
            pool.wait_ge(block_done, 8)
            load("small1", small_raw[:, :, :],
                 mla_w_in[0][:, 2 * LORA:2 * LORA + ROPE].rearrange("(k p) n -> p k n", p=P))
            load("x", X[:, :, :], x[0].rearrange("(a p) n -> p a n", p=P))
            ada_units(0, 4)
            pool.wait_ge(ev("q_roped"), 2)
            pool.wait_ge(*complete("qrT"))
            load("rows0", *bcast(row_w[:, :], ln_w[0:1, :]))
            load("rows0", *bcast(row_b[:, :], ln_b[0:1, :]))
            ada_units(4, 5)
            pool.wait_ge(ev("x1_rows"), 4)
            nc.gpsimd.memset(small_raw[:, :, 0:40], 0.0).then_inc(ev("small_zero"), 1)
            pool.wait_ge(ev("small_zero"), 1)
            for half in range(2):
                load("small2", small_raw[:, :, 32 * half:32 * half + 8],
                     ml_w_in[0][:, 6144 + 8 * half:6152 + 8 * half].rearrange("(k p) n -> p k n", p=P))
            init_acc(1, acc_g[:, :], 2 * D, D, 2)
            ada_units(5, 7)
            pool.wait_ge(*complete("gates"))
            for half in range(2):
                load("gate_bias", gate_bias[32 * half:32 * half + 8, :], gate_b[8 * half:8 * half + 8, :])
            load("causal", causal[:, :], cst("causal"))
            load("select", select[:, :, :].rearrange(flat), cst("select", 0, 8))
            ada_units(7, 12)
            pool.wait_ge(tile_split, SPLIT_BASE["yTb"] + 8)
            load("rows1", *bcast(row_w[:, :], ln_w[1:2, :]))
            load("rows1", *bcast(row_b[:, :], ln_b[1:2, :]))
            load("tables2", cos2[:, :, :].rearrange(flat), cst("cos"))
            load("tables2", sin2[:, :, :].rearrange(flat), cst("sin"))
            load("tables2", qkn[:, 0, :], qk_norm[0:1, :].partition_broadcast(P))
            load("tables2", qkn[:, 1, :], qk_norm[1:2, :].partition_broadcast(P))
            load("toep", toep[:, :], cst("toeplitz"))
            load("window", window[:, :], cst("window"))
            nc.gpsimd.memset(rel[:, :, :], 0.0).then_inc(ev("rel_zero"), 1)
            pool.wait_ge(ev("rel_zero"), 1)
            for part in range(2):
                load("rel", rel[64 * part:64 * part + 31, :, :], rpbT[:, :, 5:11])
                load("rel", rel[64 * part + 32:64 * part + 63, :, :], rpbT[:, :, 4:10])
            pool.wait_ge(*complete("ada1"))
            init_acc(2, acc_s[:, :, :].rearrange(flat), 3 * D, 2 * D, 3)
            ada_units(12, 15)
            pool.wait_ge(*complete("g1"))
            init_acc(3, acc_g[:, :], 5 * D, D, 4)
            ada_units(15, N_UNITS)
            pool.wait_ge(*complete("ffn10"))
            load("final_row", *bcast(final_row[:, :], final_w))

        @block.scalar
        def _(act):
            own = [0]

            def link(ins):
                own[0] += 1
                ins.then_inc(s_act, 1)
                act.wait_ge(s_act, own[0])

            def hi_block(n, j, count):
                act.wait_ge(w_landed[j], count)
                if not isinstance(n, int) or n >= RING:
                    act.wait_ge(block_done, n - RING + 1)
                nc.scalar.copy(hi[:, j, :], raw[:, j, :]).then_inc(hi_ready, 1)

            def first4(n0):
                for j in range(RING):
                    hi_block(n0 + j, j, landed(n0 + j, j))

            def first3(n0):
                for j in range(RING - 1):
                    hi_block(n0 + j, j, landed(n0 + j, j))

            def fourth(n0):
                hi_block(n0 + 3, 3, landed(n0 + 3, 3))

            def rest(n0, nb, g0=1):
                c0 = landed(n0, 0)
                with act.Fori(g0, nb // RING) as g:
                    for j in range(RING):
                        hi_block(RING * g + (n0 + j), j, 16 * g + c0)

            def rest_blocks(n0, b0, b1, before=lambda b: None):
                for b in range(b0, b1):
                    before(b)
                    hi_block(n0 + b, b % RING, landed(n0 + b, b % RING))

            def turn(name):
                act.wait_ge(*complete(name))
                return grp(name)

            def bank_turned(name, n):
                act.wait_ge(tiles_turned, BANKS_BEFORE[name] + n + 1)

            def each_tok(name, dst, func=None, scale=1.0, width=COLS, src=lambda ap: ap):
                turn(name)
                for tok in range(TOK):
                    if func is not None:
                        ins = nc.scalar.activation(dst(tok), src(T(name, tok, width)), func)
                    elif scale != 1.0:
                        ins = nc.scalar.mul(dst(tok), src(T(name, tok, width)), scale)
                    else:
                        ins = nc.scalar.copy(dst(tok), src(T(name, tok, width)))
                ins.then_inc(freed_sem["act"], 1)

            def whole(name, dst, scale=1.0, width=4 * HALF):
                g = turn(name)
                src = ps[:, g:g + width]
                (nc.scalar.mul(dst, src, scale) if scale != 1.0 else nc.scalar.copy(dst, src)) \
                    .then_inc(freed_sem["act"], 1)

            def operand_full(names, event, gain, shift):
                for n, name in enumerate(names):
                    g = grp(name)
                    for k in range(8):
                        kk = 8 * n + k
                        if k % 2 == 0:
                            bank_turned(name, k // 2)
                        if kk >= 4 and kk % 2 == 0:
                            act.wait_ge(tile_split, SPLIT_BASE[names[0]] + kk // 2 - 1)
                        ins = nc.scalar.activation(tmp[:, (kk % 4) * SEQ:(kk % 4 + 1) * SEQ],
                                                   ps[:, g + k * SEQ:g + (k + 1) * SEQ], ACT.Identity,
                                                   scale=gain(kk), bias=shift(kk))
                        if kk % 2:
                            ins.then_inc(ev(event), 1)

            def half_squares(q, event, scratch):
                for tok in range(TOK):
                    act.wait_ge(ev(event), 2 * q + tok + 1)
                    nc.scalar.activation(scratch(tok, q), X[:, tok, q * COLS:(q + 1) * COLS], ACT.Square,
                                         accum_out=ss[:, 2 * q + tok:2 * q + tok + 1]).then_inc(ev("x_squares"), 1)

            def rms_tile(n, squares):
                act.wait_ge(ev("x_squares"), squares)
                act.wait_ge(ev("rms"), n)
                nc.scalar.mul(h_norm[:, 1, :], X[:, 1, :], ry[:, 1:2]).then_inc(ev("h_normed"), 1)

            def attention(S, units, pr, prT, nm, rs, keys, H):
                for i in range(units + 6):
                    if 2 <= i < units + 2:
                        u = i - 2
                        nk = keys(u)
                        b = bank(S, 3 + u % 2)
                        act.wait_ge(S["turned"], u + 1)
                        if u >= 2:
                            act.wait_ge(S["summed"], u - 1)
                        nc.scalar.copy(prT[:, u % 2, 0:nk], ps[:, b:b + nk]).then_inc(S["copied"], 1)
                    if i < units:
                        u = i
                        nk = keys(u)
                        act.wait_ge(S["maxed"], u + 1)
                        if u >= 3:
                            act.wait_ge(S["turned"], u - 2)
                        nc.scalar.activation(pr[:, u % 3, 0:nk], ps[:, bank(S, u % 3):bank(S, u % 3) + nk], ACT.Exp,
                                             bias=nm[:, u:u + 1], accum_out=rs[:, u:u + 1]).then_inc(S["exped"], 1)
                    if i >= 6 and i % 2 == 0:
                        h = (i - 6) // 2
                        act.wait_ge(S["backed"], h + 1)
                        nc.scalar.copy(H(h), ps[:, bank(S, 7):bank(S, 7) + SEQ]).then_inc(S["hi"], 1)

            for q in range(4):
                act.wait_ge(ev(f"xT{q}"), 16)
                nc.scalar.copy(XH[:, 4 * q:4 * q + 4, :], xT_raw[:, 4 * q:4 * q + 4, :]).then_inc(ev("x_hi"), 1)
                if q == 0:
                    first4(B_C)
            act.wait_ge(ev("pack"), 16)
            nc.scalar.activation(c_act[:, :], pk[:, PACK["c"][0]:PACK["c"][0] + 16], ACT.Silu).then_inc(ev("c_act"), 1)
            rest(B_C, 16)
            first4(B_Z)
            act.wait_ge(ev("angles"), 1)
            nc.scalar.activation(sin_t[:, :, :], rot[:, :, :], ACT.Sin).then_inc(ev("sincos"), 1)
            nc.scalar.activation(cos_t[:, :, :], ang[:, :, :], ACT.Sin).then_inc(ev("sincos"), 1)
            g = turn("c")
            for i in range(4):
                if i >= 2:
                    act.wait_ge(ev("c_squares"), i - 1)
                nc.scalar.activation(tmp[:, (i % 2) * HALF:(i % 2 + 1) * HALF], ps[:, g + i * HALF:g + (i + 1) * HALF],
                                     ACT.Square, accum_out=ss[:, i:i + 1]).then_inc(ev("c_squares"), 1)
            act.wait_ge(ev("small1"), 16)
            nc.scalar.copy(small_hi[:, :, :], small_raw[:, :, :]).then_inc(ev("small_hi"), 1)
            rest(B_Z, 16)
            first4(B_Z + 16)
            each_tok("z0", lambda t: z_tok[:, t, 0:COLS], ACT.Silu)
            act.wait_ge(*complete("kr"))
            nc.scalar.copy(krf[:, :], ps[0:ROPE, grp("kr"):grp("kr") + SEQ]).then_inc(freed_sem["act"], 1)
            each_tok("krt", lambda t: kr_tok[:, t, :], width=ROPE)
            rest(B_Z + 16, 16)
            first3(B_QN)
            each_tok("z1", lambda t: z_tok[:, t, COLS:], ACT.Silu)
            whole("krT", krT[:, :], width=SEQ)
            g = grp("cT")
            for k in range(8):
                if k % 2 == 0:
                    bank_turned("cT", k // 2)
                nc.scalar.mul(CH[:, k, :], ps[:, g + k * SEQ:g + (k + 1) * SEQ],
                              col("q_norm", k) if k < 4 else col("kv_norm", k - 4)).then_inc(ev("c_hi"), 1)
            fourth(B_QN)
            first4(B_QN + 4)
            whole("qn0", qT[:, 0:8, :].rearrange(flat), MLA_SCALE)
            first4(B_QR)
            whole("qn1", qT[:, 8:16, :].rearrange(flat), MLA_SCALE)
            first4(B_KN)
            each_tok("qr", lambda t: qr_tok[:, t].rearrange(flat), None, MLA_SCALE)
            first4(B_KN + 4)
            first4(B_V)
            whole("kn1", kT[:, 8:16, :].rearrange(flat))
            first4(B_V + 4)
            each_tok("v0", lambda t: v_tok[:, t, 0:COLS])
            first3(B_MO)
            each_tok("v1", lambda t: v_tok[:, t, COLS:])
            attention(A1, 32, prob, probT, nmax, rsum, lambda u: P * (1 + u % 2), lambda h: XH[:, h, :])
            fourth(B_MO)
            rest(B_MO, 16)
            first4(B_MO + 16)
            rest(B_MO + 16, 16)
            first4(B_CONV)
            act.wait_ge(ev("shift_col"), 1)
            nc.scalar.activation(X[:, 1, :], X[:, 1, :], ACT.Identity, scale=ry[:, 1:2], bias=shift_col[:, :]) \
              .then_inc(ev("normed"), 1)
            operand_full(("x1Ta", "x1Tb"), "x1_full", lambda k: col("ln_w0", k), lambda k: col("ln_b0", k))
            rest(B_CONV, 16)

            def conv_before(q):
                g = grp(("mlq", "mlk")[q])

                def do(b):
                    for k in range(2 * (b - 4), 2 * (b - 4) + 2) if b < 8 else ():
                        f = 8 * q + k
                        nc.scalar.activation(conv_tmp[:, k, :], ps[:, g + k * SEQ:g + (k + 1) * SEQ], ACT.Identity,
                                             scale=col("conv_w", 3 * 16 + f), bias=col("conv_b", f)) \
                          .then_inc(ev("last_tap"), 1)
                    if 7 <= b < 15:
                        act.wait_ge(taps_done, 8 * q + b - 6)
                        nc.scalar.activation(qkT[:, b - 7, q, :], conv_tmp[:, b - 7, :], ACT.Silu).then_inc(ev("qk"), 1)
                return do

            first4(B_CONV + 16)
            turn("mlq")
            rest_blocks(B_CONV + 16, 4, 16, conv_before(0))
            act.wait_ge(ev("small2"), 32)
            nc.scalar.copy(small_hi[:, :, 0:40], small_raw[:, :, 0:40]).then_inc(ev("small_hi"), 1)
            first4(B_VOZ)
            turn("mlk")
            rest_blocks(B_VOZ, 4, 16, conv_before(1))
            first4(B_VOZ + 16)

            def v_out(name, q):
                each_tok(name, lambda t: mv[:, t, 4 * q:4 * q + 4, 0:ML_V],
                         src=lambda ap: ap.rearrange("p (h e) -> p h e", e=ML_V))

            v_out("mv0", 0)
            act.wait_ge(ev("neg_abs"), 1)
            link(nc.scalar.activation(ge[:, :], ge[:, :], ACT.Exp))
            nc.scalar.activation(ge[:, :], ge[:, :], ACT.Ln, bias=1.0).then_inc(ev("log1p"), 1)
            rest(B_VOZ + 16, 16)
            act.wait_ge(ev("stabiliser"), 1)
            nc.scalar.activation(gF[:, :], gF[:, :], ACT.Exp, scale=-1.0).then_inc(ev("exp_m"), 1)
            first4(B_VOZ + 32)
            v_out("mv1", 1)
            rest(B_VOZ + 32, 16)
            first4(B_VOZ + 48)
            each_tok("mo_0", lambda t: oz[:, t, 0:COLS], ACT.Sigmoid)
            rest(B_VOZ + 48, 16)
            first4(B_VOZ + 64)
            each_tok("mo_1", lambda t: oz[:, t, COLS:], ACT.Sigmoid)

            def heads_before(b):
                if b >= 6 and (b - 6) % 4 == 0:
                    h = (b - 6) // 4
                    act.wait_ge(M2["arg"], h + 1)
                    nc.scalar.activation(decay[:, h % 2, :], decay[:, h % 2, :], ACT.Exp).then_inc(M2["exp"], 1)
                if b >= 9 and (b - 9) % 4 == 0:
                    h = (b - 9) // 4
                    for tok in range(TOK):
                        u = 2 * h + tok
                        act.wait_ge(M2["h"], u + 1)
                        if u >= 4:
                            act.wait_ge(M2["sq"], u - 3)
                        nc.scalar.activation(tmp[:, (u % 4) * ML_V:(u % 4 + 1) * ML_V], h_tok[:, h, tok, :], ACT.Square,
                                             accum_out=ss[:, u:u + 1]).then_inc(M2["sq"], 1)

            rest_blocks(B_VOZ + 64, 4, 19, heads_before)
            each_tok("mz0", lambda t: z_tmp[:, t, :], ACT.Silu)
            rest_blocks(B_VOZ + 64, 19, 35, heads_before)
            act.wait_ge(ev("z_used"), 1)
            each_tok("mz1", lambda t: z_tmp[:, t, :], ACT.Silu)
            for name, k0, b0, b1 in (("yTa", 0, 3, 8), ("yTb", 8, 8, 16)):
                for k in range(8):
                    if k % 2 == 0:
                        bank_turned(name, k // 2)
                    o = grp(name) + k * SEQ
                    nc.scalar.mul(XH[:, k0 + k, :], ps[:, o:o + SEQ], col("head_norm", k0 + k)).then_inc(M2["hi"], 1)
                    if k0 == 0 and k == 3:
                        heads_before(37)
                rest_blocks(B_LO, b0, b1)
            first4(B_LO + 16)
            act.wait_ge(ev("toep"), 16)
            nc.scalar.copy(toep_r[:, :], toep[:, :]).then_inc(ev("toep_r"), 1)
            act.wait_ge(ev("rel"), 64)
            nc.scalar.copy(rel_parts[:, :, :], rel[:, :, :]).then_inc(ev("rel_hi"), 1)
            rest(B_LO + 16, 16)

            first4(B_QA)
            for name, kc0, kc1 in (("biasa", 0, 40), ("biasb", 40, GRID_W)):
                g = turn(name)
                for c0 in range(kc0, kc1, 10):
                    n = min(10, kc1 - c0)
                    o = g + (c0 - kc0) // 10 * HALF
                    ins = nc.scalar.copy(na_bias[:, c0:c0 + n].rearrange("p c h i -> p (c h i)"),
                                         ps[:, o:o + n * N_A * REL_R])
                ins.then_inc(freed_sem["act"], 1)
            for tok in range(TOK):
                act.wait_ge(ev("x2_rows"), tok + 1)
                nc.scalar.activation(h_norm[:, tok, :], X[:, tok, :], ACT.Square, accum_out=ss[:, tok:tok + 1]) \
                  .then_inc(ev("x_squares"), 1)
            rms_tile(1, 2)
            act.wait_ge(freed_sem["dve"], FREED["ada1"][1])
            operand_full(("hTa", "hTb"), "h_full", lambda k: A_col[:, k:k + 1], lambda k: mods[:, 0, k:k + 1])
            rest(B_QA, 16)
            first4(B_KVA)
            each_tok("qa", lambda t: qa_tok[:, t].rearrange(flat))
            rest(B_KVA, 8)
            first4(B_QB)
            each_tok("kva", lambda t: kva_tok[:, t].rearrange(flat), width=HALF)
            rest(B_QB, 16)
            first4(B_KB)
            whole("qb", qbT[:, :, :].rearrange(flat), HD_SCALE)
            rest(B_KB, 16)
            first4(B_VB)
            whole("kb", kbT[:, :, :].rearrange(flat))
            rest(B_VB, 16)
            first3(B_MERGE)
            each_tok("vb", lambda t: vb_tok[:, t, :])
            whole("g1", g_row[:, :])
            whole("qaT", qaT[:, :, :].rearrange(flat), HD_SCALE)
            whole("kaT", kaT[:, :, :].rearrange(flat), width=2 * SEQ)
            attention(A3, 32, prob2, probT2, nmax2, rsum2, lambda u: SEQ,
                      lambda h: yaH[:, h, :] if h < N_A else ybH[:, h - N_A, :])
            fourth(B_MERGE)
            rest(B_MERGE, 16)
            for n, (name, sig) in enumerate((("ga0", sig_a), ("ga1", sig_a), ("gb0", sig_b), ("gb1", sig_b))):
                first4(B_MERGE + 16 * (n + 1))
                c0 = n % 2 * COLS
                each_tok(name, lambda t: sig[:, t, c0:c0 + COLS], ACT.Sigmoid)
                rest(B_MERGE + 16 * (n + 1), 16 if n < 3 else 8)
            for n in range(3):
                first4(B_MERGE + 72 + 8 * n)
                rest(B_MERGE + 72 + 8 * n, 8)
            first4(B_WO)
            for name in ("mTa", "mTb"):
                g = grp(name)
                for k in range(4):
                    k0 = (8 if name == "mTb" else 0) + 2 * k
                    bank_turned(name, k)
                    nc.scalar.copy(XH[:, k0:k0 + 2, :].rearrange(flat), ps[:, g + k * HALF:g + (k + 1) * HALF]) \
                      .then_inc(ev("m_hi"), 1)
                if name == "mTa":
                    rest_blocks(B_WO, 4, 8)
            rest_blocks(B_WO, 8, 16)
            first4(B_WO + 16)
            half_squares(0, "x3", lambda t, q: h_norm[:, t, q * COLS:(q + 1) * COLS])
            rest(B_WO + 16, 16)
            first4(B_FFN)
            whole("g2", g2_row[:, :])
            half_squares(1, "x3", lambda t, q: h_norm[:, t, q * COLS:(q + 1) * COLS])
            rms_tile(2, 6)
            act.wait_ge(freed_sem["dve"], FREED["ada2"][1])
            operand_full(("h2Ta", "h2Tb"), "h2_full", lambda k: A_col[:, k:k + 1], lambda k: mods[:, 0, k:k + 1])

            def ffn_blocks(p, g0, g1):
                def four(g):
                    for j in range(RING):
                        hi_block(16 * p + (RING * g + (B_FFN + j)), j, 128 * p + (32 * g + landed(B_FFN, 0)))
                if g1 - g0 == 1:
                    four(g0)
                else:
                    with act.Fori(g0, g1) as g:
                        four(g)

            def ffn_out(p, parity):
                act.wait_ge(block_done, 16 * p + (B_FFN + 16))
                if not isinstance(p, int) or p > 0:
                    act.wait_ge(ev("ffn_lo"), p)
                g = ((GROUP["ffn0"] + parity) % 2) * 4 * HALF
                nc.scalar.activation(tmp[:, :], ps[:, g:g + COLS], ACT.Silu).then_inc(ev("ffn_silu"), 1)
                act.wait_ge(product_done, p + 1)
                dst = FH[:, 4 * p:4 * p + 4, :] if isinstance(p, int) else FH[:, bass.ds(4 * p, 4), :]
                nc.scalar.copy(dst, tmp[:, :].rearrange("p (k t) -> p k t", k=4)).then_inc(ev("ffn_hi"), 1)

            ffn_blocks(0, 1, 4)
            for s in range(2):
                ffn_blocks(1 + s, 0, 1)
                ffn_out(s, s)
                ffn_blocks(1 + s, 1, 4)
            with act.Fori(1, (FFN_PASSES - 1) // 2) as i:
                for s in range(2):
                    ffn_blocks(2 * i + (1 + s), 0, 1)
                    ffn_out(2 * i + s, s)
                    ffn_blocks(2 * i + (1 + s), 1, 4)
            first4(B_DOWN)
            ffn_out(FFN_PASSES - 1, 0)
            rest(B_DOWN, KF)
            first4(B_DOWN + KF)
            rest_blocks(B_DOWN + KF, 4, 8)
            half_squares(0, "x4", lambda t, q: xsq[:, 2 * t + q, :])
            rest(B_DOWN + KF, KF, g0=2)
            half_squares(1, "x4", lambda t, q: xsq[:, 2 * t + q, :])
            act.wait_ge(ev("rms"), 3)
            act.wait_ge(ev("x4_weighted"), 2)
            for tok in range(TOK):
                nc.scalar.mul(X[:, tok, 0:COLS], X[:, tok, 0:COLS], ry[:, tok:tok + 1]).then_inc(ev("result0"), 1)

        @block.vector
        def _(dve):
            own = [0]

            def mark(ins):
                own[0] += 1
                ins.then_inc(s_dve, 1)
                return own[0]

            def after(n):
                dve.wait_ge(s_dve, n)

            def link(ins):
                after(mark(ins))

            def lo_block(n, j):
                dve.wait_ge(hi_ready, n + 1)
                nc.vector.tensor_tensor(lo[:, j, :], raw[:, j, :], hi[:, j, :].bitcast(F32), ALU.subtract) \
                  .then_inc(lo_ready, 1)

            def ada_block(u, k):
                acc, init = acc_part(u)
                m = 16 * u + k
                if k == 0:
                    dve.wait_ge(bias_landed[init], 16)
                else:
                    dve.wait_ge(ada_used, m)
                dve.wait_ge(ada_landed[m % RING], 16 * (m // RING + 1))
                nc.vector.scalar_tensor_tensor(out=acc, in0=ada_raw[:, m % RING, :], scalar=c_act[:, k:k + 1], in1=acc,
                                               op0=ALU.mult, op1=ALU.add).then_inc(ada_used, 1)

            def first4(n0):
                for j in range(RING):
                    lo_block(n0 + j, j)

            def first3(n0):
                for j in range(RING - 1):
                    lo_block(n0 + j, j)

            def rest(n0, nb, name=None, hooks=(), g0=1):
                if name not in ADA_BESIDE and not hooks:
                    with dve.Fori(g0, nb // RING) as g:
                        for j in range(RING):
                            lo_block(RING * g + (n0 + j), j)
                    return
                rest_blocks(n0, RING, nb, nb, name, hooks)

            def rest_blocks(n0, b0, b1, nb, name=None, hooks=(), before=lambda b: None, beside=None):
                name, start = beside or (name, 0)
                nb -= start
                count = ADA_BESIDE.get(name, 0)
                for b in range(b0, b1):
                    before(b)
                    lo_block(n0 + b, b % RING)
                    done = b - start - RING
                    for m in range(count * done // (nb - RING), count * (done + 1) // (nb - RING)):
                        ada_block((ADA_FIRST[name] + m) // KD, (ADA_FIRST[name] + m) % KD)
                    if done < len(hooks):
                        hooks[done]()

            def turn(name):
                dve.wait_ge(*complete(name))
                return grp(name)

            def free(ins):
                ins.then_inc(freed_sem["dve"], 1)

            rms_done = [0]

            def rsqrt(n, scale, src, event=None):
                a, y, t = ra[:, 0:n], ry[:, 0:n], rt[:, 0:n]
                link(nc.vector.tensor_scalar(a, src, scale, EPS, ALU.mult, ALU.add))
                link(nc.vector.tensor_scalar(t.bitcast(I32), a.bitcast(I32), 1, None, ALU.logical_shift_right))
                link(nc.vector.tensor_scalar(y.bitcast(I32), t.bitcast(I32), -1.0, 1597463007.0, ALU.mult, ALU.add))
                for _i in range(3):
                    link(nc.vector.scalar_tensor_tensor(out=t, in0=y, scalar=-0.5, in1=y, op0=ALU.mult, op1=ALU.mult))
                    link(nc.vector.tensor_tensor(t, t, a, ALU.mult))
                    ins = nc.vector.scalar_tensor_tensor(out=y, in0=t, scalar=1.5, in1=y, op0=ALU.add, op1=ALU.mult)
                    if event is not None and _i == 2:
                        rms_done[0] += 1
                        ins.then_inc(event, 1)
                        dve.wait_ge(event, rms_done[0])
                    else:
                        link(ins)

            def rotate(out1, out2, x1, x2, c, s, t1, t2):
                mark(nc.vector.tensor_tensor(t1, x1, c, ALU.mult))
                link(nc.vector.tensor_tensor(t2, x2, s, ALU.mult))
                link(nc.vector.tensor_tensor(out1, t1, t2, ALU.subtract))
                mark(nc.vector.tensor_tensor(t1, x1, s, ALU.mult))
                link(nc.vector.tensor_tensor(t2, x2, c, ALU.mult))
                return nc.vector.tensor_tensor(out2, t1, t2, ALU.add)

            def residual(name, q):
                turn(name)
                for tok in range(TOK):
                    xs = X[:, tok, q * COLS:(q + 1) * COLS]
                    ins = nc.vector.scalar_tensor_tensor(out=xs, in0=xs, scalar=ALPHA, in1=T(name, tok), op0=ALU.mult,
                                                         op1=ALU.add)
                    if tok == 0:
                        n_first = mark(ins)
                free(ins)
                for tok in range(TOK):
                    if tok == 0:
                        after(n_first)
                    else:
                        dve.wait_ge(freed_sem["dve"], FREED[name][1])
                    for n in range(2 * q, 2 * q + 2):
                        mark(nc.vector.bn_stats(st[:, tok, n, :], X[:, tok, n * HALF:(n + 1) * HALF]))

            def mean_and_rstd():
                after(own[0])
                for tok in range(TOK):
                    n_last = mark(nc.vector.bn_aggr(mvar[:, tok, :], st[:, tok, :, :]))
                after(n_last)
                rsqrt(TOK, 1.0, mvar[:, :, 1])

            def split_operand(first, event):
                for k in range(0, KD, 2):
                    src = tmp[:, (k % 4) * SEQ:(k % 4 + 2) * SEQ]
                    h, l = (m[:, k:k + 2, :].rearrange(flat) for m in (XH, XL))
                    dve.wait_ge(ev(event), k // 2 + 1)
                    link(nc.vector.tensor_copy(h, src))
                    nc.vector.tensor_tensor(l, src, h.bitcast(F32), ALU.subtract).then_inc(tile_split, 1)

            def attention(S, units, nm, rs, ri, yt, keys, prepare, gate, H, L):
                inverse = {}
                for i in range(units + 6):
                    if i < units:
                        u = i
                        nk = keys(u)
                        b = bank(S, u % 3)
                        dve.wait_ge(S["scored"], u + 1)
                        prepare(u, b, nk)
                        nc.vector.tensor_reduce(nm[:, u:u + 1], ps[:, b:b + nk], AX_X, ALU.max, negate=True) \
                          .then_inc(S["maxed"], 1)
                    if 1 <= i <= units:
                        u = i - 1
                        dve.wait_ge(S["exped"], u + 1)
                        mark(nc.vector.reciprocal(ri[:, u:u + 1], rs[:, u:u + 1]))
                        inverse[u] = own[0]
                    if 4 <= i < units + 4:
                        u = i - 4
                        b = bank(S, 5 + u % 2)
                        after(inverse[u])
                        dve.wait_ge(S["summed"], u + 1)
                        if u >= 4:
                            dve.wait_ge(S["backed"], (u - 4) // 2 + 1)
                        if gate is None:
                            ins = nc.vector.tensor_scalar(yt[:, u % 4, :], ps[:, b:b + P], ri[:, u:u + 1], None,
                                                          ALU.mult)
                        else:
                            ins = nc.vector.scalar_tensor_tensor(out=yt[:, u % 4, :], in0=ps[:, b:b + P],
                                                                 scalar=ri[:, u:u + 1], in1=gate(u), op0=ALU.mult,
                                                                 op1=ALU.mult)
                        ins.then_inc(S["scaled"], 1)
                    if i >= 7 and i % 2 == 1:
                        h = (i - 7) // 2
                        dve.wait_ge(S["hi"], h + 1)
                        nc.vector.tensor_tensor(L(h), ps[:, bank(S, 7):bank(S, 7) + SEQ], H(h).bitcast(F32),
                                                ALU.subtract) \
                          .then_inc(S["lo"], 1)

            skip = lambda: None

            nc.vector.memset(ones[:, :], 1.0).then_inc(ev("ones"), 1)
            for q in range(4):
                dve.wait_ge(ev("x_hi"), q + 1)
                nc.vector.tensor_tensor(XL[:, 4 * q:4 * q + 4, :], xT_raw[:, 4 * q:4 * q + 4, :],
                                        XH[:, 4 * q:4 * q + 4, :].bitcast(F32), ALU.subtract).then_inc(ev("x_lo"), 1)
                if q == 0:
                    first4(B_C)
            dve.wait_ge(ev("pos"), 16)
            dve.wait_ge(ev("inv_freq"), 16)
            link(nc.vector.tensor_copy(pos_f[:, :], pos_i[:, :]))
            for tok in range(TOK):
                n_last = mark(nc.vector.tensor_scalar(ang[:, tok, :], inv_freq[:, :], pos_f[:, tok:tok + 1], None,
                                                      ALU.mult))
            after(n_last)
            magic = 12582912.0
            link(nc.vector.tensor_scalar(turns_n[:, :, :], ang[:, :, :], 1.0 / (2 * np.pi), magic, ALU.mult, ALU.add))
            link(nc.vector.tensor_scalar(turns_n[:, :, :], turns_n[:, :, :], magic, None, ALU.subtract))
            left = 2 * np.pi
            src = ang
            for part in range(4):
                c = float(np.float32(left))
                if part < 3:
                    e = int(np.floor(np.log2(left)))
                    c = float(np.floor(left / 2.0 ** (e - 7)) * 2.0 ** (e - 7))
                left -= c
                link(nc.vector.scalar_tensor_tensor(out=rot[:, :, :], in0=turns_n[:, :, :], scalar=-c, in1=src[:, :, :],
                                                    op0=ALU.mult, op1=ALU.add))
                src = rot
            link(nc.vector.tensor_scalar(ang[:, :, :], rot[:, :, :], float(np.pi / 2), None, ALU.add))
            link(nc.vector.tensor_scalar(turns_n[:, :, :], ang[:, :, :], float(np.pi), -2 * float(np.pi), ALU.is_gt,
                                         ALU.mult))
            link(nc.vector.tensor_tensor(ang[:, :, :], ang[:, :, :], turns_n[:, :, :], ALU.add))
            mark(nc.vector.tensor_scalar(ang[:, :, :], ang[:, :, :], 3.1415925, -3.1415925, ALU.min, ALU.max))
            nc.vector.tensor_scalar(rot[:, :, :], rot[:, :, :], 3.1415925, -3.1415925, ALU.min, ALU.max) \
              .then_inc(ev("angles"), 1)
            rest(B_C, 16)
            first4(B_Z)
            g = turn("c")
            dve.wait_ge(ev("c_squares"), 4)
            rsqrt(4, 1.0 / LORA, ss[:, 0:4])
            for i in range(4):
                ins = nc.vector.tensor_scalar(c_tok[:, i // 2, (i % 2) * LORA:(i % 2 + 1) * LORA],
                                              ps[:, g + i * HALF:g + (i + 1) * HALF], ry[:, i:i + 1], None, ALU.mult)
            free(ins)
            dve.wait_ge(ev("small_hi"), 1)
            nc.vector.tensor_tensor(small_lo[:, :, :], small_raw[:, :, :], small_hi[:, :, :].bitcast(F32),
                                    ALU.subtract).then_inc(ev("small_lo"), 1)
            dve.wait_ge(ev("c_act"), 1)
            rest(B_Z, 16, "z0")
            first4(B_Z + 16)
            def rope_k():
                dve.wait_ge(ev("sincos"), 2)
                dve.wait_ge(freed_sem["act"], FREED["krt"][1])
                t1, t2 = (rope_tmp[:, i, 0:64].rearrange("p (a b) -> p a b", a=TOK) for i in range(2))
                link(rotate(krr_tok[:, :, 0, 0:32], krr_tok[:, :, 0, 32:64], kr_tok[:, :, 0:32], kr_tok[:, :, 32:64],
                            cos_t[:, :, :], sin_t[:, :, :], t1, t2))
                nc.vector.tensor_copy(krr_tok[:, :, 1, :], krr_tok[:, :, 0, :]).then_inc(ev("k_roped"), 1)

            rest(B_Z + 16, 16, "z1", [skip] * 8 + [rope_k])
            first3(B_QN)
            g = grp("cT")
            for k in range(8):
                dve.wait_ge(ev("c_hi"), (k | 1) + 1)
                nc.vector.scalar_tensor_tensor(out=CL[:, k, :], in0=ps[:, g + k * SEQ:g + (k + 1) * SEQ],
                                               scalar=col("q_norm", k) if k < 4 else col("kv_norm", k - 4),
                                               in1=CH[:, k, :].bitcast(F32), op0=ALU.mult, op1=ALU.subtract) \
                  .then_inc(tile_split, 1)
            lo_block(B_QN + 3, 3)
            first4(B_QN + 4)
            first4(B_QR)

            def rope_q(tok):
                dve.wait_ge(freed_sem["act"], FREED["qr"][1])
                t1, t2 = (rope_tmp[:, i, :].rearrange("p (h e) -> p h e", h=16) for i in range(2))
                if tok:
                    dve.wait_ge(ev("q_roped"), tok)
                c, s = (tab[:, tok, :].unsqueeze(1).broadcast_to([P, 16, 32]) for tab in (cos_t, sin_t))
                rotate(qrr_tok[:, tok, :, 0:32], qrr_tok[:, tok, :, 32:64], qr_tok[:, tok, :, 0:32],
                       qr_tok[:, tok, :, 32:64], c, s, t1, t2).then_inc(ev("q_roped"), 1)

            first4(B_KN)
            rope_q(0)
            first4(B_KN + 4)
            rope_q(1)
            g = turn("kn0")
            free(nc.vector.tensor_copy(kT[:, 0:8, :].rearrange(flat), ps[:, g:g + 4 * HALF]))
            first4(B_V)
            g = turn("qrT")
            free(nc.vector.tensor_copy(qrT[:, :, :].rearrange(flat), ps[:, g:g + 4 * HALF]))
            first4(B_V + 4)
            first3(B_MO)

            def mask_chunk(u, b, nk):
                link(nc.vector.memset(ps[0:64, b + nk - 64:b + nk], NEG))

            attention(A1, 32, nmax, rsum, rinv, y_tok, lambda u: P * (1 + u % 2), mask_chunk,
                      lambda u: z_tok[:, u % 2, (u // 2) * P:(u // 2 + 1) * P],
                      lambda h: XH[:, h, :], lambda h: XL[:, h, :])
            lo_block(B_MO + 3, 3)
            rest(B_MO, 16, "mo0")
            first4(B_MO + 16)
            dve.wait_ge(ev("x"), 16)
            residual("mo0", 0)
            rest(B_MO + 16, 16, "mo1")
            first3(B_CONV)
            residual("mo1", 1)
            mean_and_rstd()
            nc.vector.scalar_tensor_tensor(out=shift_col[:, :], in0=mvar[:, 1, 0:1], scalar=-1.0, in1=ry[:, 1:2],
                                           op0=ALU.mult, op1=ALU.mult).then_inc(ev("shift_col"), 1)
            nc.vector.tensor_scalar(X[:, 0, :], X[:, 0, :], mvar[:, 0, 0:1], ry[:, 0:1], ALU.subtract, ALU.mult) \
              .then_inc(ev("normed"), 1)
            lo_block(B_CONV + 3, 3)
            split_operand("x1Ta", "x1_full")

            def x1_rows(i):
                def do():
                    tok = i // 2
                    if i == 0:
                        dve.wait_ge(ev("rows0"), 32)
                        dve.wait_ge(*complete("x1Tb"))
                    if i % 2:
                        dve.wait_ge(ev("x1_rows"), i)
                    nc.vector.tensor_tensor(X[:, tok, :], X[:, tok, :], (row_b if i % 2 else row_w)[:, :],
                                            ALU.add if i % 2 else ALU.mult).then_inc(ev("x1_rows"), 1)
                return do

            rest(B_CONV, 16, "mlq", [skip, x1_rows(0), skip, skip, x1_rows(1), skip, skip, x1_rows(2), skip, skip,
                                     x1_rows(3)])

            def conv_before(q):
                g = grp(("mlq", "mlk")[q])

                def do(b):
                    if not 5 <= b < 13:
                        return
                    k = b - 5
                    f = 8 * q + k
                    dve.wait_ge(ev("last_tap"), 8 * q + (k | 1) + 1)
                    for s in range(1, TAPS):
                        ins = nc.vector.scalar_tensor_tensor(
                            out=conv_tmp[:, k, s:], in0=ps[:, g + k * SEQ:g + (k + 1) * SEQ - s],
                            scalar=col("conv_w", (TAPS - 1 - s) * 16 + f), in1=conv_tmp[:, k, s:],
                            op0=ALU.mult, op1=ALU.add)
                        ins.then_inc(taps_done, 1) if s == TAPS - 1 else link(ins)
                return do

            first4(B_CONV + 16)
            turn("mlq")
            rest_blocks(B_CONV + 16, 4, 16, 16, "mlk", before=conv_before(0))
            dve.wait_ge(ev("small_hi"), 2)
            nc.vector.tensor_tensor(small_lo[:, :, 0:40], small_raw[:, :, 0:40], small_hi[:, :, 0:40].bitcast(F32),
                                    ALU.subtract).then_inc(ev("small_lo"), 1)
            first4(B_VOZ)
            turn("mlk")
            for tok in range(TOK):
                mark(nc.vector.memset(mv[:, tok, :, ML_V:ML_V + 1], 1.0))
            rest_blocks(B_VOZ, 4, 16, 16, "mv0", before=conv_before(1))
            first4(B_VOZ + 16)
            g = turn("gates")
            dve.wait_ge(ev("gate_bias"), 32)
            mark(nc.vector.tensor_scalar(gi[:, :], ps[0:8, g:g + SEQ], gate_bias[0:8, :], None, ALU.add))
            free(nc.vector.tensor_scalar(gf[:, :], ps[32:40, g:g + SEQ], gate_bias[32:40, :], None, ALU.add))
            dve.wait_ge(freed_sem["dve"], FREED["gates"][1])
            link(nc.vector.tensor_scalar(ge[:, :], gf[:, :], -1.0, None, ALU.mult))
            nc.vector.tensor_tensor(ge[:, :], ge[:, :], gf[:, :], ALU.min).then_inc(ev("neg_abs"), 1)
            link(nc.vector.memset(gM[:, :], 1.0))
            dve.wait_ge(ev("log1p"), 1)
            link(nc.vector.scalar_tensor_tensor(out=gf[:, :], in0=gf[:, :], scalar=0.0, in1=ge[:, :], op0=ALU.min,
                                                op1=ALU.subtract))
            link(nc.vector.tensor_tensor_scan(gF[:, :], gM[:, :], gf[:, :], 0.0, ALU.mult, ALU.add))
            link(nc.vector.tensor_tensor(gi[:, :], gi[:, :], gF[:, :], ALU.subtract))
            link(nc.vector.tensor_tensor_scan(gM[:, :], gi[:, :], gi[:, :], 0.0, ALU.max, ALU.max))
            mark(nc.vector.tensor_scalar(ge[:, :], gM[:, :], -1.0, None, ALU.mult))
            nc.vector.tensor_tensor(gF[:, :], gF[:, :], gM[:, :], ALU.add).then_inc(ev("stabiliser"), 1)
            rest(B_VOZ + 16, 16, "mv1")
            first4(B_VOZ + 32)
            rest(B_VOZ + 32, 16, "mo_0")
            first4(B_VOZ + 48)
            rest(B_VOZ + 48, 16, "mo_1")
            first4(B_VOZ + 64)

            def gate_z(name, q):
                dve.wait_ge(freed_sem["act"], FREED[name][1])
                for tok in range(TOK):
                    o = oz[:, tok, q * COLS:(q + 1) * COLS]
                    ins = nc.vector.tensor_tensor(o, o, z_tmp[:, tok, :], ALU.mult)
                    if tok == 0:
                        mark(ins)
                ins.then_inc(ev("z_used"), 1)

            def decay_argument(h):
                b = 4 * HALF
                if h == 0:
                    dve.wait_ge(M2["prep"], 1)
                    mark(nc.vector.tensor_copy(G_col[:, :, :].rearrange(flat), ps[:, 6 * HALF:6 * HALF + 16]))
                    nc.vector.tensor_copy(E_col[:, :, :].rearrange(flat), ps[:, 6 * HALF + 16:6 * HALF + 32]) \
                      .then_inc(M2["prepc"], 1)
                    dve.wait_ge(M2["prepc"], 1)
                    after(own[0])
                    dve.wait_ge(ev("causal"), 16)
                dve.wait_ge(M2["bc"], h + 1)
                if h >= 2:
                    dve.wait_ge(M2["pv"], 2 * (h - 1))
                mark(nc.vector.scalar_tensor_tensor(out=decay[:, h % 2, 0:SEQ], in0=ps[:, b:b + SEQ],
                                                    scalar=G_col[:, 0, h:h + 1], in1=causal[:, :], op0=ALU.add,
                                                    op1=ALU.add))
                nc.vector.scalar_tensor_tensor(out=decay[:, h % 2, SEQ:SEQ + P], in0=ps[:, b + P:b + SEQ],
                                               scalar=G_col[:, 1, h:h + 1], in1=causal[:, 0:P], op0=ALU.add,
                                               op1=ALU.add).then_inc(M2["arg"], 1)

            def weights(h):
                dve.wait_ge(M2["exp"], h + 1)
                dve.wait_ge(M2["st"], h + 1)
                nc.vector.scalar_tensor_tensor(out=decay[:, h % 2, :], in0=ps[:, 5 * HALF:5 * HALF + 384],
                                               scalar=ML_SCALE, in1=decay[:, h % 2, :], op0=ALU.mult, op1=ALU.mult) \
                  .then_inc(M2["w"], 1)

            def head_result(h):
                for tok in range(TOK):
                    u = 2 * h + tok
                    b = (6 + tok) * HALF
                    dve.wait_ge(M2["pv"], u + 1)
                    d = dens[:, u:u + 1]
                    link(nc.vector.tensor_scalar(d, ps[:, b + ML_V:b + ML_V + 1], -1.0, None, ALU.mult))
                    link(nc.vector.tensor_tensor(d, d, ps[:, b + ML_V:b + ML_V + 1], ALU.max))
                    link(nc.vector.tensor_tensor(d, d, E_col[:, tok, h:h + 1], ALU.max))
                    link(nc.vector.reciprocal(dinv[:, u:u + 1], d))
                    nc.vector.tensor_scalar(h_tok[:, h, tok, :], ps[:, b:b + ML_V], dinv[:, u:u + 1], None,
                                            ALU.mult).then_inc(M2["h"], 1)

            def norm_factors(u0):
                if u0:
                    dve.wait_ge(M2["y"], u0)
                dve.wait_ge(M2["sq"], u0 + 8)
                rsqrt(8, 1.0 / ML_V, ss[:, u0:u0 + 8])

            def gated(u0, n):
                dve.wait_ge(ev("z_used"), 1 + u0 // 8)
                for u in range(u0, u0 + n):
                    h, tok = u // 2, u % 2
                    o = oz[:, tok, h * ML_V:(h + 1) * ML_V]
                    nc.vector.scalar_tensor_tensor(out=o, in0=h_tok[:, h, tok, :], scalar=ry[:, u % 8:u % 8 + 1], in1=o,
                                                   op0=ALU.mult, op1=ALU.mult).then_inc(M2["y"], 1)

            def heads_before(b):
                if b >= 5 and (b - 5) % 4 == 0:
                    decay_argument((b - 5) // 4)
                if b >= 6 and (b - 6) % 4 == 0:
                    weights((b - 6) // 4)
                if b >= 8 and b % 4 == 0:
                    head_result(b // 4 - 2)
                if b == 23:
                    gate_z("mz0", 0)
                if b == 26:
                    norm_factors(0)
                if b in (27, 31):
                    gated(b - 27, 4)

            rest_blocks(B_VOZ + 64, 4, 16, 16, "mz0", before=heads_before)
            rest_blocks(B_VOZ + 64, 16, 20, 32, before=heads_before)
            rest_blocks(B_VOZ + 64, 20, 32, 32, before=heads_before, beside=("mz1", 16))
            rest_blocks(B_VOZ + 64, 32, 35, 36, before=heads_before)
            head_result(7)

            def split_y(name, k0):
                for k in range(8):
                    dve.wait_ge(M2["hi"], k0 + (k | 1) + 1)
                    o = grp(name) + k * SEQ
                    nc.vector.scalar_tensor_tensor(out=XL[:, k0 + k, :], in0=ps[:, o:o + SEQ],
                                                   scalar=col("head_norm", k0 + k),
                                                   in1=XH[:, k0 + k, :].bitcast(F32), op0=ALU.mult, op1=ALU.subtract) \
                      .then_inc(tile_split, 1)

            split_y("yTa", 0)
            lo_block(B_LO + 3, 3)
            rest_blocks(B_LO, 4, 6, 16, "lo0")
            gate_z("mz1", 1)
            norm_factors(8)
            gated(8, 8)
            rest_blocks(B_LO, 6, 8, 16, "lo0")
            split_y("yTb", 8)
            rest_blocks(B_LO, 8, 16, 16, "lo0")
            first4(B_LO + 16)
            residual("lo0", 0)

            def modulation(name, norm):
                g = turn(name)
                mark(nc.vector.tensor_copy(mods[:, 0, :], ps[:, g:g + 16]))
                o = PACK[norm][0]
                free(nc.vector.scalar_tensor_tensor(out=A_col[:, :], in0=ps[:, g + 16:g + 32], scalar=1.0,
                                                    in1=pk[:, o:o + 16], op0=ALU.add, op1=ALU.mult))

            rest(B_LO + 16, 16)
            first3(B_QA)
            dve.wait_ge(ev("rel_hi"), 1)
            nc.vector.tensor_tensor(rel_parts[64:, :, :], rel[64:, :, :], rel_parts[64:, :, :].bitcast(F32),
                                    ALU.subtract).then_inc(ev("rel_parts"), 1)
            residual("lo1", 1)

            mean_and_rstd()
            dve.wait_ge(ev("rows1"), 32)
            for tok in range(TOK):
                link(nc.vector.scalar_tensor_tensor(out=X[:, tok, :], in0=X[:, tok, :], scalar=mvar[:, tok, 0:1],
                                                    in1=row_w[:, :], op0=ALU.subtract, op1=ALU.mult))
                nc.vector.scalar_tensor_tensor(out=X[:, tok, :], in0=X[:, tok, :], scalar=ry[:, tok:tok + 1],
                                               in1=row_b[:, :], op0=ALU.mult, op1=ALU.add) \
                  .then_inc(ev("x2_rows"), 1)

            def rms_rows(n_squares, src):
                dve.wait_ge(ev("x_squares"), n_squares)
                if src is None:
                    src = ss[:, 4:6]
                    link(nc.vector.tensor_tensor(src, ss[:, 0:2], ss[:, 2:4], ALU.add))
                rsqrt(TOK, 1.0 / D, src, ev("rms"))
                nc.vector.tensor_scalar(h_norm[:, 0, :], X[:, 0, :], ry[:, 0:1], None, ALU.mult) \
                  .then_inc(ev("h_normed"), 1)

            rms_rows(2, ss[:, 0:2])
            modulation("ada1", "norm1")
            lo_block(B_QA + 3, 3)
            split_operand("hTa", "h_full")
            rest(B_QA, 16, "qa")
            first4(B_KVA)
            rest(B_KVA, 8, "kva")
            first4(B_QB)

            def norm_heads(x, heads, which):
                sq = tmp[:, 0:heads * HD].rearrange("p (h e) -> p h e", e=HD)

                def squares():
                    link(nc.vector.tensor_tensor(sq, x, x, ALU.mult))
                    link(nc.vector.tensor_reduce(ss[:, 0:heads], sq, AX_X, ALU.add))

                def scale():
                    rsqrt(heads, 1.0 / HD, ss[:, 0:heads])
                    link(nc.vector.tensor_tensor(x, x, ry[:, 0:heads].unsqueeze(2).broadcast_to([P, heads, HD]),
                                                 ALU.mult))

                def gain():
                    link(nc.vector.tensor_tensor(x, x, qkn[:, which, :].unsqueeze(1).broadcast_to([P, heads, HD]),
                                                 ALU.mult))
                return [squares, scale, gain]

            roped = [0]

            def rope_heads(x, heads, tok, event):
                v = x.rearrange("p h (i two) -> p h i two", two=2)
                x0, x1 = v[:, :, :, 0], v[:, :, :, 1]
                w = heads * HD // 2
                sh = "p (h i) -> p h i"
                t = [rope2[:, 0, 0:w].rearrange(sh, h=heads), rope2[:, 1, 0:w].rearrange(sh, h=heads),
                     tmp[:, 0:w].rearrange(sh, h=heads), tmp[:, HALF:HALF + w].rearrange(sh, h=heads)]
                c, s = (tab[:, tok, :].unsqueeze(1).broadcast_to([P, heads, HD // 2]) for tab in (cos2, sin2))

                def products():
                    mark(nc.vector.tensor_tensor(t[0], x0, c, ALU.mult))
                    mark(nc.vector.tensor_tensor(t[1], x1, s, ALU.mult))

                def products2():
                    mark(nc.vector.tensor_tensor(t[2], x0, s, ALU.mult))
                    link(nc.vector.tensor_tensor(t[3], x1, c, ALU.mult))

                def sums():
                    mark(nc.vector.tensor_tensor(x0, t[0], t[1], ALU.subtract))
                    nc.vector.tensor_tensor(x1, t[2], t[3], ALU.add).then_inc(ev(event), 1)
                    roped[0] += 1
                    dve.wait_ge(ev(event), roped[0])
                return [products, products2, sums]

            def wait_tables():
                dve.wait_ge(ev("tables2"), 64)
                dve.wait_ge(freed_sem["act"], FREED["qa"][1])

            def wait_kva():
                dve.wait_ge(freed_sem["act"], FREED["kva"][1])

            steps = []
            for tok in range(TOK):
                steps += norm_heads(qa_tok[:, tok], N_A, 0) + rope_heads(qa_tok[:, tok], N_A, tok, "qk_roped")
            for tok in range(TOK):
                steps += norm_heads(kva_tok[:, tok, 0:N_KV], N_KV, 1) \
                    + rope_heads(kva_tok[:, tok, 0:N_KV], N_KV, tok, "qk_roped")
            rest(B_QB, 16, "qb", [wait_tables] + steps[0:10])
            first4(B_KB)
            wait_kva()
            rest(B_KB, 16, "kb", steps[10:22])
            first4(B_VB)
            def add_window(c0, c1):
                def do():
                    if c0 == 0:
                        dve.wait_ge(ev("window"), 16)
                        dve.wait_ge(freed_sem["act"], FREED["biasb"][1])
                    v = na_bias[:, c0:c1].rearrange("p c h i -> p c (h i)")
                    mark(nc.vector.tensor_tensor(
                        v, v, window[:, c0:c1].unsqueeze(2).broadcast_to([P, c1 - c0, N_A * REL_R]), ALU.add))
                return do

            rest(B_VB, 16, "vb", steps[22:] + [add_window(16 * i, 16 * i + 16) for i in range(4)])
            first3(B_MERGE)
            after(own[0])
            dve.wait_ge(ev("qk_roped"), 4)

            def add_bias(u, b, nk):
                if u >= 16:
                    h, blk = (u - 16) // 2, u % 2
                    i0 = 2 - 2 * blk
                    v = ps[:, b:b + SEQ].rearrange("p (r c) -> p r c", r=4)
                    link(nc.vector.tensor_tensor(v, v, na_bias[:, :, h, i0:i0 + 4].rearrange("p c r -> p r c"),
                                                 ALU.add))

            attention(A3, 32, nmax2, rsum2, rinv2, y_tok2, lambda u: SEQ, add_bias, None,
                      lambda h: yaH[:, h, :] if h < N_A else ybH[:, h - N_A, :],
                      lambda h: yaL[:, h, :] if h < N_A else ybL[:, h - N_A, :])
            lo_block(B_MERGE + 3, 3)
            rest(B_MERGE, 16, "ga0")
            for n, name in enumerate(("ga1", "gb0", "gb1")):
                first4(B_MERGE + 16 * (n + 1))
                rest(B_MERGE + 16 * (n + 1), 16, name)
            first4(B_MERGE + 64)
            rest(B_MERGE + 64, 8, "oa0")
            def merge_columns(name, q, first_tok):
                for tok in range(TOK):
                    if tok == 0:
                        after(first_tok)
                    else:
                        dve.wait_ge(freed_sem["dve"], FREED[name][1])
                    m = merged[:, tok, q * COLS:(q + 1) * COLS]
                    nc.vector.tensor_tensor(m, m, sig_b[:, tok, q * COLS:(q + 1) * COLS], ALU.add) \
                      .then_inc(ev("merged"), 1)

            for n, name in enumerate(("oa0", "ob0", "oa1", "ob1")):
                n0 = B_MERGE + 72 + 8 * n
                first3(n0) if n == 3 else first4(n0)
                turn(name)
                q = n // 2
                sig = (sig_a, sig_b)[n % 2]
                dve.wait_ge(freed_sem["act"], FREED[("ga", "gb")[n % 2] + str(q)][1])
                for tok in range(TOK):
                    v = sig[:, tok, q * COLS:(q + 1) * COLS]
                    ins = nc.vector.tensor_tensor(v, v, T(name, tok), ALU.mult)
                    if tok == 0:
                        first_tok = mark(ins)
                free(ins)
                if n == 1:
                    merge_columns(name, q, first_tok)
                if n < 3:
                    rest(n0, 8, ("ob0", "oa1", "ob1")[n])
            for name in ("mTa", "mTb"):
                g = grp(name)
                for k in range(4):
                    k0 = (8 if name == "mTb" else 0) + 2 * k
                    dve.wait_ge(ev("m_hi"), k0 // 2 + 1)
                    nc.vector.tensor_tensor(XL[:, k0:k0 + 2, :].rearrange(flat), ps[:, g + k * HALF:g + (k + 1) * HALF],
                                            XH[:, k0:k0 + 2, :].rearrange(flat).bitcast(F32), ALU.subtract) \
                      .then_inc(tile_split, 1)
                if name == "mTa":
                    lo_block(B_WO + 3, 3)
                    merge_columns("ob1", 1, first_tok)
                    rest_blocks(B_WO, 4, 8, 16, "wo0")

            def gated_residual(name, q, row, event):
                turn(name)
                for tok in range(TOK):
                    xs = X[:, tok, q * COLS:(q + 1) * COLS]
                    ins = nc.vector.tensor_tensor(tmp[:, :], T(name, tok), row[:, q * COLS:(q + 1) * COLS], ALU.mult)
                    if tok == 0:
                        link(ins)
                    else:
                        free(ins)
                        dve.wait_ge(freed_sem["dve"], FREED[name][1])
                    nc.vector.tensor_tensor(xs, xs, tmp[:, :], ALU.add).then_inc(ev(event), 1)
                    dve.wait_ge(ev(event), 2 * q + tok + 1)

            rest_blocks(B_WO, 8, 16, 16, "wo0")
            first4(B_WO + 16)
            dve.wait_ge(freed_sem["act"], FREED["g1"][1])
            gated_residual("wo0", 0, g_row, "x3")
            rest(B_WO + 16, 16, "wo1")
            first3(B_FFN)
            gated_residual("wo1", 1, g_row, "x3")
            rms_rows(6, None)
            modulation("ada2", "norm2")
            lo_block(B_FFN + 3, 3)
            split_operand("h2Ta", "h2_full")

            def ffn_blocks(p, g0, g1):
                def four(g):
                    for j in range(RING):
                        lo_block(16 * p + (RING * g + (B_FFN + j)), j)
                if g1 - g0 == 1:
                    four(g0)
                else:
                    with dve.Fori(g0, g1) as g:
                        four(g)

            def ffn_out(p, parity):
                g = ((GROUP["ffn0"] + parity) % 2) * 4 * HALF
                dve.wait_ge(ev("ffn_silu"), p + 1)
                nc.vector.tensor_tensor(tmp[:, :], tmp[:, :], ps[:, g + COLS:g + 2 * COLS], ALU.mult) \
                  .then_inc(product_done, 1)
                dve.wait_ge(ev("ffn_hi"), p + 1)
                sl = (slice(None), slice(4 * p, 4 * p + 4) if isinstance(p, int) else bass.ds(4 * p, 4), slice(None))
                nc.vector.tensor_tensor(FL[sl], tmp[:, :].rearrange("p (k t) -> p k t", k=4), FH[sl].bitcast(F32),
                                        ALU.subtract).then_inc(ev("ffn_lo"), 1)

            rest(B_FFN, 16, "ffn0")
            for s in range(2):
                ffn_blocks(1 + s, 0, 1)
                ffn_out(s, s)
                ffn_blocks(1 + s, 1, 4)
            with dve.Fori(1, (FFN_PASSES - 1) // 2) as i:
                for s in range(2):
                    ffn_blocks(2 * i + (1 + s), 0, 1)
                    ffn_out(2 * i + s, s)
                    ffn_blocks(2 * i + (1 + s), 1, 4)
            first4(B_DOWN)
            ffn_out(FFN_PASSES - 1, 0)
            rest(B_DOWN, KF)
            first4(B_DOWN + KF)
            dve.wait_ge(freed_sem["act"], FREED["g2"][1])
            gated_residual("down0", 0, g2_row, "x4")
            rest_blocks(B_DOWN + KF, 4, 8, KF)
            dve.wait_ge(ev("x_squares"), 8)
            dve.wait_ge(ev("final_row"), 16)
            for tok in range(TOK):
                nc.vector.tensor_tensor(X[:, tok, 0:COLS], X[:, tok, 0:COLS], final_row[:, 0:COLS], ALU.mult) \
                  .then_inc(ev("x4_weighted"), 1)
            rest(B_DOWN + KF, KF, g0=2)
            gated_residual("down1", 1, g2_row, "x4")
            dve.wait_ge(ev("x_squares"), 10)
            link(nc.vector.tensor_tensor(ss[:, 4:6], ss[:, 0:2], ss[:, 2:4], ALU.add))
            rsqrt(TOK, 1.0 / D, ss[:, 4:6], ev("rms"))
            for tok in range(TOK):
                nc.vector.scalar_tensor_tensor(out=X[:, tok, COLS:], in0=X[:, tok, COLS:], scalar=ry[:, tok:tok + 1],
                                               in1=final_row[:, COLS:], op0=ALU.mult, op1=ALU.mult) \
                  .then_inc(ev("result1"), 1)

        @block.tensor
        def _(pe):
            mm = nc.tensor.matmul

            def start(name):
                if LAST_IN_GROUP[name] is not None:
                    kind, n = FREED[LAST_IN_GROUP[name]]
                    pe.wait_ge(freed_sem[kind], n)
                return grp(name)

            def done(ins):
                ins.then_inc(turn_done, 1)

            def token_major(name, n0, nb, H, L, need=None, width=COLS, per_block=1, blocks=None,
                            then=lambda b: None):
                b0, b1 = blocks or (0, nb)
                g = start(name) if b0 == 0 else grp(name)
                for b in range(b0, b1):
                    j = b % RING
                    pe.wait_ge(lo_ready, n0 + b + 1)
                    for sub in range(per_block):
                        k = b * per_block + sub
                        if need is not None:
                            pe.wait_ge(*need(k))
                        for tok in range(TOK):
                            xh, xl = (m[:, k, tok * P:(tok + 1) * P] for m in (H, L))
                            for x, w, first in ((xh, hi, k == 0), (xh, lo, False), (xl, hi, False)):
                                for c in range(COLS // per_block // HALF):
                                    o = g + (2 * tok + c) * HALF
                                    c0 = (sub + c) * HALF
                                    ins = mm(ps[:, o:o + HALF], x, w[:, j, c0:c0 + HALF], start=first,
                                             stop=(k == nb * per_block - 1 and x is xl), skip_group_check=True)
                    ins.then_inc(block_done, 1)
                    then(b)

            def feature_block(g, k, j, H, L, first, last):
                for m in range(8):
                    for w, x, lead in ((hi, H, True), (hi, L, False), (lo, H, False)):
                        o = g + m * SEQ
                        ins = mm(ps[:, o:o + SEQ], w[:, j, m * P:(m + 1) * P], x(k),
                                 start=first and lead and m % 2 == 0, stop=last and w is lo, skip_group_check=True)
                ins.then_inc(block_done, 1)

            def feature_major(name, n0, nb, H, L, need=None, per=1):
                g = start(name)
                for j in range(RING):
                    pe.wait_ge(lo_ready, n0 + j + 1)
                    if need is not None:
                        pe.wait_ge(need[0], need[1] + j // per + 1)
                    feature_block(g, j, j, lambda k: H[:, k, :], lambda k: L[:, k, :], j == 0,
                                  nb == RING and j == RING - 1)
                if nb > RING:
                    with pe.Fori(1, nb // RING) as gg:
                        for j in range(RING):
                            pe.wait_ge(lo_ready, RING * gg + (n0 + j + 1))
                            if need is not None:
                                pe.wait_ge(need[0], RING // per * gg + (need[1] + j // per + 1))
                            feature_block(g, RING * gg + j, j, lambda k: H[:, bass.ds(k, 1), :].rearrange(flat),
                                          lambda k: L[:, bass.ds(k, 1), :].rearrange(flat), False, True)

            def small_linear(name, n, count):
                g = start(name)
                pe.wait_ge(ev("small_lo"), count)
                for k in range(KD):
                    for w, x in ((small_hi, XH), (small_hi, XL), (small_lo, XH)):
                        ins = mm(ps[0:n, g:g + SEQ], w[:, k, 0:n], x[:, k, :],
                                 start=(k == 0 and w is small_hi and x is XH),
                                 stop=(k == KD - 1 and w is small_lo), skip_group_check=True)
                done(ins)

            def transposes(name, tiles, waits={}):
                g = start(name)
                for n, (o, src) in enumerate(tiles):
                    if n in waits:
                        pe.wait_ge(*waits[n])
                    ins = nc.tensor.transpose(ps[0:src.shape[1], g + o:g + o + P], src, ident[:, :])
                    if name in BANKS_BEFORE and n % 4 == 3:
                        ins.then_inc(tiles_turned, 1)
                if name not in BANKS_BEFORE:
                    done(ins)

            def operand_tiles(src, k0):
                return [(k * SEQ + tok * P, src[:, tok, (k0 + k) * P:(k0 + k + 1) * P])
                        for k in range(8) for tok in range(TOK)]

            def attention(S, units, pr, prT, yt, keys, operands, values):
                for i in range(units + 6):
                    if i < units:
                        u = i
                        nk = keys(u)
                        b = bank(S, u % 3)
                        if u >= 3:
                            pe.wait_ge(S["exped"], u - 2)
                        ops = operands(u)
                        for n, (q, kk) in enumerate(ops):
                            ins = mm(ps[:, b:b + nk], q, kk, start=(n == 0), stop=(n == len(ops) - 1),
                                     skip_group_check=True)
                        ins.then_inc(S["scored"], 1)
                    if 2 <= i < units + 2:
                        u = i - 2
                        b = bank(S, 3 + u % 2)
                        pe.wait_ge(S["exped"], u + 1)
                        if u >= 2:
                            pe.wait_ge(S["copied"], u - 1)
                        for t in range(keys(u) // P):
                            ins = nc.tensor.transpose(ps[:, b + t * P:b + (t + 1) * P], pr[:, u % 3, t * P:(t + 1) * P],
                                                      ident[:, :])
                        ins.then_inc(S["turned"], 1)
                    if 3 <= i < units + 3:
                        u = i - 3
                        b = bank(S, 5 + u % 2)
                        pe.wait_ge(S["copied"], u + 1)
                        if u >= 2:
                            pe.wait_ge(S["scaled"], u - 1)
                        n = keys(u) // P
                        for t in range(n):
                            ins = mm(ps[:, b:b + P], prT[:, u % 2, t * P:(t + 1) * P], values(u, t), start=(t == 0),
                                     stop=(t == n - 1), skip_group_check=True)
                        ins.then_inc(S["summed"], 1)
                    if i >= 6 and i % 2 == 0:
                        h = (i - 6) // 2
                        pe.wait_ge(S["scaled"], 2 * h + 2)
                        if h >= 1:
                            pe.wait_ge(S["lo"], h)
                        for tok in range(TOK):
                            ins = nc.tensor.transpose(ps[:, bank(S, 7) + tok * P:bank(S, 7) + (tok + 1) * P],
                                                      yt[:, (2 * h + tok) % 4, :], ident[:, :])
                        ins.then_inc(S["backed"], 1)

            pe.wait_ge(ev("ones"), 1)
            token_major("c", B_C, 16, XH, XL, lambda k: (ev("x_lo"), k // 4 + 1))
            token_major("z0", B_Z, 16, XH, XL)
            small_linear("kr", ROPE, 1)
            g = start("krt")
            pe.wait_ge(ev("ident"), 16)
            pe.wait_ge(freed_sem["act"], FREED["kr"][1])
            for tok in range(TOK):
                ins = nc.tensor.transpose(ps[:, g + 2 * tok * HALF:g + 2 * tok * HALF + ROPE],
                                          krf[:, tok * P:(tok + 1) * P], ident[0:ROPE, 0:ROPE])
            done(ins)
            token_major("z1", B_Z + 16, 16, XH, XL)
            transposes("cT", operand_tiles(c_tok, 0))
            pe.wait_ge(ev("k_roped"), 1)
            transposes("krT", [(tok * P, krr_tok[:, tok].rearrange(flat)) for tok in range(TOK)])
            for q in range(2):
                feature_major(f"qn{q}", B_QN + 4 * q, 4, CH, CL, (tile_split, 0))
            token_major("qr", B_QR, 4, CH, CL)
            CHv, CLv = CH[:, 4:8, :], CL[:, 4:8, :]
            for q in range(2):
                feature_major(f"kn{q}", B_KN + 4 * q, 4, CHv, CLv, (tile_split, 4))
            pe.wait_ge(ev("q_roped"), 2)
            transposes("qrT", [(k * SEQ + tok * P, qrr_tok[:, tok, 2 * k:2 * k + 2, :].rearrange(flat))
                               for k in range(8) for tok in range(TOK)])
            for q in range(2):
                token_major(f"v{q}", B_V + 4 * q, 4, CHv, CLv)
            pe.wait_ge(freed_sem["act"], FREED["v0"][1])

            def mla_operands(u):
                h, blk = u // 2, u % 2
                r0 = (h % 2) * ROPE
                t, nk = slice(blk * P, (blk + 1) * P), P * (1 + blk)
                return [(qT[:, h, t], kT[:, h, 0:nk]), (qrT[r0:r0 + ROPE, h // 2, t], krT[r0:r0 + ROPE, 0:nk])]

            attention(A1, 32, prob, probT, y_tok, lambda u: P * (1 + u % 2), mla_operands,
                      lambda u, t: v_tok[:, t, (u // 2) * P:(u // 2 + 1) * P])
            token_major("mo0", B_MO, 16, XH, XL, lambda k: (A1["lo"], k + 1))
            token_major("mo1", B_MO + 16, 16, XH, XL)
            pe.wait_ge(ev("normed"), 2)
            transposes("x1Ta", operand_tiles(X, 0))
            transposes("x1Tb", operand_tiles(X, 8))

            feature_major("mlq", B_CONV, 16, XH, XL, (tile_split, SPLIT_BASE["x1Ta"]), 2)
            feature_major("mlk", B_CONV + 16, 16, XH, XL)
            token_major("mv0", B_VOZ, 16, XH, XL)
            small_linear("gates", 40, 2)
            for n, name in enumerate(("mv1", "mo_0", "mo_1")):
                token_major(name, B_VOZ + 16 * (n + 1), 16, XH, XL)

            def ada_columns(name, units):
                g = start(name)
                pe.wait_ge(ada_used, 16 * units)
                for vec in range(2):
                    for k in range(KD):
                        o = g + 16 * vec + k
                        ins = mm(ps[:, o:o + 1], acc_s[:, vec, k * P:(k + 1) * P], ones[:, 0:1], start=True, stop=True,
                                 skip_group_check=True)
                done(ins)

            def prepare_heads():
                pe.wait_ge(freed_sem["act"], FREED["mo_1"][1])
                pe.wait_ge(ev("exp_m"), 1)
                for n, src in enumerate((gi, gF)):
                    for tok in range(TOK):
                        o = 6 * HALF + 16 * n + 8 * tok
                        ins = nc.tensor.transpose(ps[:, o:o + 8], src[:, tok * P:(tok + 1) * P], ident[0:8, 0:8])
                ins.then_inc(M2["prep"], 1)
                pe.wait_ge(ev("select"), 16)
                pe.wait_ge(ev("qk"), 16)

            def head_scores(h):
                if h >= 1:
                    pe.wait_ge(M2["arg"], h)
                b = 4 * HALF
                mm(ps[:, b:b + SEQ], select[:, h, :], ge[:, :], start=True, stop=True,
                   skip_group_check=True).then_inc(M2["bc"], 1)
                if h >= 1:
                    pe.wait_ge(M2["w"], h)
                b = 5 * HALF
                kk, qq = qkT[:, h, 1, :], qkT[:, h, 0, :]
                mm(ps[:, b:b + SEQ], kk[:, 0:P], qq, start=True, stop=True, skip_group_check=True)
                mm(ps[:, b + SEQ:b + SEQ + P], kk[:, P:SEQ], qq[:, P:SEQ], start=True, stop=True,
                   skip_group_check=True).then_inc(M2["st"], 1)

            def head_values(h):
                pe.wait_ge(M2["w"], h + 1)
                d = decay[:, h % 2, :]
                for tok in range(TOK):
                    if h >= 1:
                        pe.wait_ge(M2["h"], 2 * (h - 1) + tok + 1)
                    else:
                        pe.wait_ge(M2["prepc"], 1)
                    b = (6 + tok) * HALF
                    parts = [(d[:, 0:P], 0)] if tok == 0 else [(d[:, P:SEQ], 0), (d[:, SEQ:SEQ + P], 1)]
                    for n, (w, s) in enumerate(parts):
                        ins = mm(ps[:, b:b + ML_V + 1], w, mv[:, s, h, :], start=(n == 0),
                                 stop=(n == len(parts) - 1), skip_group_check=True)
                    ins.then_inc(M2["pv"], 1)

            def heads_after(b):
                if b == 0:
                    prepare_heads()
                if b % 4 == 0:
                    head_scores(b // 4)
                if b % 4 == 3:
                    head_values(b // 4)

            token_major("mz0", B_VOZ + 64, 16, XH, XL, then=heads_after)
            token_major("mz1", B_VOZ + 80, 16, XH, XL, then=lambda b: heads_after(16 + b))
            pe.wait_ge(M2["w"], ML_H)
            pe.wait_ge(M2["y"], 8)
            transposes("yTa", operand_tiles(oz, 0), {8: (M2["h"], 15), 12: (M2["h"], 16)})
            y_tiles = lambda k: (tile_split, SPLIT_BASE["yTa"] + k + 1)
            token_major("lo0", B_LO, 16, XH, XL, y_tiles, blocks=(0, 6))
            pe.wait_ge(M2["y"], 16)
            transposes("yTb", operand_tiles(oz, 8))
            token_major("lo0", B_LO, 16, XH, XL, y_tiles, blocks=(6, 16))
            token_major("lo1", B_LO + 16, 16, XH, XL)

            def ada_row(name, units):
                g = start(name)
                pe.wait_ge(ada_used, 16 * units)
                for n in range(4):
                    ins = mm(ps[:, g + n * HALF:g + (n + 1) * HALF], ones[:, :], acc_g[:, n * HALF:(n + 1) * HALF],
                             start=True, stop=True, skip_group_check=True)
                done(ins)

            pe.wait_ge(ev("toep_r"), 1)
            pe.wait_ge(ev("rel_parts"), 1)
            for name, kc0, kc1 in (("biasa", 0, 40), ("biasb", 40, GRID_W)):
                g = start(name)
                for kc in range(kc0, kc1):
                    o = g + (kc - kc0) // 10 * HALF + (kc - kc0) % 10 * N_A * REL_R
                    c0 = GRID_W - 1 - kc
                    ins = mm(ps[:, o:o + N_A * REL_R], toep_r[:, c0:c0 + P],
                             rel_parts[:, :, :].rearrange(flat), start=True, stop=True, skip_group_check=True)
                done(ins)
            ada_columns("ada1", 8)
            pe.wait_ge(ev("h_normed"), 2)
            transposes("hTa", operand_tiles(h_norm, 0))
            transposes("hTb", operand_tiles(h_norm, 8))
            token_major("qa", B_QA, 16, XH, XL, lambda k: (tile_split, SPLIT_BASE["hTa"] + k // 2 + 1))
            token_major("kva", B_KVA, 8, XH, XL, per_block=2)
            feature_major("qb", B_QB, 16, XH, XL)
            feature_major("kb", B_KB, 16, XH, XL)
            token_major("vb", B_VB, 16, XH, XL)
            pe.wait_ge(ev("qk_roped"), 4)
            ada_row("g1", 12)
            transposes("qaT", [(h * SEQ + tok * P, qa_tok[:, tok, h, :]) for h in range(N_A) for tok in range(TOK)])
            transposes("kaT", [(h * SEQ + tok * P, kva_tok[:, tok, h, :]) for h in range(N_KV) for tok in range(TOK)])
            pe.wait_ge(freed_sem["act"], FREED["kaT"][1])

            def blk_operands(u):
                h, blk = (u % 16) // 2, u % 2
                t = slice(blk * P, (blk + 1) * P)
                if u < 16:
                    return [(qaT[:, h, t], kaT[:, h // (N_A // N_KV), :])]
                return [(qbT[:, h, t], kbT[:, h, :])]

            def blk_values(u, t):
                h = (u % 16) // 2
                return kva_tok[:, t, N_KV + h // (N_A // N_KV), :] if u < 16 else vb_tok[:, t, h * HD:(h + 1) * HD]

            attention(A3, 32, prob2, probT2, y_tok2, lambda u: SEQ, blk_operands, blk_values)
            pe.wait_ge(A3["lo"], 16)
            for n, name in enumerate(("ga0", "ga1", "gb0", "gb1")):
                token_major(name, B_MERGE + 16 * n, 16, XH, XL)
            for n, name in enumerate(("oa0", "ob0", "oa1", "ob1")):
                token_major(name, B_MERGE + 64 + 8 * n, 8, *((yaH, yaL) if n % 2 == 0 else (ybH, ybL)))
            pe.wait_ge(ev("merged"), 2)
            transposes("mTa", operand_tiles(merged, 0))
            m_tiles = lambda k: (tile_split, SPLIT_BASE["mTa"] + k // 2 + 1)
            token_major("wo0", B_WO, 16, XH, XL, m_tiles, blocks=(0, 5))
            pe.wait_ge(ev("merged"), 4)
            transposes("mTb", operand_tiles(merged, 8))
            token_major("wo0", B_WO, 16, XH, XL, m_tiles, blocks=(5, 16))
            token_major("wo1", B_WO + 16, 16, XH, XL)
            ada_row("g2", 24)
            ada_columns("ada2", 20)
            pe.wait_ge(ev("h_normed"), 4)
            transposes("h2Ta", operand_tiles(h_norm, 0))
            transposes("h2Tb", operand_tiles(h_norm, 8))

            def ffn_pass(p, parity, freed=None, tiles=None):
                g = ((GROUP["ffn0"] + parity) % 2) * 4 * HALF
                if freed is None:
                    pe.wait_ge(product_done, p - 1)
                else:
                    pe.wait_ge(tile_split, freed)

                def four(kg, static):
                    for j in range(RING):
                        pe.wait_ge(lo_ready, 16 * p + (RING * kg + (B_FFN + j + 1)))
                        if tiles is not None:
                            pe.wait_ge(tile_split, 2 * kg + (tiles + j // 2 + 1))
                        if static:
                            feature_block(g, j, j, lambda k: XH[:, k, :], lambda k: XL[:, k, :], j == 0, False)
                        else:
                            feature_block(g, RING * kg + j, j, lambda k: XH[:, bass.ds(k, 1), :].rearrange(flat),
                                          lambda k: XL[:, bass.ds(k, 1), :].rearrange(flat), False, True)
                four(0, True)
                with pe.Fori(1, KD // RING) as kg:
                    four(kg, False)

            base = SPLIT_BASE["h2Ta"]
            ffn_pass(0, 0, base + 4, base)
            ffn_pass(1, 1, base + 8)
            ffn_pass(2, 0)
            with pe.Fori(1, (FFN_PASSES - 1) // 2) as i:
                for s in range(2):
                    ffn_pass(2 * i + (1 + s), 1 - s)
            token_major("down0", B_DOWN, KF, FH, FL, lambda k: (ev("ffn_lo"), k // 4 + 1))
            token_major("down1", B_DOWN + KF, KF, FH, FL)


def shape_constants():
    c = np.zeros((P, N_CONST), np.float32)

    def put(name, value, rows=P):
        o, n = CONST[name]
        c[:rows, o:o + n] = np.asarray(value, np.float32).reshape(rows, n)

    put("ident", np.eye(P))
    put("inv_freq", np.tile(10000.0 ** (-np.arange(0, ROPE, 2) / ROPE), (P, 1)))
    p, t = np.arange(P)[:, None], np.arange(SEQ)[None]
    put("causal", np.where(p <= t, 0.0, NEG))
    qc, kc = (np.arange(P) % GRID_W)[:, None], np.arange(GRID_W)[None]
    start = np.clip(qc - NA_COLS // 2, 0, GRID_W - NA_COLS)
    put("window", np.where((kc >= start) & (kc < start + NA_COLS), 0.0, NEG))
    toep = np.zeros((64, 191))
    for half in range(2):
        for j in range(REL_C):
            toep[32 * half + j, GRID_W * half + 78 - j] = 1.0
    put("toeplitz", np.tile(toep, (2, 1)))
    inv = (np.float32(10000.0) ** (-np.arange(0, HD // 2, 2, dtype=np.float32) / (HD // 2))).astype(np.float32)
    tok = np.arange(SEQ)
    ang = np.concatenate([(tok // GRID_W).astype(np.float32)[:, None] * inv,
                          (tok % GRID_W).astype(np.float32)[:, None] * inv], axis=1).astype(np.float64)
    for name, f in (("cos", np.cos), ("sin", np.sin)):
        put(name, f(ang).reshape(TOK, P, HD // 2).transpose(1, 0, 2))
    put("select", np.repeat(np.eye(8), P, axis=1), 8)
    return c


_OUTS = [((1, SEQ, D), "float32")]


def kernel(**inputs):
    import concourse.bacc as _bacc
    from concourse.bass_utils import run_bass_kernel_spmd as _run

    i = {n: np.asarray(a) for n, a in inputs.items()}

    def cols(a):
        return a.reshape(-1, P).T

    pack = {"q_norm": cols(i["mla_q_norm"][0]), "kv_norm": cols(i["mla_kv_norm"][0]), "ln_w0": cols(i["ln_w"][0]),
            "ln_b0": cols(i["ln_b"][0]), "head_norm": cols(i["ml_head_norm"][0]), "conv_w": cols(i["ml_conv_w"][0]),
            "conv_b": cols(i["ml_conv_b"][0]), "norm1": cols(i["norm1_w_2"][0]), "norm2": cols(i["norm2_w_2"][0]),
            "c": cols(i["c_2"][0])}
    args = {
        "positions": i["positions"].reshape(TOK, P).T, "x": i["x"], "xT": i["x"][0].T,
        "pack": np.concatenate([pack[n] for n in PACK], axis=1), "const": shape_constants(),
        "gate_b": i["ml_gate_b"].reshape(2 * ML_H, 1),
        "qk_norm": np.concatenate([i["q_norm_w_2"], i["k_norm_w_2"]], axis=0),
        "rpbT": i["nat_rpb_2"][0].transpose(2, 0, 1),
        "mla_w_in": i["mla_w_in"], "mla_w_qb": i["mla_w_qb"], "mla_w_kvb": i["mla_w_kvb"], "mla_w_out": i["mla_w_out"],
        "ml_w_in": i["ml_w_in"], "ml_w_out": i["ml_w_out"], "ln_w": i["ln_w"], "ln_b": i["ln_b"],
        "w_ada": i["w_ada_2"], "b_ada": i["b_ada_2"], "w_in": i["w_in_2"], "w_oa": i["w_oa_2"], "w_ob": i["w_ob_2"],
        "w_out": i["w_out_2"], "w_gate": i["w_ffn_gate_2"], "w_up": i["w_ffn_up_2"], "w_down": i["w_ffn_down_2"],
        "final_w": i["final_w_2"].reshape(1, D),
    }
    nc = _bacc.Bacc("TRN2", target_bir_lowering=False, num_devices=1)
    arrays, aps = {}, []
    for name, a in args.items():
        a = np.ascontiguousarray(a)
        arrays[f"in_{name}_dram"] = a
        aps.append(nc.dram_tensor(f"in_{name}_dram", a.shape, mybir.dt.from_np(a.dtype), kind="ExternalInput").ap())
    for n, (shape, dtype) in enumerate(_OUTS):
        aps.append(nc.dram_tensor(f"out_{n}_dram", shape, mybir.dt.from_np(np.dtype(dtype)),
                                  kind="ExternalOutput").ap())
    two_block_kernel(nc, *aps)
    r = _run(nc, [arrays], core_ids=[0])
    return r.results[0]["out_0_dram"]
```
